# Optimizing a Trainium2 kernel written in Bass

```python
import jax, jax.numpy as jnp
from jax import lax
import numpy as np

D_MODEL = 1024
BATCH = 1
SEQ = 512
DEPTH = 1

D_MIX = 1024
POOL_WINDOWS = (2, 4, 8, 16)
POOL_WIDTH = 512
POOL_GROUP = POOL_WIDTH // len(POOL_WINDOWS)
N_HEADS = 8
N_KV_HEADS = 2
HEAD_DIM = 64
ATTN_WIDTH = N_HEADS * HEAD_DIM
KV_WIDTH = N_KV_HEADS * HEAD_DIM
N_IDX_HEADS = 8
IDX_DIM = 64
TOPK_MAX = 256
ROPE_THETA = 10000.0
Q_BLOCK = 128
EPS = 1e-6
SPLITS = (POOL_WIDTH, POOL_WIDTH, ATTN_WIDTH, KV_WIDTH, KV_WIDTH, ATTN_WIDTH,
          N_IDX_HEADS * IDX_DIM, IDX_DIM, N_IDX_HEADS)
D_IN_PROJ = 2888


def rms_norm(x, w):
    xf = x.astype(jnp.float32)
    y = xf * lax.rsqrt(jnp.mean(xf * xf, axis=-1, keepdims=True) + EPS)
    return (y * w.astype(jnp.float32)).astype(x.dtype)

def rope(x, pos):
    d = x.shape[-1]
    half = d // 2
    freqs = ROPE_THETA ** (-jnp.arange(half, dtype=jnp.float32) / half)
    ang = pos.astype(jnp.float32)[:, None] * freqs[None, :]
    cos = jnp.cos(ang)[None, :, None, :]
    sin = jnp.sin(ang)[None, :, None, :]
    xf = x.astype(jnp.float32)
    x1, x2 = xf[..., :half], xf[..., half:]
    out = jnp.concatenate([x1 * cos - x2 * sin, x2 * cos + x1 * sin], axis=-1)
    return out.astype(x.dtype)

def pool_mixer(u, w_pool, pool_scale):
    B, S, _ = u.shape
    ug = u.reshape(B, S, len(POOL_WINDOWS), POOL_GROUP).astype(jnp.float32)
    cs = jnp.cumsum(ug, axis=1)
    n_avail = jnp.arange(1, S + 1)
    means = []
    for g, w in enumerate(POOL_WINDOWS):
        csg = cs[:, :, g]
        lag = jnp.pad(csg, ((0, 0), (w, 0), (0, 0)))[:, :S]
        cnt = jnp.minimum(n_avail, w).astype(jnp.float32)[None, :, None]
        means.append((csg - lag) / cnt)
    pooled = jnp.stack(means, axis=2) - ug
    mixed = jnp.einsum('bsgc,gcd->bsgd', pooled, w_pool.astype(jnp.float32))
    mixed = mixed.reshape(B, S, POOL_WIDTH) * pool_scale.astype(jnp.float32)
    return mixed.astype(u.dtype)

def dsa_attention(q, k, v, q_idx, k_idx, w_idx):
    B, S = q.shape[0], q.shape[1]
    nb = S // Q_BLOCK
    k_top = min(TOPK_MAX, S // 4)
    grp = N_HEADS // N_KV_HEADS
    key_pos = jnp.arange(S)
    kf_idx = k_idx.astype(jnp.float32)

    def to_blocks(a):
        return jnp.moveaxis(a.reshape(B, nb, Q_BLOCK, *a.shape[2:]), 1, 0)

    def one_block(args):
        blk, qb, qib, wb = args
        q_pos = blk * Q_BLOCK + jnp.arange(Q_BLOCK)
        logits = jnp.einsum('bqhd,bsd->bqhs', qib.astype(jnp.float32), kf_idx) * (IDX_DIM ** -0.5)
        score = jnp.einsum('bqhs,bqh->bqs', jax.nn.relu(logits),
                           wb.astype(jnp.float32)) * (N_IDX_HEADS ** -0.5)
        causal = key_pos[None, :] <= q_pos[:, None]
        score = jnp.where(causal[None], score, -jnp.inf)
        _, sel = lax.top_k(score, k_top)
        valid = sel <= q_pos[None, :, None]
        k_sel = jax.vmap(lambda kk, ii: kk[ii])(k, sel)
        v_sel = jax.vmap(lambda vv, ii: vv[ii])(v, sel)
        qg = qb.reshape(B, Q_BLOCK, N_KV_HEADS, grp, HEAD_DIM).astype(jnp.float32)
        s = jnp.einsum('bqhgd,bqkhd->bqhgk', qg, k_sel.astype(jnp.float32)) * (HEAD_DIM ** -0.5)
        s = jnp.where(valid[:, :, None, None, :], s, -jnp.inf)
        p = jax.nn.softmax(s, axis=-1)
        o = jnp.einsum('bqhgk,bqkhd->bqhgd', p, v_sel.astype(jnp.float32))
        return o.reshape(B, Q_BLOCK, ATTN_WIDTH).astype(q.dtype)

    out = lax.map(one_block, (jnp.arange(nb), to_blocks(q), to_blocks(q_idx), to_blocks(w_idx)))
    return jnp.moveaxis(out, 0, 1).reshape(B, S, ATTN_WIDTH)

def first_inputs(seed: int = 0) -> dict:
    key = jax.random.key(seed)
    ks = jax.random.split(key, 12)
    f32 = jnp.float32
    x = jax.random.normal(ks[0], (BATCH, SEQ, D_MODEL), f32)
    c = jax.random.normal(ks[1], (BATCH, D_MODEL), f32)
    norm_w = 1.0 + 0.1 * jax.random.normal(ks[2], (DEPTH, D_MODEL), f32)
    w_ada = jax.random.normal(ks[3], (DEPTH, D_MODEL, 3 * D_MODEL), f32) * D_MODEL ** -0.5
    b_ada = 0.01 * jax.random.normal(ks[4], (DEPTH, 3 * D_MODEL), f32)
    w_in = jax.random.normal(ks[5], (DEPTH, D_MODEL, D_IN_PROJ), f32) * D_MODEL ** -0.5
    q_norm_w = 1.0 + 0.1 * jax.random.normal(ks[6], (DEPTH, HEAD_DIM), f32)
    k_norm_w = 1.0 + 0.1 * jax.random.normal(ks[7], (DEPTH, HEAD_DIM), f32)
    w_pool = jax.random.normal(ks[8], (DEPTH, len(POOL_WINDOWS), POOL_GROUP, POOL_GROUP), f32) * POOL_GROUP ** -0.5
    pool_scale = 1.0 + 0.1 * jax.random.normal(ks[9], (DEPTH, POOL_WIDTH), f32)
    w_out = jax.random.normal(ks[10], (DEPTH, D_MIX, D_MODEL), f32) * D_MIX ** -0.5
    return {"x": x, "c": c, "norm_w": norm_w, "w_ada": w_ada, "b_ada": b_ada,
            "w_in": w_in, "q_norm_w": q_norm_w, "k_norm_w": k_norm_w,
            "w_pool": w_pool, "pool_scale": pool_scale, "w_out": w_out}

def first_block(x, c, norm_w, w_ada, b_ada, w_in, q_norm_w, k_norm_w, w_pool, pool_scale, w_out):
    B, S, _ = x.shape
    pos = jnp.arange(S)
    split_points = [int(p) for p in np.cumsum(SPLITS)[:-1]]
    for l in range(DEPTH):
        mod = jnp.einsum('bd,de->be', jax.nn.silu(c), w_ada[l]) + b_ada[l]
        shift, scale, gate = jnp.split(mod, 3, axis=-1)
        h = rms_norm(x, norm_w[l]) * (1.0 + scale[:, None, :]) + shift[:, None, :]
        proj = jnp.einsum('bsd,de->bse', h, w_in[l])
        u_pool, g_pool, q, k, v, g_attn, qi, ki, wi = jnp.split(proj, split_points, axis=-1)
        pool_out = pool_mixer(u_pool, w_pool[l], pool_scale[l]) * jax.nn.silu(g_pool)
        q = rope(rms_norm(q.reshape(B, S, N_HEADS, HEAD_DIM), q_norm_w[l]), pos)
        k = rope(rms_norm(k.reshape(B, S, N_KV_HEADS, HEAD_DIM), k_norm_w[l]), pos)
        v = v.reshape(B, S, N_KV_HEADS, HEAD_DIM)
        qi = rope(qi.reshape(B, S, N_IDX_HEADS, IDX_DIM), pos)
        ki = rope(ki[:, :, None, :], pos)[:, :, 0, :]
        attn_out = dsa_attention(q, k, v, qi, ki, wi) * jax.nn.silu(g_attn)
        y = jnp.einsum('bse,ed->bsd', jnp.concatenate([pool_out, attn_out], axis=-1), w_out[l])
        x = x + gate[:, None, :] * y
    return x


PLE_DIM = 256
MLA_HEADS = 8
QK_NOPE_DIM = 64
QK_ROPE_DIM = 32
V_HEAD_DIM = 64
Q_LORA_RANK = 384
KV_LORA_RANK = 256
CONV_CHANNELS = 512
CONV_WIDTH = 31
MLA_WIDTH = MLA_HEADS * V_HEAD_DIM
D_MIX_2 = MLA_WIDTH + CONV_CHANNELS
IN_PROJ_DIM = Q_LORA_RANK + KV_LORA_RANK + QK_ROPE_DIM + 2 * CONV_CHANNELS
D_FF = 2816
FFN_CONV_WIDTH = 3
NORM_EPS = 1e-6


def rms_norm_2(x, g):
    xf = x.astype(jnp.float32)
    y = xf * lax.rsqrt(jnp.mean(xf * xf, axis=-1, keepdims=True) + NORM_EPS)
    return (y * g.astype(jnp.float32)).astype(x.dtype)

def layer_norm(x, g, b):
    xf = x.astype(jnp.float32)
    mu = jnp.mean(xf, axis=-1, keepdims=True)
    xc = xf - mu
    y = xc * lax.rsqrt(jnp.mean(xc * xc, axis=-1, keepdims=True) + NORM_EPS)
    return (y * g.astype(jnp.float32) + b.astype(jnp.float32)).astype(x.dtype)

def causal_depthwise_conv(x, w, b):
    k = w.shape[0]
    out = lax.conv_general_dilated(
        x, w[:, None, :].astype(x.dtype), window_strides=(1,), padding=((k - 1, 0),),
        dimension_numbers=('NWC', 'WIO', 'NWC'), feature_group_count=x.shape[-1])
    return out + b.astype(x.dtype)

def apply_rope(x, cos, sin):
    x1, x2 = jnp.split(x, 2, axis=-1)
    return jnp.concatenate([x1 * cos - x2 * sin, x1 * sin + x2 * cos], axis=-1)

def causal_mla_attention(q_nope, q_rope, k_nope, k_rope, v):
    b, s, h, _ = q_nope.shape
    nb = s // Q_BLOCK
    scale = (QK_NOPE_DIM + QK_ROPE_DIM) ** -0.5
    k_idx = jnp.arange(s)

    def to_blocks(t):
        return jnp.moveaxis(t.reshape(b, nb, Q_BLOCK, *t.shape[2:]), 1, 0)

    def block(args):
        qn, qr, start = args
        sc = (jnp.einsum('bqhd,bkhd->bhqk', qn, k_nope, preferred_element_type=jnp.float32)
              + jnp.einsum('bqhr,bkr->bhqk', qr, k_rope, preferred_element_type=jnp.float32)) * scale
        q_idx = start + jnp.arange(Q_BLOCK)
        sc = jnp.where(k_idx[None, :] <= q_idx[:, None], sc, -jnp.inf)
        pr = jax.nn.softmax(sc, axis=-1).astype(v.dtype)
        return jnp.einsum('bhqk,bkhd->bqhd', pr, v)

    starts = jnp.arange(nb) * Q_BLOCK
    out = lax.map(block, (to_blocks(q_nope), to_blocks(q_rope), starts))
    return jnp.moveaxis(out, 0, 1).reshape(b, s, h * V_HEAD_DIM)

def hybrid_mixer(xn, cos, sin, w_in, g_q_a, w_q_b, g_kv_a, w_kv_b,
                 conv_w, conv_b, conv_ln_g, conv_ln_b, w_o):
    b, s, _ = xn.shape
    proj = xn @ w_in
    o1 = Q_LORA_RANK
    o2 = o1 + KV_LORA_RANK
    o3 = o2 + QK_ROPE_DIM
    q_a, kv_a, k_rope, conv_in = jnp.split(proj, [o1, o2, o3], axis=-1)
    q = (rms_norm_2(q_a, g_q_a) @ w_q_b).reshape(b, s, MLA_HEADS, QK_NOPE_DIM + QK_ROPE_DIM)
    q_nope, q_rope = jnp.split(q, [QK_NOPE_DIM], axis=-1)
    kv = (rms_norm_2(kv_a, g_kv_a) @ w_kv_b).reshape(b, s, MLA_HEADS, QK_NOPE_DIM + V_HEAD_DIM)
    k_nope, v = jnp.split(kv, [QK_NOPE_DIM], axis=-1)
    q_rope = apply_rope(q_rope, cos[:, :, None, :], sin[:, :, None, :])
    k_rope = apply_rope(k_rope, cos, sin)
    attn = causal_mla_attention(q_nope, q_rope, k_nope, k_rope, v)
    a, gate = jnp.split(conv_in, 2, axis=-1)
    c = a * jax.nn.sigmoid(gate)
    c = causal_depthwise_conv(c, conv_w, conv_b)
    c = jax.nn.silu(layer_norm(c, conv_ln_g, conv_ln_b))
    return jnp.concatenate([attn, c], axis=-1) @ w_o

def conv_gated_ffn(xn, w_gate, w_up, dw_w, dw_b, w_down):
    g = causal_depthwise_conv(xn @ w_gate, dw_w, dw_b)
    return (jax.nn.gelu(g, approximate=True) * (xn @ w_up)) @ w_down

def second_inputs(seed: int = 0) -> dict:
    key = jax.random.key(seed)
    ks = iter(jax.random.split(key, 40))

    def w(shape, fan_in):
        return jax.random.normal(next(ks), shape, jnp.float32) * fan_in ** -0.5

    def gain(shape):
        return 1.0 + 0.05 * jax.random.normal(next(ks), shape, jnp.float32)

    def bias(shape):
        return 0.01 * jax.random.normal(next(ks), shape, jnp.float32)

    L = DEPTH
    x = jax.random.normal(next(ks), (BATCH, SEQ, D_MODEL), jnp.float32)
    p = jax.random.normal(next(ks), (DEPTH, BATCH, SEQ, PLE_DIM), jnp.float32)
    positions = jnp.broadcast_to(jnp.arange(SEQ, dtype=jnp.int32)[None, :], (BATCH, SEQ))
    return {
        "x": x,
        "p": p,
        "positions": positions,
        "g_mix_pre": gain((L, D_MODEL)),
        "w_in": w((L, D_MODEL, IN_PROJ_DIM), D_MODEL),
        "g_q_a": gain((L, Q_LORA_RANK)),
        "w_q_b": w((L, Q_LORA_RANK, MLA_HEADS * (QK_NOPE_DIM + QK_ROPE_DIM)), Q_LORA_RANK),
        "g_kv_a": gain((L, KV_LORA_RANK)),
        "w_kv_b": w((L, KV_LORA_RANK, MLA_HEADS * (QK_NOPE_DIM + V_HEAD_DIM)), KV_LORA_RANK),
        "conv_w": w((L, CONV_WIDTH, CONV_CHANNELS), CONV_WIDTH),
        "conv_b": bias((L, CONV_CHANNELS)),
        "conv_ln_g": gain((L, CONV_CHANNELS)),
        "conv_ln_b": bias((L, CONV_CHANNELS)),
        "w_o": w((L, D_MIX_2, D_MODEL), D_MIX_2),
        "g_mix_post": gain((L, D_MODEL)),
        "g_ffn_pre": gain((L, D_MODEL)),
        "w_ffn_gate": w((L, D_MODEL, D_FF), D_MODEL),
        "w_ffn_up": w((L, D_MODEL, D_FF), D_MODEL),
        "ffn_dw_w": w((L, FFN_CONV_WIDTH, D_FF), FFN_CONV_WIDTH),
        "ffn_dw_b": bias((L, D_FF)),
        "w_ffn_down": w((L, D_FF, D_MODEL), D_FF),
        "g_ffn_post": gain((L, D_MODEL)),
        "w_ple_proj": w((L, PLE_DIM, D_MODEL), PLE_DIM),
        "g_ple": gain((L, D_MODEL)),
        "w_ple_gate": w((L, D_MODEL, D_MODEL), D_MODEL),
    }

def second_block(x, p, positions, g_mix_pre, w_in, g_q_a, w_q_b, g_kv_a, w_kv_b,
              conv_w, conv_b, conv_ln_g, conv_ln_b, w_o, g_mix_post, g_ffn_pre,
              w_ffn_gate, w_ffn_up, ffn_dw_w, ffn_dw_b, w_ffn_down, g_ffn_post,
              w_ple_proj, g_ple, w_ple_gate):
    inv_freq = ROPE_THETA ** (-jnp.arange(0, QK_ROPE_DIM, 2, dtype=jnp.float32) / QK_ROPE_DIM)
    ang = positions.astype(jnp.float32)[..., None] * inv_freq
    cos = jnp.cos(ang).astype(x.dtype)
    sin = jnp.sin(ang).astype(x.dtype)

    h = x
    for i in range(DEPTH):
        mix = hybrid_mixer(rms_norm_2(h, g_mix_pre[i]), cos, sin, w_in[i], g_q_a[i], w_q_b[i],
                           g_kv_a[i], w_kv_b[i], conv_w[i], conv_b[i], conv_ln_g[i],
                           conv_ln_b[i], w_o[i])
        h = h + rms_norm_2(mix, g_mix_post[i])
        ffn = conv_gated_ffn(rms_norm_2(h, g_ffn_pre[i]), w_ffn_gate[i], w_ffn_up[i],
                             ffn_dw_w[i], ffn_dw_b[i], w_ffn_down[i])
        h = h + rms_norm_2(ffn, g_ffn_post[i])
        e = rms_norm_2(p[i] @ w_ple_proj[i], g_ple[i])
        h = h + jax.nn.sigmoid(h @ w_ple_gate[i]) * e
    return h


def setup_inputs(seed=0):
    out = dict(first_inputs(seed))
    for name, value in second_inputs(seed + 1).items():
        if name != "x":
            out[name + "_2"] = value
    return out


def reference(
    x, c, norm_w, w_ada, b_ada, w_in, q_norm_w, k_norm_w, w_pool, pool_scale, w_out, p_2,
    positions_2, g_mix_pre_2, w_in_2, g_q_a_2, w_q_b_2, g_kv_a_2, w_kv_b_2, conv_w_2, conv_b_2,
    conv_ln_g_2, conv_ln_b_2, w_o_2, g_mix_post_2, g_ffn_pre_2, w_ffn_gate_2, w_ffn_up_2,
    ffn_dw_w_2, ffn_dw_b_2, w_ffn_down_2, g_ffn_post_2, w_ple_proj_2, g_ple_2, w_ple_gate_2,
):
    x = first_block(
        x, c, norm_w, w_ada, b_ada, w_in, q_norm_w, k_norm_w, w_pool, pool_scale, w_out,
    )
    return second_block(
        x, p_2, positions_2, g_mix_pre_2, w_in_2, g_q_a_2, w_q_b_2, g_kv_a_2, w_kv_b_2,
        conv_w_2, conv_b_2, conv_ln_g_2, conv_ln_b_2, w_o_2, g_mix_post_2, g_ffn_pre_2,
        w_ffn_gate_2, w_ffn_up_2, ffn_dw_w_2, ffn_dw_b_2, w_ffn_down_2, g_ffn_post_2,
        w_ple_proj_2, g_ple_2, w_ple_gate_2,
    )


_drawn_inputs = setup_inputs


def setup_inputs(seed=0):
    import zlib

    import numpy as np

    out = dict(_drawn_inputs(seed))
    spreads = {}
    factors = {'b_ada': 4.308,
     'q_norm_w': 6.878,
     'k_norm_w': 7.204,
     'g_q_a_2': 6.939,
     'g_kv_a_2': 3.761,
     'conv_b_2': 32.814,
     'conv_ln_b_2': 55.007,
     'ffn_dw_b_2': 8.0,
     'g_ple_2': 3.846,
     'conv_ln_g_2': 8.0,
     'g_ffn_post_2': 2.74}
    for name, (base, spread) in spreads.items():
        noise = np.random.default_rng([zlib.crc32(name.encode()), seed]).standard_normal(out[name].shape)
        drawn = base * np.exp(spread * noise) if base else spread * noise
        out[name] = __import__('jax').numpy.asarray(drawn.astype(out[name].dtype))
    for name, factor in factors.items():
        out[name] = (out[name] * factor).astype(out[name].dtype)
    return out
```

```python
from contextlib import ExitStack

import concourse.bass as bass
import numpy as np
from concourse import mybir

ALU = mybir.AluOpType
ACT = mybir.ActivationFunctionType
F32 = mybir.dt.float32
F32R = mybir.dt.float32r
I32 = mybir.dt.int32

P = 128
T = 512
NT = T // P
D = 1024
KD = D // P
EPS = 1e-6
NEG = -1e30
TAKEN = -3e38
HD = 64
TOPK = min(256, T // 4)
FF = 2816
NJ = FF // P
CW = 31
CP = 32
SCALE1 = HD ** -0.5
SCALE2 = 96 ** -0.5

RAWS = 4
QORD = (3, 2, 0, 1)
SOFF = {3: 0, 2: 512, 0: 896, 1: 1024}
TOFF = {0: 0, 1: 512, 3: 896, 2: 1024}
QB = (("n", 0), ("n", 1), ("r", 0), ("n", 2), ("n", 3), ("r", 1))
INV2PI = float(np.float32(1 / (2 * np.pi)))
ROUND = 1.5 * 2 ** 23
_c1 = 6.28125
TWOPI = (_c1, float(np.uint32(np.float32(2 * np.pi - _c1).view(np.uint32) & 0xFFFFF000).view(np.float32)))
TWOPI = TWOPI + (float(np.float32(2 * np.pi - TWOPI[0] - TWOPI[1])),)
PI32 = float(np.nextafter(np.float32(np.pi), np.float32(0)))

U0, GP0, Q0, K0, V0, GA0, QI0, KI0, WI0, E1 = 0, 512, 1024, 1536, 1664, 1792, 2304, 2816, 2880, 2888

C_ID, C_R64, C_R32, C_TRI, C_HS, C_ONE, C_FREQ, C_RC, C_COS, C_SIN, C_END = (
    0, 128, 256, 384, 896, 898, 900, 901, 917, 1429, 1941)

VECS = [("c", 8), ("norm_w", 8), ("b_ada", 24), ("pool_scale", 4), ("g_mix_pre_2", 8), ("g_mix_post_2", 8),
        ("g_ffn_pre_2", 8), ("g_ffn_post_2", 8), ("ffn_dw_b_2", 22), ("conv_b_2", 4), ("conv_ln_g_2", 4),
        ("conv_ln_b_2", 4), ("g_q_a_2", 3), ("g_kv_a_2", 2), ("q_norm_w", 1), ("k_norm_w", 1),
        ("ffn_dw_w_2", 66), ("conv_w_2", 124)]
NV = sum(n for _, n in VECS)


def stream():
    def cols(c0, c1):
        return np.arange(c0, c1)

    out = [("ada", [("w_ada", k * P, (k + 1) * P, cols(0, 2 * D))]) for k in range(KD)]

    def w(name, rows, columns):
        out.append(("w", [(name, rows[0], rows[1], columns)]))

    w("w_in", (0, D), cols(KI0, E1))
    for c in (QI0, QI0 + 256, K0, Q0, Q0 + 256):
        w("w_in", (0, D), cols(c, c + 256))
    out.extend(("ada", [("w_ada", k * P, (k + 2) * P, cols(2 * D, 3 * D))]) for k in range(0, KD, 2))
    for c in (GA0, GA0 + 256, U0, U0 + 256, GP0, GP0 + 256):
        w("w_in", (0, D), cols(c, c + 256))
    for c in range(0, D, 256):
        w("w_out", (0, D), cols(c, c + 256))
    for c in (1184, 672, 1440, 928, 0, 256):
        w("w_in_2", (0, D), cols(c, c + 256))
    w("w_in_2", (0, D), cols(512, 672))
    for c in range(2):
        heads = np.arange(4 * c, 4 * c + 4)[:, None] * 96
        w("w_q_b_2", (0, 384), np.concatenate([(heads + np.arange(HD)).ravel(), (heads + np.arange(HD, 96)).ravel()]))
    heads = np.arange(8)[:, None] * P
    w("w_kv_b_2", (0, 256), np.concatenate([(heads + np.arange(HD)).ravel(), (heads + np.arange(HD, P)).ravel()]))
    for c in range(0, D, 256):
        w("w_o_2", (0, D), cols(c, c + 256))
    for j in range(NJ):
        out.append(("w", [(n, 0, D, cols(j * P, (j + 1) * P)) for n in ("w_ffn_gate_2", "w_ffn_up_2")]))
    for e in range(KD):
        for h in range(2):
            w("w_ffn_down_2", (h * 11 * P, (h + 1) * 11 * P), cols(e * P, (e + 1) * P))
    w("w_ple_proj_2", (0, 256), cols(0, D))
    for c in range(0, D, 256):
        w("w_ple_gate_2", (0, D), cols(c, c + 256))
    return out


def constants():
    c = np.zeros((P, C_END), np.float32)
    c[:, C_ID:C_ID + P] = np.eye(P)
    for base, w in ((C_R64, 64), (C_R32, 32)):
        for m in range(P):
            if m % w < w // 2:
                c[m + w // 2, base + m] = -1.0
            else:
                c[m - w // 2, base + m] = 1.0
    q, k = np.arange(P)[:, None], np.arange(P)[None, :]
    c[:, C_TRI + 384:C_TRI + 512] = np.where(k <= q, 0.0, NEG)
    c[0:64, C_HS] = 1.0
    c[64:128, C_HS + 1] = 1.0
    c[:, C_ONE:C_ONE + 2] = 1.0
    half = 16
    inv = (10000.0 ** (-np.arange(0, 32, 2, dtype=np.float32) / np.float32(32))).astype(np.float32)
    c[:, C_FREQ] = inv[np.arange(P) % half]
    c[:, C_RC:C_RC + 16] = 1.0 / np.arange(1, 17)
    freqs = (10000.0 ** (-np.arange(32, dtype=np.float32) / np.float32(32))).astype(np.float32)
    ang = (np.arange(T, dtype=np.float32)[None, :] * freqs[np.arange(P) % 32][:, None]).astype(np.float32)
    c[:, C_COS:C_COS + T] = np.cos(ang.astype(np.float64))
    c[:, C_SIN:C_SIN + T] = np.sin(ang.astype(np.float64))
    return c


def build(nc, a, out):
    ctx = ExitStack()
    with ctx:
        def sb(name, shape, dt=F32):
            return ctx.enter_context(nc.sbuf_tensor(name, shape, dt))

        def sem(name):
            return ctx.enter_context(nc.semaphore(name))

        spot = [(nc.sbuf_base + 63) // 64 * 64]

        def place(name, shape, dt=F32, at=None):
            size = int(np.prod(shape[1:])) * 4
            off = spot[0] if at is None else at
            if at is None:
                spot[0] += (size + 31) // 32 * 32
            return nc.alloc_sbuf_tensor_at(name, shape, dt, offset=off), off

        raw, raw_at = place("raw", [P, RAWS, 2048])
        wlo, _ = place("wlo", [P, RAWS, 2048], F32R, raw_at)
        whi, _ = place("whi", [P, 2, 2048], F32R)
        R, _ = place("R", [P, KD, T])
        Bh, bh_at = place("Bh", [P, 8, T], F32R)
        Bl, bl_at = place("Bl", [P, 8, T], F32R)
        Bhf, _ = place("Bhf", [P, 8 * T], F32, bh_at)
        Blf, _ = place("Blf", [P, 8 * T], F32, bl_at)
        A, a_at = place("A", [P, 44 * T])
        Ar, _ = place("Ar", [P, 44 * T], F32R, a_at)
        M, _ = place("M", [P, 4 * T + 16])
        con, _ = place("con", [P, C_END])
        wpt, _ = place("wpt", [P, 4, P])
        vec, _ = place("vec", [P, NV])
        small, _ = place("small", [P, 400])
        nrm, _ = place("nrm", [P, 4, 40])
        assert spot[0] <= nc.sbuf_usable_end
        ps = ctx.enter_context(nc.psum_tensor("ps", [P, 8, 512], F32))

        def av(tile, n=1, w=T, of=A):
            lo = int(tile * T)
            return of[:, lo:lo + n * w].rearrange("p (n w) -> p n w", n=n)

        def ar(tile, n):
            return av(tile, n, of=Ar)

        ident = con[:, C_ID:C_ID + P]
        ones = con[:, C_ONE:C_ONE + 1]
        cosT, sinT = con[:, C_COS:C_COS + T], con[:, C_SIN:C_SIN + T]
        tri = con[:, C_TRI + 384:C_TRI + 512]
        rot64, rot32 = con[:, C_R64:C_R64 + P], con[:, C_R32:C_R32 + P]

        vat, at = {}, 0
        for name, n in VECS:
            vat[name] = at
            at += n

        def col(name, i=0, n=1):
            return vec[:, vat[name] + i:vat[name] + i + n]

        csil = small[:, 0:8]
        mcol = small[:, 8:16]
        gtcol = small[:, 24:32]
        mtmp = small[:, 32:48]
        wiT = small[:, 48:80].rearrange("p (t h) -> p t h", t=NT)
        m8 = small[:, 80:88]
        mx = small[:, 88:96].rearrange("p (b t) -> p b t", b=2)
        nb = small[:, 96:104].rearrange("p (b t) -> p b t", b=2)
        sm = small[:, 104:112].rearrange("p (b t) -> p b t", b=2)
        rsm = small[:, 112:120].rearrange("p (b t) -> p b t", b=2)
        rqs = small[:, 120:152].rearrange("p (t h) -> p t h", t=NT)
        mu = small[:, 152:156]
        sse = small[:, 168:176].rearrange("p (t h) -> p t h", t=NT)
        rqk = small[:, 176:216].rearrange("p (t h) -> p t h", t=NT)
        keep = small[:, 216:296]

        qiT, kid, kiw, sc = av(0, 4), av(4)[:, 0], av(5)[:, 0], av(6, 4)
        qT, kdup, vtok, gat = av(10, 4), av(14, 2), av(16)[:, 0], av(17, 4)
        uT, gp = av(21, 4), av(25, 4)
        kraw = uT[:, 3]
        aoh, aol = ar(21, 4), ar(25, 4)
        xr = av(29, 8)
        pmh, pml = ar(29, 4), ar(33, 4)
        pp = [A[:, 37 * T:37 * T + T + CP], A[:, 38 * T + CP:39 * T + 2 * CP]]
        acc = A[:, 40 * T:44 * T]
        gacc = M[:, 0:2 * T]
        t1, t2, rl = av(40)[:, 0], av(41)[:, 0], av(42, 2)
        kbx = av(43, 1)[:, 0].rearrange("p (t w) -> p t w", t=NT)
        vT, sqk = M[:, 2 * T:3 * T], M[:, 3 * T:4 * T]
        sqx = [vT, sqk]
        p1 = [A[:, 1280 * i:1280 * (i + 1)] for i in range(2)]
        pT1 = [A[:, 37 * T + 1280 * i:37 * T + 1280 * (i + 1)] for i in range(2)]
        ao = av(42)[:, 0]
        sqy = [av(40)[:, 0], av(41)[:, 0]]
        cpad = A[:, 0:4 * (T + CP)].rearrange("p (n w) -> p n w", n=4)
        cacc = av(4.25, 4)
        gt2, qa, kva = av(8.25, 2), av(10.25, 3), av(13.25, 2)
        qnh, qnl, kvh, kvl = ar(15.25, 3), ar(18.25, 3), ar(21.25, 2), ar(23.25, 2)
        qno, qro, kno, kro = av(25.25, 4), av(29.25, 2), av(31.25, 4), av(35.25)[:, 0]
        v2 = av(36.25, 4)
        s2a, s2b, s2c = av(40.25)[:, 0], av(41.25)[:, 0], av(42.25)[:, 0]
        sq2 = [s2a, s2b]
        p2 = [A[:, int(8.25 * T) + 1280 * i:int(8.25 * T) + 1280 * (i + 1)] for i in range(2)]
        pT2 = [A[:, int(13.25 * T) + 1280 * i:int(13.25 * T) + 1280 * (i + 1)] for i in range(2)]
        mix = av(25.25, 8)
        rB, tmpa = M[:, 0:T], M[:, T:2 * T]
        posi, posf = M[:, 2 * T:3 * T].bitcast(I32), M[:, 3 * T:4 * T]
        fh, fl = ar(0, NJ), ar(NJ, NJ)
        zg = M[:, 0:T + 16]
        cv = [M[:, T + 16:2 * T + 16], M[:, 2 * T + 16:3 * T + 16]]
        up = M[:, 3 * T + 16:4 * T + 16]
        rBf = sinT
        fo = Bhf[:, :].rearrange("p (n w) -> p n w", n=8)
        etok, htok, otok = av(0, 4, D), av(8, 4, D), av(32, 4, D)
        h3h, h3l = ar(16, 8), ar(24, 8)
        pTf = Blf[:, 0:2 * T].rearrange("p (k n) -> p k n", k=2)
        pTh, pTl = Bl[:, 2:4, :], Bl[:, 4:6, :]
        grow = Blf[:, 6 * T:8 * T]

        chunks, at = [], 0
        for kind, parts in stream():
            k, n = (parts[0][2] - parts[0][1]) // P, sum(len(x[3]) for x in parts)
            chunks.append((kind, a["stream"][at:at + P * k * n].rearrange("(p n) -> p n", p=P), k, n))
            at += P * k * n
        wchunk = [i for i, c in enumerate(chunks) if c[0] == "w"]
        wnum = {ci: w for w, ci in enumerate(wchunk)}
        W_FFN = len(wchunk) - NJ - 2 * KD - 5
        W_DOWN = W_FFN + NJ
        landed = [16 * (ci // RAWS + 1) for ci in range(len(chunks))]

        plan = ([("kiw", "A")] + [("qi", "A")] * 4 + [("k", "A"), ("vT", "A")] + [("q", "A")] * 4
                + [("ga", "A")] * 4 + [("u", "A")] * 4 + [("gp", "A")] * 4 + [("y", "D")] * 8
                + [("in2", "D")] * 14 + [("qb", "A")] * 6 + [("kn", "A")] * 4 + [("v2", "A")] * 4 + [("mix", "A")] * 8
                + [("ffn", "D")] * (2 * NJ) + [("down", "A")] * 8 + [("e", "A")] * 8 + [("plg", "A")] * 4
                + [("h3", "D")] * 8 + [("plh", "A")] * 12)
        aplan = ([("n0", "D"), ("mod", "D"), ("kirot", "D"), ("wiT", "D")] + [("qirot", "D")] * 4
                 + [("idx", "A")] * 24 + [("gmod", "D"), ("krot", "D")] + [("qrot", "D")] * 4
                 + [("kb", "D"), ("vtok", "A")] + [("pool", "D")] * 4
                 + [("n2", "A"), ("krrot", "D"), ("n3", "D"), ("n4", "D")] + [("q2rot", "D")] * 2
                 + [("lnm", "D"), ("lnv", "D"), ("n6", "D"), ("n7", "A"), ("n8", "D")])

        def takers(order):
            first, done, count = {}, [], {"A": 0, "D": 0}
            for i, (name, e) in enumerate(order):
                first.setdefault(name, i)
                count[e] += 1
                done.append((e, count[e]))
            return first, done

        first, done_at = takers(plan)
        afirst, adone_at = takers(aplan)
        per_chunk = ([1] + [2] * 11 + [2] * 4 + [2] * 7 + [3, 3, 8] + [2] * 4 + [2] * NJ + [0, 1] * KD + [8, 4, 12, 4, 4])
        chunk_end = [int(x) for x in np.cumsum(per_chunk)]

        s_raw = [sem(f"s_raw{i}") for i in range(RAWS)]
        s_hi = sem("s_hi")
        s_lo = sem("s_lo")
        s_half = sem("s_half")
        s_blk = sem("s_blk")
        s_ev = {"A": sem("s_evA"), "D": sem("s_evD")}
        s_aux = sem("s_aux")
        s_aev = {"A": sem("s_aevA"), "D": sem("s_aevD")}
        s_con, s_vec, s_wp = sem("s_con"), sem("s_vec"), sem("s_wp")
        s_x = [sem(f"s_x{i}") for i in range(4)]
        s_pos, s_p, s_grow, s_out = sem("s_pos"), sem("s_p"), sem("s_grow"), sem("s_out")
        dch, ach, pch = sem("dve_chain"), sem("act_chain"), sem("pool_chain")
        s_csil = sem("s_csil")
        s_v, s_rt, s_rs = sem("s_v"), sem("s_rt"), sem("s_rs")
        s_sq, s_cs = sem("s_sq"), sem("s_cs")
        s_mod = sem("s_mod")
        s_xr = sem("s_xr")
        s_hh, s_hl = sem("s_hh"), sem("s_hl")
        s_ki, s_kid, s_qi = sem("s_ki"), sem("s_kid"), sem("s_qi")
        s_idx = sem("s_idx")
        s_kd, s_qr = sem("s_kd"), sem("s_qr")
        s_pool, s_pld = sem("s_pool"), sem("s_pld")
        s_qk, s_msk, s_nb, s_exp = sem("s_qk"), sem("s_msk"), sem("s_nb"), sem("s_exp")
        s_pn, s_pt, s_pc, s_pv = sem("s_pn"), sem("s_pt"), sem("s_pc"), sem("s_pv")
        s_ao = sem("s_ao")
        s_mh, s_ml = sem("s_mh"), sem("s_ml")
        s_ang, s_tab, s_sg = sem("s_ang"), sem("s_tab"), sem("s_sg")
        s_cpz, s_qn, s_kr, s_kr4, s_q2 = sem("s_cpz"), sem("s_qn"), sem("s_kr"), sem("s_kr4"), sem("s_q2")
        s_cv, s_mus, s_mu, s_ln, s_ln2 = sem("s_cv"), sem("s_mus"), sem("s_mu"), sem("s_ln"), sem("s_ln2")
        s_h2, s_z, s_gl, s_fd, s_fh, s_fl = sem("s_h2"), sem("s_z"), sem("s_gl"), sem("s_fd"), sem("s_fh"), sem("s_fl")
        s_pTh, s_pTl, s_h3, s_ot = sem("s_pTh"), sem("s_pTl"), sem("s_h3"), sem("s_ot")

        def bank(name, i):
            return (first[name] + i) % 4

        def took(eng, name, i):
            e, v = done_at[first[name] + i]
            eng.wait_ge(s_ev[e], v)

        def abank(name, i=0):
            return 5 + (afirst[name] + i) % 3

        def atook(eng, name, i=0):
            e, v = adone_at[afirst[name] + i]
            eng.wait_ge(s_aev[e], v)

        def filled(eng, name, i):
            eng.wait_ge(s_blk, first[name] + i + 1)
            return ps[:, bank(name, i), :]

        def afilled(eng, name, i=0):
            eng.wait_ge(s_aux, afirst[name] + i + 1)
            return ps[:, abank(name, i), :]

        def used(eng, w):
            if W_DOWN <= w < W_DOWN + 2 * KD and (w - W_DOWN) % 2 == 0:
                eng.wait_ge(s_half, (w - W_DOWN) // 2 + 1)
            else:
                eng.wait_ge(s_blk, chunk_end[w])

        def obank(pair):
            return 3 if pair % 2 == 0 else 7

        block = ctx.enter_context(nc.Block())

        @block.sync
        def _(sp):
            sp.dma_start(vec[:, :], a["vecs"]).then_inc(s_vec, 16)
            for i in range(4):
                sp.dma_start(R[:, 2 * i:2 * i + 2, :], a["xT"][2 * i:2 * i + 2].rearrange("k p t -> p k t")) \
                    .then_inc(s_x[i], 16)
            sp.dma_start(con[:, :], a["con"]).then_inc(s_con, 16)
            for ci, (kind, src, k, n) in enumerate(chunks):
                if ci >= RAWS:
                    if chunks[ci - RAWS][0] == "w":
                        used(sp, wnum[ci - RAWS])
                    else:
                        sp.wait_ge(s_lo, ci - RAWS + 1)
                sp.dma_start(raw[:, ci % RAWS, 0:k * n], src).then_inc(s_raw[ci % RAWS], 16)
                if ci == 7:
                    sp.dma_start(wpt[:, :, :], a["w_pool"][0].rearrange("g c d -> c g d")).then_inc(s_wp, 16)
            for i in range(16):
                sp.wait_ge(s_ot, i + 1)
                c, t = i // 4, i % 4
                sp.dma_start(out[0, t * P:(t + 1) * P, c * 256:(c + 1) * 256],
                             otok[:, t, c * 256:(c + 1) * 256]).then_inc(s_out, 16)
            sp.wait_ge(s_out, 16 * 16)

        @block.gpsimd
        def _(g):
            pc = [0]

            def link(ins):
                pc[0] += 1
                ins.then_inc(pch, 1)
                g.wait_ge(pch, pc[0])

            for i in range(2):
                ins = g.memset(pp[i][:, 0:CP], 0.0)
                link(ins)
            for grp in range(4):
                took(g, "u", grp)
                if grp:
                    g.wait_ge(s_pld, grp)
                link(g.tensor_copy(pp[1][:, CP:CP + T], uT[:, grp, :]))
                for step in range(grp + 1):
                    d = 1 << step
                    src, dst = pp[(step + 1) % 2], pp[step % 2]
                    ins = g.tensor_tensor(dst[:, CP:CP + T], src[:, CP:CP + T], src[:, CP - d:CP - d + T], ALU.add)
                    if step < grp:
                        link(ins)
                ins.then_inc(s_pool, 1)
            took(g, "y", 0)
            g.dma_start(posi, a["positions_2"].partition_broadcast(P)).then_inc(s_pos, 16)
            for j in range(4):
                ins = g.memset(cpad[:, j, 0:CP], 0.0)
                if j < 3:
                    link(ins)
            ins.then_inc(s_cpz, 1)
            g.wait_ge(s_blk, first["down"])
            g.dma_start(pTf, a["pT"].rearrange("k p t -> p k t")).then_inc(s_p, 16)
            g.dma_start(grow, a["g_ple_2"][0].partition_broadcast(P)).then_inc(s_grow, 16)

        @block.scalar
        def _(act):
            f = nc.scalar.activation
            ac, hw, sqn, rt = [0], [0], [0], [0]

            def link(ins):
                ac[0] += 1
                ins.then_inc(ach, 1)
                act.wait_ge(ach, ac[0])

            def hi(n=1):
                for _ in range(n):
                    w = hw[0]
                    ci = wchunk[w]
                    act.wait_ge(s_raw[ci % RAWS], landed[ci])
                    if w >= 2:
                        used(act, w - 2)
                    k, nn = chunks[ci][2:]
                    f(whi[:, w % 2, 0:k * nn], raw[:, ci % RAWS, 0:k * nn], ACT.Copy).then_inc(s_hi, 1)
                    hw[0] += 1

            def square(tile, src, signal=None, depth=1):
                if sqn[0] >= depth:
                    act.wait_ge(s_cs, sqn[0] - depth + 1)
                sqn[0] += 1
                return f(tile, src, ACT.Square).then_inc(signal or s_sq, 1)

            def root(n=NT):
                rt[0] += 1
                act.wait_ge(s_v, rt[0])
                f(nrm[:, 1, 0:n], nrm[:, 0, 0:n], ACT.Sqrt).then_inc(s_rt, 1)

            evA = s_ev["A"]

            act.wait_ge(s_vec, 16)
            f(csil, col("c", 0, 8), ACT.Silu).then_inc(s_csil, 1)
            for k in range(KD):
                act.wait_ge(s_x[k // 2], 16)
                square(sqx[k % 2], R[:, k, :], depth=2)
            root()
            hi(1)
            act.wait_ge(s_mod, 1)
            for k in range(KD):
                act.wait_ge(s_xr, k + 1)
                f(Bh[:, k, :], xr[:, k, :], ACT.Identity, scale=mcol[:, k:k + 1],
                  bias=mtmp[:, k:k + 1]).then_inc(s_hh, 1)
            hi(1)
            f(kiw[0:72, :], filled(act, "kiw", 0)[0:72, :], ACT.Copy).then_inc(evA, 1)
            hi(1)
            for i in range(2):
                f(qiT[:, i, :], filled(act, "qi", i), ACT.Copy).then_inc(evA, 1)
            hi(1)
            act.wait_ge(s_ki, 1)
            f(kid[HD:P, :], kid[0:HD, :], ACT.Copy).then_inc(s_kid, 1)
            for i in range(2, 4):
                f(qiT[:, i, :], filled(act, "qi", i), ACT.Copy).then_inc(evA, 1)
            hi(1)
            src = filled(act, "k", 0)
            link(f(kraw, src, ACT.Copy, scale=col("k_norm_w")))
            square(sqk, src, evA, depth=1)
            f(vT, filled(act, "vT", 0), ACT.Copy).then_inc(evA, 1)
            hi(1)
            for n in range(24):
                w = (n // 8 + 2) * P
                src = afilled(act, "idx", n)
                if n >= 2:
                    act.wait_ge(s_idx, n - 1)
                f(rl[:, n % 2, 0:w], src[:, 0:w], ACT.Relu, scale=HD ** -0.5).then_inc(s_aev["A"], 1)
            for i in range(4):
                src = filled(act, "q", i)
                link(f(qT[:, i, :], src, ACT.Copy, scale=col("q_norm_w")))
                square(gat[:, i, :], src, evA, 99)
                if i % 2:
                    hi(1)
            for i in range(2):
                if i == 0:
                    act.wait_ge(s_cs, 11)
                f(gat[:, i, :], filled(act, "ga", i), ACT.Silu).then_inc(evA, 1)
            hi(1)
            root(40)
            for i in range(2, 4):
                f(gat[:, i, :], filled(act, "ga", i), ACT.Silu).then_inc(evA, 1)
            hi(1)
            atook(act, "kb")
            for i in range(2):
                for h in range(2):
                    f(kdup[h * HD:(h + 1) * HD, i, :], kraw[i * HD:(i + 1) * HD, :], ACT.Copy).then_inc(s_kd, 1)
            f(vtok, afilled(act, "vtok"), ACT.Copy).then_inc(s_aev["A"], 1)
            act.wait_ge(s_kd, 4)
            for i in range(4):
                f(uT[:, i, :], filled(act, "u", i), ACT.Copy).then_inc(evA, 1)
                if i % 2:
                    hi(1)
            for i in range(4):
                f(gp[:, i, :], filled(act, "gp", i), ACT.Silu).then_inc(evA, 1)
                if i % 2:
                    hi(1)
            for i in range(4):
                atook(act, "pool", i)
                f(pmh[:, i, :], uT[:, i, :], ACT.Copy).then_inc(s_mh, 1)

            def attention(base, scale_of, p, pT, out_pair):
                def evac(h):
                    for b, wd in enumerate((512, 512, 256)):
                        act.wait_ge(s_pt, base * 24 + 3 * h + b + 1)
                        if b == 0 and h >= 2:
                            act.wait_ge(s_pv, base * 8 + h - 1)
                        f(pT[h % 2][:, 512 * b:512 * b + wd], ps[:, b, 0:wd], ACT.Copy).then_inc(s_pc, 1)

                for h in range(8):
                    act.wait_ge(s_nb, base * 8 + h + 1)
                    for qt in QORD:
                        o, w = SOFF[qt], (qt + 1) * P
                        f(p[h % 2][:, o:o + w], p[h % 2][:, o:o + w], ACT.Exp, bias=nb[:, h % 2, qt:qt + 1],
                          scale=scale_of(h, qt), accum_out=sm[:, h % 2, qt:qt + 1]).then_inc(s_exp, 1)
                    if h:
                        evac(h - 1)
                    if h >= 3 and h % 2:
                        out_pair(h // 2 - 1)
                evac(7)
                out_pair(3)

            def out1(pair):
                act.wait_ge(s_ao, pair + 1)
                f(aoh[:, pair, :], ao, ACT.Copy).then_inc(s_mh, 1)

            attention(0, lambda h, qt: rqs[:, qt, h:h + 1], p1, pT1, out1)
            for k in range(KD):
                took(act, "y", k)
                f(Bh[:, k, :], R[:, k, :], ACT.Copy, scale=col("g_mix_pre_2", k)).then_inc(s_hh, 1)
                square(sqy[k % 2], R[:, k, :], depth=2)
                if k % 2:
                    hi(1)
            root()
            f(rB, afilled(act, "n2"), ACT.Copy).then_inc(s_aev["A"], 1)
            for j in range(4):
                took(act, "in2", 4 * (j // 2) + j % 2)
                f(gt2[:, j % 2, :], gt2[:, j % 2, :], ACT.Sigmoid).then_inc(s_sg, 1)
                if j % 2:
                    hi(2)
            act.wait_ge(s_ang, 2)
            f(sinT, s2a, ACT.Sin).then_inc(s_tab, 1)
            f(cosT, s2b, ACT.Sin).then_inc(s_tab, 1)
            act.wait_ge(s_tab, 2)
            for i in range(2):
                took(act, "in2", 8 + i)
                square(sq2[i % 2], qa[:, i, :], depth=2)
            hi(1)
            took(act, "in2", 10)
            square(sq2[0], qa[:, 2, :], depth=2)
            took(act, "in2", 11)
            square(sq2[1], kva[:, 0, :], depth=2)
            hi(1)
            took(act, "in2", 12)
            square(sq2[0], kva[:, 1, :], depth=2)
            root()
            root()
            for i in range(3):
                act.wait_ge(s_qn, i + 1) if i < 2 else atook(act, "n3")
                f(qnh[:, i, :], qa[:, i, :], ACT.Copy).then_inc(s_hh, 1)
            for i in range(2):
                act.wait_ge(s_qn, 3) if i < 1 else atook(act, "n4")
                f(kvh[:, i, :], kva[:, i, :], ACT.Copy).then_inc(s_hh, 1)
            hi(1)
            act.wait_ge(s_kr, 1)
            for g4 in range(3):
                f(kro[g4 * 32:g4 * 32 + 32, :], kro[96:128, :], ACT.Copy).then_inc(s_kr4, 1)
            for i, (what, n) in enumerate(QB):
                f((qno if what == "n" else qro)[:, n, :], filled(act, "qb", i), ACT.Copy).then_inc(evA, 1)
                if i % 3 == 2:
                    hi(1)
            for i in range(4):
                f(kno[:, i, :], filled(act, "kn", i), ACT.Copy).then_inc(evA, 1)
            for i in range(4):
                f(v2[:, i, :], filled(act, "v2", i), ACT.Copy).then_inc(evA, 1)
            hi(1)

            def out2(pair):
                act.wait_ge(s_pv, 8 + 2 * pair + 2)
                f(Bh[:, pair, :], ps[:, obank(pair), :], ACT.Copy).then_inc(s_mh, 1)

            attention(1, lambda h, qt: SCALE2, p2, pT2, out2)
            for j in range(4):
                act.wait_ge(s_ln, j + 1) if j < 3 else atook(act, "lnm")
                square(sq2[j % 2], cacc[:, j, :], depth=2)
            root()
            for j in range(4):
                act.wait_ge(s_ln2, j + 1) if j < 3 else atook(act, "lnv")
                link(f(cacc[:, j, :], cacc[:, j, :], ACT.Silu, scale=col("conv_ln_g_2", j),
                       bias=col("conv_ln_b_2", j)))
                f(Bh[:, 4 + j, :], cacc[:, j, :], ACT.Copy).then_inc(s_mh, 1)
            for k in range(KD):
                link(f(mix[:, k, :], filled(act, "mix", k), ACT.Copy))
                square(sq2[k % 2], ps[:, bank("mix", k), :], evA, 2)
                if k % 2:
                    hi(1)
            root()
            for k in range(KD):
                act.wait_ge(s_h2, k + 1)
                f(Bh[:, k, :], R[:, k, :], ACT.Copy, scale=col("g_ffn_pre_2", k)).then_inc(s_hh, 1)
                square(sq2[k % 2], R[:, k, :], depth=2)
            root()
            f(rBf, afilled(act, "n7"), ACT.Copy).then_inc(s_aev["A"], 1)
            for j in range(NJ):
                act.wait_ge(s_z, j + 1)
                f(cv[j % 2], cv[j % 2], ACT.Gelu_apprx_tanh).then_inc(s_gl, 1)
                hi(1)
                act.wait_ge(s_fd, j + 1)
                f(fh[:, j, :], cv[j % 2], ACT.Copy).then_inc(s_fh, 1)
            for e in range(KD):
                hi(1)
                link(f(fo[:, e, :], filled(act, "down", e), ACT.Copy))
                square(cv[e % 2], ps[:, bank("down", e), :], evA, 2)
                if e == 0:
                    act.wait_ge(s_p, 16)
                    for k in range(2):
                        f(pTh[:, k, :], pTf[:, k, :], ACT.Copy).then_inc(s_pTh, 1)
                hi(1)
            root()
            for i in range(8):
                t, hf = i // 2, i % 2
                src = filled(act, "e", i)
                link(f(etok[:, t, 512 * hf:512 * hf + 512], src, ACT.Copy))
                ins = f(cosT, src, ACT.Square, accum_out=sse[:, t, hf:hf + 1])
                ins.then_inc(evA, 1)
                act.wait_ge(evA, done_at[first["e"] + i][1])
            hi(1)
            for k in range(KD):
                act.wait_ge(s_h3, k + 1)
                f(h3h[:, k, :], R[:, k, :], ACT.Copy).then_inc(s_hh, 1)
            root()
            for i in range(16):
                c, t = i // 4, i % 4
                src = filled(act, "plg", i) if i < 4 else filled(act, "plh", i - 4)
                f(otok[:, t, c * 256:(c + 1) * 256], src[:, 0:256], ACT.Sigmoid).then_inc(evA, 1)
                if i % 4 == 3 and c < 2:
                    hi(1)
            assert hw[0] == len(wchunk), (hw[0], len(wchunk))

        @block.tensor
        def _(pe):
            mm = nc.tensor.matmul
            an, bn = [0], [0]

            def begin(name, i):
                b = first[name] + i
                assert b == bn[0], (name, i, b, bn[0])
                bn[0] += 1
                if b >= 4:
                    e, v = done_at[b - 4]
                    pe.wait_ge(s_ev[e], v)
                return ps[:, b % 4, :]

            def abegin(name, i=0):
                b = afirst[name] + i
                assert b == an[0], (name, i, b, an[0])
                an[0] += 1
                if b >= 3:
                    e, v = adone_at[b - 3]
                    pe.wait_ge(s_aev[e], v)
                return ps[:, 5 + b % 3, :]

            def exact(dst, wh, wl, xh, xl, start, stop):
                mm(dst, wh, xh, start=start, stop=False)
                mm(dst, wh, xl, start=False, stop=False)
                return mm(dst, wl, xh, start=False, stop=stop)

            def weights(w, sel):
                ci = wchunk[w]
                k, n = chunks[ci][2:]
                pe.wait_ge(s_lo, ci + 1)
                h = whi[:, w % 2, 0:k * n].rearrange("p (k n) -> p k n", k=k)
                lo = wlo[:, ci % RAWS, 0:k * n].rearrange("p (k n) -> p k n", k=k)
                return [(sel(h[:, i, :]), sel(lo[:, i, :])) for i in range(k)]

            def cols_of(c0, c1):
                return lambda v: v[:, c0:c1]

            def product(dst, wts, movers, k0=0, k1=None, start=True, stop=True):
                k1 = len(wts) if k1 is None else k1
                for k in range(k0, k1):
                    xh, xl, wait = movers[k]
                    if wait:
                        pe.wait_ge(*wait)
                    ins = exact(dst, *wts[k], xh, xl, start and k == k0, stop and k == k1 - 1)
                return ins

            def sums(tile, k, n):
                for t in range(NT):
                    ins = mm(ps[:, 4, t:t + 1], tile[:, t * P:(t + 1) * P], ones,
                             start=(k == 0 and t == 0), stop=(k == n - 1), skip_group_check=True)
                return ins

            def spread(name, rcol):
                dst = abegin(name)
                for t in range(NT):
                    ins = nc.tensor.transpose(dst[:, t * P:(t + 1) * P], rcol[:, t:t + 1].to_broadcast([P, P]), ident)
                ins.then_inc(s_aux, 1)

            def kcol(n):
                return keep[:, 8 * n:8 * n + NT]

            sqs = [0]

            def sum_sq(tile, k, n, free=None, via=None):
                if via is None:
                    sqs[0] += 1
                    pe.wait_ge(s_sq, sqs[0])
                else:
                    took(pe, *via)
                if free:
                    pe.wait_ge(*free)
                sums(tile, k, n).then_inc(s_cs, 1)

            pe.wait_ge(s_con, 16)
            for k in range(KD):
                sum_sq(sqx[k % 2], k, KD)
            pe.wait_ge(s_rs, 1)
            spread("n0", kcol(0))
            pe.wait_ge(s_lo, 8)
            dst = abegin("mod")
            for c in range(16):
                ins = mm(dst[:, c:c + 1], acc[:, c * P:(c + 1) * P], ones, start=True, stop=True)
            ins.then_inc(s_aux, 1)

            h1 = [(Bh[:, k, :], Bl[:, k, :], (s_hl, k + 1)) for k in range(KD)]
            w = [0]

            def chunk(names, movers=h1, step=P):
                for n, (name, i) in enumerate(names):
                    product(begin(name, i), weights(w[0], cols_of(n * step, (n + 1) * step)), movers) \
                        .then_inc(s_blk, 1)
                w[0] += 1

            dst = begin("kiw", 0)
            product(dst[0:72, :], weights(0, cols_of(0, 72)), h1).then_inc(s_blk, 1)
            w[0] = 1
            chunk([("qi", 0), ("qi", 1)])
            took(pe, "kiw", 0)
            mm(abegin("kirot")[0:HD, :], rot64[0:HD, 0:HD], kiw[0:HD, :], start=True, stop=True).then_inc(s_aux, 1)
            dst = abegin("wiT")
            for t in range(NT):
                ins = nc.tensor.transpose(dst[:, 8 * t:8 * t + 8], kiw[64:72, t * P:(t + 1) * P], ident[64:72, 64:72])
            ins.then_inc(s_aux, 1)
            chunk([("qi", 2), ("qi", 3)])

            def turn(name, i, rot, src, of):
                took(pe, *of)
                mm(abegin(name, i), rot, src, start=True, stop=True).then_inc(s_aux, 1)

            for i in range(2):
                turn("qirot", i, rot64, qiT[:, i, :], ("qi", i))
            chunk([("k", 0), ("vT", 0)])
            for i in range(2, 4):
                turn("qirot", i, rot64, qiT[:, i, :], ("qi", i))
            pe.wait_ge(s_kid, 1)
            pe.wait_ge(s_qi, 4)
            for n in range(24):
                qt, h = n // 8 + 1, n % 8
                b0, wd = HD * (h % 2), (qt + 1) * P
                mm(abegin("idx", n)[:, 0:wd], qiT[b0:b0 + HD, h // 2, qt * P:(qt + 1) * P],
                   kid[b0:b0 + HD, 0:wd], start=True, stop=True).then_inc(s_aux, 1)
            chunk([("q", 0), ("q", 1)])
            chunk([("q", 2), ("q", 3)])

            def head_sums(i, tile, via):
                took(pe, *via)
                for t in range(NT):
                    ins = mm(ps[:, 4, t * 10 + 2 * i:t * 10 + 2 * i + 2], tile[:, t * P:(t + 1) * P],
                             con[:, C_HS:C_HS + 2], start=(i == 0 and t == 0), stop=True, skip_group_check=True)
                return ins

            pe.wait_ge(s_v, 1)
            head_sums(0, sqk, ("k", 0)).then_inc(s_cs, 1)
            for i in range(3):
                head_sums(1 + i, gat[:, i, :], ("q", i)).then_inc(s_cs, 1)
            chunk([("ga", 0), ("ga", 1)])
            head_sums(4, gat[:, 3, :], ("q", 3)).then_inc(s_cs, 1)
            pe.wait_ge(s_lo, 18)
            dst = abegin("gmod")
            for c in range(8):
                ins = mm(dst[:, c:c + 1], gacc[:, c * P:(c + 1) * P], ones, start=True, stop=True)
            ins.then_inc(s_aux, 1)
            turn("krot", 0, rot64, kraw, ("k", 0))
            turn("qrot", 0, rot64, qT[:, 0, :], ("q", 0))
            chunk([("ga", 2), ("ga", 3)])
            for i in range(1, 4):
                turn("qrot", i, rot64, qT[:, i, :], ("q", i))
            pe.wait_ge(s_rs, 2)
            dst = abegin("kb")
            for t in range(NT):
                ins = nc.tensor.transpose(dst[:, t * P:(t + 1) * P], kbx[:, t, :], ident)
            ins.then_inc(s_aux, 1)
            dst = abegin("vtok")
            took(pe, "vT", 0)
            for t in range(NT):
                ins = nc.tensor.transpose(dst[:, t * P:(t + 1) * P], vT[:, t * P:(t + 1) * P], ident)
            ins.then_inc(s_aux, 1)
            chunk([("u", 0), ("u", 1)])
            chunk([("u", 2), ("u", 3)])
            chunk([("gp", 0), ("gp", 1)])
            pe.wait_ge(s_wp, 16)

            def pool(i):
                pe.wait_ge(s_pld, i + 1)
                mm(abegin("pool", i), wpt[:, i, :], uT[:, i, :], start=True, stop=True).then_inc(s_aux, 1)

            pool(0)
            chunk([("gp", 2), ("gp", 3)])
            for i in range(1, 4):
                pool(i)

            def attention(base, scores, values, p, pT, pair_free):
                def qk(h):
                    for n, qt in enumerate(QORD):
                        b = (4, 5, 5, 6)[n]
                        if h and n != 2:
                            pe.wait_ge(s_msk, base * 32 + 4 * (h - 1) + (1, 3, 3, 4)[n])
                        o = SOFF[qt] % 512
                        scores(h, qt, ps[:, b, o:o + (qt + 1) * P]).then_inc(s_qk, 1)

                def turn_p(h):
                    pe.wait_ge(s_pn, base * 32 + 4 * h + 4)
                    for b, kts in enumerate(((0,), (1, 3), (2,))):
                        if h:
                            pe.wait_ge(s_pc, base * 24 + 3 * (h - 1) + b + 1)
                        for kt in kts:
                            for qt in range(kt, NT):
                                o = TOFF[kt] % 512 + P * (qt - kt)
                                s = SOFF[qt] + P * kt
                                ins = nc.tensor.transpose(ps[:, b, o:o + P], p[h % 2][:, s:s + P], ident)
                        ins.then_inc(s_pt, 1)

                def pv(h):
                    if h % 2 == 0 and h >= 4:
                        pe.wait_ge(*pair_free(h // 2 - 2))
                    pe.wait_ge(s_pc, base * 24 + 3 * h + 3)
                    for kt in range(NT):
                        ins = mm(ps[HD * (h % 2):HD * (h % 2) + HD, obank(h // 2), P * kt:T], values(h, kt),
                                 pT[h % 2][:, TOFF[kt]:TOFF[kt] + T - P * kt], start=(kt == 0), stop=(kt == NT - 1),
                                 skip_group_check=True)
                    ins.then_inc(s_pv, 1)

                qk(0)
                for h in range(8):
                    if h < 7:
                        qk(h + 1)
                    if h:
                        pv(h - 1)
                    turn_p(h)
                pv(7)

            def scores1(h, qt, dst):
                b0 = HD * (h % 2)
                return mm(dst, qT[b0:b0 + HD, h // 2, qt * P:(qt + 1) * P], kdup[b0:b0 + HD, h // 4, 0:(qt + 1) * P],
                          start=True, stop=True)

            for i in range(4):
                took(pe, "gp", i)
            for i in range(2, 4):
                atook(pe, "pool", i)
            pe.wait_ge(s_kd, 4)
            pe.wait_ge(s_qr, 4)
            attention(0, scores1, lambda h, kt: vtok[:, kt * P + HD * (h // 4):kt * P + HD * (h // 4) + HD], p1, pT1,
                      lambda pair: (s_ao, pair + 1))
            mixer1 = ([(pmh[:, k, :], pml[:, k, :], (s_ml, k + 1)) for k in range(4)]
                      + [(aoh[:, k, :], aol[:, k, :], (s_ml, k + 5)) for k in range(4)])
            for i in range(0, 8, 2):
                chunk([("y", i), ("y", i + 1)], mixer1)
                if i:
                    for j in (i - 2, i - 1):
                        sum_sq(sqy[j % 2], j, KD, (s_v, 2) if j == 0 else None)
            hg = [(Bh[:, k, :], Bl[:, k, :], (s_hl, 8 + k + 1)) for k in range(KD)]
            product(begin("in2", 0), weights(w[0], cols_of(0, P)), hg).then_inc(s_blk, 1)
            for j in (6, 7):
                sum_sq(sqy[j % 2], j, KD)
            product(begin("in2", 1), weights(w[0], cols_of(P, 2 * P)), hg).then_inc(s_blk, 1)
            w[0] += 1
            pe.wait_ge(s_rs, 3)
            spread("n2", kcol(2))
            for i in range(2, 12, 2):
                chunk([("in2", i), ("in2", i + 1)], hg)
            for i in range(2):
                sum_sq(sq2[i % 2], i, 3, (s_v, 3))
            product(begin("in2", 12), weights(w[0], cols_of(0, P)), hg).then_inc(s_blk, 1)
            sum_sq(sq2[0], 2, 3)
            product(begin("in2", 13), weights(w[0], cols_of(32, 160)), hg).then_inc(s_blk, 1)
            w[0] += 1
            sum_sq(sq2[1], 0, 2, (s_v, 4))
            sum_sq(sq2[0], 1, 2)
            turn("krrot", 0, rot32, kro, ("in2", 13))
            pe.wait_ge(s_rs, 4)
            spread("n3", kcol(3))
            pe.wait_ge(s_rs, 5)
            spread("n4", kcol(4))
            qn = [(qnh[:, k, :], qnl[:, k, :], (s_hl, 16 + k + 1)) for k in range(3)]
            kvn = [(kvh[:, k, :], kvl[:, k, :], (s_hl, 19 + k + 1)) for k in range(2)]

            for c in range(2):
                chunk([("qb", 3 * c + n) for n in range(3)], qn)
            for i in range(4):
                product(begin("kn", i), weights(w[0], cols_of(P * i, P * i + P)), kvn).then_inc(s_blk, 1)
            for i in range(2):
                turn("q2rot", i, rot32, qro[:, i, :], ("qb", 3 * i + 2))
            for t in range(NT):
                wts = weights(w[0], cols_of(512, 1024))
                dst = begin("v2", t)
                for k in range(2):
                    sl = slice(t * P, (t + 1) * P)
                    (wh, wl), (xh, xl, _) = wts[k], kvn[k]
                    mm(dst, xh[:, sl], wh, start=(k == 0), stop=False)
                    mm(dst, xh[:, sl], wl, start=False, stop=False)
                    ins = mm(dst, xl[:, sl], wh, start=False, stop=(k == 1))
                ins.then_inc(s_blk, 1)
            w[0] += 1

            def scores2(h, qt, dst):
                b0, r0 = HD * (h % 2), 32 * (h % 4)
                q0, n = qt * P, (qt + 1) * P
                mm(dst, qno[b0:b0 + HD, h // 2, q0:q0 + P], kno[b0:b0 + HD, h // 2, 0:n], start=True, stop=False)
                return mm(dst, qro[r0:r0 + 32, h // 4, q0:q0 + P], kro[r0:r0 + 32, 0:n], start=False, stop=True,
                          tile_position=(r0, 0))

            for i in range(4):
                took(pe, "v2", i)
            atook(pe, "q2rot", 1)
            pe.wait_ge(s_kr4, 3)
            pe.wait_ge(s_q2, 2)
            attention(1, scores2, lambda h, kt: v2[:, kt, HD * h:HD * h + HD], p2, pT2,
                      lambda pair: (s_ml, 8 + pair + 1))
            mixer2 = [(Bh[:, k, :], Bl[:, k, :], (s_ml, 8 + k + 1)) for k in range(KD)]
            pe.wait_ge(s_v, 5)
            for j in range(4):
                pe.wait_ge(s_cv, j + 1)
                ins = sums(cacc[:, j, :], j, 4)
            ins.then_inc(s_mus, 1)
            halves = []
            for i in range(4):
                dst = begin("mix", i)
                wts = weights(w[0] + i // 2, cols_of(P * (i % 2), P * (i % 2) + P))
                halves.append((dst, wts))
                product(dst, wts, mixer2, 0, 4, stop=False)
                if i == 1:
                    pe.wait_ge(s_mu, 1)
                    spread("lnm", mu)
            for j in range(4):
                sum_sq(sq2[j % 2], j, 4)
            pe.wait_ge(s_rs, 6)
            spread("lnv", kcol(5))
            for i in range(4):
                product(*halves[i], mixer2, 4, 8, start=False).then_inc(s_blk, 1)
                if i >= 2:
                    sum_sq(sq2[i % 2], i - 2, KD, (s_v, 6), via=("mix", i - 2))
            w[0] += 2
            for i in range(4, 8, 2):
                chunk([("mix", i), ("mix", i + 1)], mixer2)
                for j in (i - 2, i - 1):
                    sum_sq(sq2[j % 2], j, KD, via=("mix", j))
            for j in (6, 7):
                sum_sq(sq2[j % 2], j, KD, via=("mix", j))
            pe.wait_ge(s_rs, 7)
            spread("n6", kcol(6))
            h2 = [(Bh[:, k, :], Bl[:, k, :], (s_hl, 21 + k + 1)) for k in range(KD)]
            pair = [(begin("ffn", i), weights(w[0], cols_of(P * i, P * i + P))) for i in range(2)]
            for k in range(KD):
                for i in range(2):
                    ins = product(*pair[i], h2, k, k + 1, start=(k == 0), stop=(k == KD - 1))
                    if k == KD - 1:
                        ins.then_inc(s_blk, 1)
                sum_sq(sq2[k % 2], k, KD, (s_v, 7))
            w[0] += 1
            pe.wait_ge(s_rs, 8)
            spread("n7", kcol(7))
            for j in range(1, NJ):
                chunk([("ffn", 2 * j), ("ffn", 2 * j + 1)], h2)
            ff = [(fh[:, k, :], fl[:, k, :], (s_fl, k + 1)) for k in range(NJ)]
            for e in range(KD):
                dst = begin("down", e)
                product(dst, weights(w[0], cols_of(0, P)), ff[0:11], stop=False).then_inc(s_half, 1)
                product(dst, weights(w[0] + 1, cols_of(0, P)), ff[11:22], start=False).then_inc(s_blk, 1)
                w[0] += 2
                if e:
                    sum_sq(cv[(e - 1) % 2], e - 1, KD, (s_v, 8), via=("down", e - 1))
            sum_sq(cv[1], 7, KD, via=("down", 7))
            pe.wait_ge(s_pTl, 2)
            for i in range(8):
                t, hf = i // 2, i % 2
                wts = weights(w[0], cols_of(512 * hf, 512 * hf + 512))
                dst = begin("e", i)
                for k in range(2):
                    sl = slice(t * P, (t + 1) * P)
                    wh, wl = wts[k]
                    mm(dst, pTh[:, k, sl], wh, start=(k == 0), stop=False)
                    mm(dst, pTh[:, k, sl], wl, start=False, stop=False)
                    ins = mm(dst, pTl[:, k, sl], wh, start=False, stop=(k == 1))
                ins.then_inc(s_blk, 1)
                if i == 3:
                    pe.wait_ge(s_rs, 9)
                    spread("n8", kcol(8))
            w[0] += 1
            for c in range(4):
                for t in range(NT):
                    wts = weights(w[0], cols_of(0, 256))
                    dst = (begin("plg", t) if c == 0 else begin("plh", 4 * (c - 1) + t))[:, 0:256]
                    for k in range(KD):
                        pe.wait_ge(s_hl, 29 + k + 1)
                        sl = slice(t * P, (t + 1) * P)
                        wh, wl = wts[k]
                        mm(dst, h3h[:, k, sl], wh, start=(k == 0), stop=False)
                        mm(dst, h3h[:, k, sl], wl, start=False, stop=False)
                        ins = mm(dst, h3l[:, k, sl], wh, start=False, stop=(k == KD - 1))
                    ins.then_inc(s_blk, 1)
                w[0] += 1
                if c == 0:
                    for i in range(8):
                        t, hf = i // 2, i % 2
                        dst = begin("h3", i)
                        for k in range(4):
                            ins = nc.tensor.transpose(dst[:, k * P:(k + 1) * P], R[:, 4 * hf + k, t * P:(t + 1) * P],
                                                      ident)
                        ins.then_inc(s_blk, 1)
            assert w[0] == len(wchunk) and an[0] == len(aplan) and bn[0] == len(plan)

        @block.vector
        def _(dve):
            v = nc.vector
            dc, lw, ci_at, nn = [0], [0], [0], [0]
            evD, aevD = s_ev["D"], s_aev["D"]

            def link(ins):
                dc[0] += 1
                ins.then_inc(dch, 1)
                dve.wait_ge(dch, dc[0])

            def lo(n=1):
                for _ in range(n):
                    w = lw[0]
                    ci = wchunk[w]
                    assert ci == ci_at[0], (ci, ci_at[0])
                    dve.wait_ge(s_hi, w + 1)
                    k, m = chunks[ci][2:]
                    src = raw[:, ci % RAWS, 0:k * m]
                    v.tensor_tensor(wlo[:, ci % RAWS, 0:k * m], src, whi[:, w % 2, 0:k * m].bitcast(F32),
                                    ALU.subtract).then_inc(s_lo, 1)
                    lw[0] += 1
                    ci_at[0] += 1

            def ada(dst, k0, parts, width, cont):
                ci = ci_at[0]
                dve.wait_ge(s_raw[ci % RAWS], landed[ci])
                for i in range(parts):
                    src = raw[:, ci % RAWS, i * width:(i + 1) * width]
                    c = csil[:, k0 + i:k0 + i + 1]
                    if i == 0 and not cont:
                        ins = v.tensor_scalar(dst, src, c, None, ALU.mult)
                    else:
                        ins = v.scalar_tensor_tensor(dst, src, c, dst, ALU.mult, ALU.add)
                    if i < parts - 1:
                        link(ins)
                ins.then_inc(s_lo, 1)
                ci_at[0] += 1
                dve.wait_ge(s_lo, ci_at[0])

            def variance(src, n, count=NT):
                v.tensor_scalar(nrm[:, 0, 0:count], src, 1.0 / n, EPS, ALU.mult, ALU.add).then_inc(s_v, 1)

            def rstd(dst, count=NT):
                nn[0] += 1
                dve.wait_ge(s_rt, nn[0])
                va, ro, r, tt = (nrm[:, i, 0:count] for i in range(4))
                link(v.reciprocal(r, ro))
                link(v.tensor_tensor(tt, r, r, ALU.mult))
                link(v.tensor_tensor(tt, tt, va, ALU.mult))
                link(v.tensor_scalar(tt, tt, -0.5, 1.5, ALU.mult, ALU.add))
                return v.tensor_tensor(dst, r, tt, ALU.mult)

            def norm(summed, count, idx):
                dve.wait_ge(s_cs, summed)
                variance(ps[:, 4, 0:NT], count)
                rstd(keep[:, 8 * idx:8 * idx + NT]).then_inc(s_rs, 1)

            def rope(dst, src, name, i, parts=P, cos=cosT, sin=sinT, tmp=(t1, t2)):
                rot = afilled(dve, name, i)
                link(v.tensor_tensor(tmp[0][0:parts, :], src, cos[0:parts, :], ALU.mult))
                v.tensor_tensor(tmp[1][0:parts, :], rot[0:parts, :], sin[0:parts, :], ALU.mult).then_inc(aevD, 1)
                atook(dve, name, i)
                return v.tensor_tensor(dst, tmp[0][0:parts, :], tmp[1][0:parts, :], ALU.add)

            dve.wait_ge(s_con, 16)
            dve.wait_ge(s_vec, 16)
            dve.wait_ge(s_csil, 1)
            for k in range(KD):
                ada(acc, k, 1, 2 * D, k > 0)
                if k == 1:
                    norm(8, D, 0)
                if k == 4:
                    v.tensor_copy(rB, afilled(dve, "n0")).then_inc(aevD, 1)
                    atook(dve, "n0")
            for k in range(KD):
                if k == 1:
                    mod = afilled(dve, "mod")
                    v.tensor_tensor(mtmp, mod[:, 0:16], col("b_ada", 0, 16), ALU.add).then_inc(aevD, 1)
                    atook(dve, "mod")
                    v.scalar_tensor_tensor(mcol, mtmp[:, 8:16], 1.0, col("norm_w", 0, 8), ALU.add,
                                           ALU.mult).then_inc(s_mod, 1)
                v.tensor_tensor(xr[:, k, :], R[:, k, :], rB, ALU.mult).then_inc(s_xr, 1)
            lo(1)
            dve.wait_ge(s_xr, KD)
            dve.wait_ge(s_mod, 1)
            for k in range(KD):
                dve.wait_ge(s_hh, k + 1)
                link(v.tensor_scalar(xr[:, k, :], xr[:, k, :], mcol[:, k:k + 1], mtmp[:, k:k + 1], ALU.mult, ALU.add))
                v.tensor_tensor(Bl[:, k, :], xr[:, k, :], Bh[:, k, :].bitcast(F32), ALU.subtract).then_inc(s_hl, 1)
            lo(2)
            took(dve, "kiw", 0)
            rope(kid[0:HD, :], kiw[0:HD, :], "kirot", 0, HD).then_inc(s_ki, 1)
            v.tensor_scalar(small[:, 48:80], afilled(dve, "wiT")[:, 0:32], 8 ** -0.5, None, ALU.mult).then_inc(aevD, 1)
            atook(dve, "wiT")
            lo(1)
            for i in range(4):
                took(dve, "qi", i)
                if i:
                    dve.wait_ge(s_qi, i)
                rope(qiT[:, i, :], qiT[:, i, :], "qirot", i).then_inc(s_qi, 1)
                if i == 1:
                    lo(1)
            lo(1)
            for n in range(24):
                qt, h = n // 8 + 1, n % 8
                wd = (qt + 1) * P
                atook(dve, "idx", n)
                dst, r, wcol = sc[:, qt, 0:wd], rl[:, n % 2, 0:wd], wiT[:, qt, h:h + 1]
                if h == 0:
                    v.tensor_scalar(dst, r, wcol, None, ALU.mult).then_inc(s_idx, 1)
                else:
                    dve.wait_ge(s_idx, n)
                    v.scalar_tensor_tensor(dst, r, wcol, dst, ALU.mult, ALU.add).then_inc(s_idx, 1)
                if h == 7:
                    dve.wait_ge(s_idx, n + 1)
                    diag = sc[:, qt, qt * P:wd]
                    link(v.tensor_tensor(diag, diag, tri, ALU.add))
            for k in range(0, KD, 2):
                ada(gacc, k, 2, D, k > 0)
            tk = [0]

            def topk(n):
                for _ in range(n):
                    qt, r = tk[0] // (TOPK // 8) + 1, tk[0] % (TOPK // 8)
                    s = sc[:, qt, 0:(qt + 1) * P]
                    link(v.max(m8, s))
                    link(v.match_replace(s, m8, s, TAKEN))
                    if r == TOPK // 8 - 1:
                        link(v.tensor_scalar(s, s, -2e38, NEG, ALU.is_gt, ALU.mult))
                    tk[0] += 1

            lo(1)
            topk(5)
            gm = afilled(dve, "gmod")
            v.tensor_tensor(gtcol, gm[:, 0:8], col("b_ada", 16, 8), ALU.add).then_inc(aevD, 1)
            took(dve, "k", 0)
            link(rope(kraw, kraw, "krot", 0))
            took(dve, "q", 0)
            rope(qT[:, 0, :], qT[:, 0, :], "qrot", 0).then_inc(s_qr, 1)
            lo(1)
            dve.wait_ge(s_cs, 13)
            variance(ps[:, 4, 0:40], HD, 40)
            topk(3)
            link(rstd(small[:, 176:216], 40))
            link(v.tensor_scalar(rqs, rqk[:, :, 2:10], SCALE1, None, ALU.mult))
            for h in range(2):
                ins = v.tensor_copy(kbx[:, :, h * HD:(h + 1) * HD], rqk[:, :, h:h + 1].to_broadcast([P, NT, HD]))
                if h == 0:
                    link(ins)
            ins.then_inc(s_rs, 1)
            for i in range(1, 4):
                dve.wait_ge(s_qr, i)
                took(dve, "q", i)
                rope(qT[:, i, :], qT[:, i, :], "qrot", i).then_inc(s_qr, 1)
            v.tensor_tensor(kraw, kraw, afilled(dve, "kb"), ALU.mult).then_inc(aevD, 1)
            lo(1)
            topk(9)
            lo(1)
            topk(9)

            def pooled(g):
                wdw = 2 << g
                S = pp[g % 2][:, CP:CP + T]
                dve.wait_ge(s_pool, g + 1)
                took(dve, "u", g)
                link(v.tensor_tensor(t1[:, 0:wdw], S[:, 0:wdw], con[:, C_RC:C_RC + wdw], ALU.mult))
                link(v.tensor_tensor(uT[:, g, 0:wdw], t1[:, 0:wdw], uT[:, g, 0:wdw], ALU.subtract))
                v.scalar_tensor_tensor(uT[:, g, wdw:T], S[:, wdw:T], 1.0 / wdw, uT[:, g, wdw:T], ALU.mult,
                                       ALU.subtract).then_inc(s_pld, 1)

            def mixed(g):
                dve.wait_ge(s_pld, g + 1)
                m = afilled(dve, "pool", g)
                took(dve, "gp", g)
                v.scalar_tensor_tensor(uT[:, g, :], m, col("pool_scale", g), gp[:, g, :], ALU.mult,
                                       ALU.mult).then_inc(aevD, 1)

            pooled(0)
            lo(1)
            topk(6)
            pooled(1)
            pooled(2)
            topk(4)
            pooled(3)
            lo(1)
            topk(9)
            mixed(0)
            lo(1)
            topk(48 - tk[0])
            for g in range(1, 4):
                mixed(g)
            for g in range(4):
                dve.wait_ge(s_mh, g + 1)
                v.tensor_tensor(pml[:, g, :], uT[:, g, :], pmh[:, g, :].bitcast(F32), ALU.subtract).then_inc(s_ml, 1)

            def attention(base, mask, negate, p, out_pair, between):
                def masked(h):
                    if h >= 2:
                        dve.wait_ge(s_pt, base * 24 + 3 * (h - 1))
                    for n, qt in enumerate(QORD):
                        o, wd = SOFF[qt], (qt + 1) * P
                        dve.wait_ge(s_qk, base * 32 + 4 * h + (1, 3, 3, 4)[n])
                        b = (4, 5, 5, 6)[n]
                        v.tensor_tensor_reduce(out=p[h % 2][:, o:o + wd], in0=ps[:, b, o % 512:o % 512 + wd],
                                               in1=mask(qt), scale=1.0, scalar=-3e38, op0=ALU.add, op1=ALU.max,
                                               accum_out=mx[:, h % 2, qt:qt + 1]).then_inc(s_msk, 1)
                    dve.wait_ge(s_msk, base * 32 + 4 * h + 4)
                    negate(h).then_inc(s_nb, 1)

                def normalised(h):
                    dve.wait_ge(s_exp, base * 32 + 4 * h + 4)
                    link(v.reciprocal(rsm[:, h % 2, :], sm[:, h % 2, :]))
                    for qt in QORD:
                        o, wd = SOFF[qt], (qt + 1) * P
                        s = p[h % 2][:, o:o + wd]
                        v.tensor_scalar(s, s, rsm[:, h % 2, qt:qt + 1], None, ALU.mult).then_inc(s_pn, 1)

                masked(0)
                for h in range(8):
                    between(h)
                    normalised(h)
                    if h < 7:
                        masked(h + 1)
                    if h >= 3 and h % 2:
                        out_pair(h // 2 - 1)
                out_pair(3)

            def negate1(h):
                return v.scalar_tensor_tensor(nb[:, h % 2, :], mx[:, h % 2, :], -1.0, rqs[:, :, h], ALU.mult, ALU.mult)

            def out1(pair):
                dve.wait_ge(s_pv, 2 * pair + 2)
                if pair:
                    dve.wait_ge(s_ml, 4 + pair)
                v.tensor_tensor(ao, ps[:, obank(pair), :], gat[:, pair, :], ALU.mult).then_inc(s_ao, 1)
                dve.wait_ge(s_mh, 4 + pair + 1)
                v.tensor_tensor(aol[:, pair, :], ao, aoh[:, pair, :].bitcast(F32), ALU.subtract).then_inc(s_ml, 1)

            attention(0, lambda qt: tri if qt == 0 else sc[:, qt, 0:(qt + 1) * P], negate1, p1, out1, lambda h: None)
            lo(1) if lw[0] < 14 else None
            for k in range(KD):
                v.scalar_tensor_tensor(R[:, k, :], filled(dve, "y", k), gtcol[:, k:k + 1], R[:, k, :], ALU.mult,
                                       ALU.add).then_inc(evD, 1)
                took(dve, "y", k)
                dve.wait_ge(s_hh, 8 + k + 1)
                v.scalar_tensor_tensor(Bl[:, k, :], R[:, k, :], col("g_mix_pre_2", k), Bh[:, k, :].bitcast(F32),
                                       ALU.mult, ALU.subtract).then_inc(s_hl, 1)
                if k % 2:
                    lo(1)
            norm(21, D, 2)
            atook(dve, "n2")

            def tmul(dst, i, signal):
                v.tensor_tensor(dst, filled(dve, "in2", i), rB, ALU.mult).then_inc(signal, 1)

            cs = [0]

            def conv(n):
                for _ in range(n):
                    if cs[0] == 4 * CW:
                        return
                    j, t = cs[0] // CW, cs[0] % CW
                    src = cpad[:, j, CP - (CW - 1) + t:CP - (CW - 1) + t + T]
                    wcol = col("conv_w_2", t * 4 + j)
                    if t == 0:
                        link(v.tensor_scalar(cacc[:, j, :], src, wcol, col("conv_b_2", j), ALU.mult, ALU.add))
                    elif t < CW - 1:
                        link(v.scalar_tensor_tensor(cacc[:, j, :], src, wcol, cacc[:, j, :], ALU.mult, ALU.add))
                    else:
                        v.scalar_tensor_tensor(cacc[:, j, :], src, wcol, cacc[:, j, :], ALU.mult,
                                               ALU.add).then_inc(s_cv, 1)
                    cs[0] += 1

            dve.wait_ge(s_cpz, 1)
            for half in range(2):
                for i in range(2):
                    tmul(gt2[:, i, :], 4 * half + i, evD)
                lo(1)
                if half == 0:
                    dve.wait_ge(s_pos, 16)
                    link(v.tensor_copy(posf, posi))
                    link(v.tensor_scalar(posf, posf, con[:, C_FREQ:C_FREQ + 1], None, ALU.mult))
                    for dst, quarter in ((s2a, 0.0), (s2b, 0.25)):
                        link(v.tensor_scalar(s2c, posf, INV2PI, quarter, ALU.mult, ALU.add))
                        link(v.tensor_scalar(s2c, s2c, ROUND, None, ALU.add))
                        link(v.tensor_scalar(s2c, s2c, -ROUND, None, ALU.add))
                        src = posf
                        for part in TWOPI:
                            link(v.scalar_tensor_tensor(dst, s2c, -part, src, ALU.mult, ALU.add))
                            src = dst
                        link(v.tensor_scalar(dst, dst, quarter * 2 * np.pi, PI32, ALU.add, ALU.min))
                        v.tensor_scalar(dst, dst, -PI32, None, ALU.max).then_inc(s_ang, 1)
                for i in range(2):
                    tmul(tmpa, 4 * half + 2 + i, evD)
                    took(dve, "in2", 4 * half + 2 + i)
                    dve.wait_ge(s_sg, 2 * half + i + 1)
                    link(v.tensor_tensor(cpad[:, 2 * half + i, CP:CP + T], tmpa, gt2[:, i, :], ALU.mult))
                lo(1)
                conv(16)
            conv(4)
            for i in range(2):
                tmul(qa[:, i, :], 8 + i, evD)
            lo(1)
            conv(6)
            tmul(qa[:, 2, :], 10, evD)
            tmul(kva[:, 0, :], 11, evD)
            lo(1)
            tmul(kva[:, 1, :], 12, evD)
            tmul(kro, 13, evD)
            took(dve, "in2", 13)
            norm(24, 384, 3)
            norm(26, 256, 4)
            dve.wait_ge(s_tab, 2)
            rope(kro, kro, "krrot", 0, tmp=(s2c, tmpa)).then_inc(s_kr, 1)
            b = afilled(dve, "n3")
            for i in range(3):
                v.scalar_tensor_tensor(qa[:, i, :], qa[:, i, :], col("g_q_a_2", i), b, ALU.mult, ALU.mult) \
                    .then_inc(s_qn if i < 2 else aevD, 1)
            b = afilled(dve, "n4")
            for i in range(2):
                v.scalar_tensor_tensor(kva[:, i, :], kva[:, i, :], col("g_kv_a_2", i), b, ALU.mult, ALU.mult) \
                    .then_inc(s_qn if i < 1 else aevD, 1)
            for i in range(3):
                dve.wait_ge(s_hh, 16 + i + 1)
                v.tensor_tensor(qnl[:, i, :], qa[:, i, :], qnh[:, i, :].bitcast(F32), ALU.subtract).then_inc(s_hl, 1)
            for i in range(2):
                dve.wait_ge(s_hh, 19 + i + 1)
                v.tensor_tensor(kvl[:, i, :], kva[:, i, :], kvh[:, i, :].bitcast(F32), ALU.subtract).then_inc(s_hl, 1)
            lo(1)
            conv(2)
            lo(1)
            conv(6)
            for i in range(2):
                took(dve, "qb", 3 * i + 2)
                rope(qro[:, i, :], qro[:, i, :], "q2rot", i, tmp=(s2c, tmpa)).then_inc(s_q2, 1)
                if i == 0:
                    lo(1)
                dve.wait_ge(s_q2, i + 1)
            conv(6)
            lo(1)

            def negate2(h):
                return v.tensor_scalar(nb[:, h % 2, :], mx[:, h % 2, :], -SCALE2, None, ALU.mult)

            def out2(pair):
                dve.wait_ge(s_mh, 8 + pair + 1)
                v.tensor_tensor(Bl[:, pair, :], ps[:, obank(pair), :], Bh[:, pair, :].bitcast(F32),
                                ALU.subtract).then_inc(s_ml, 1)

            attention(1, lambda qt: con[:, C_TRI + 384 - P * qt:C_TRI + 512], negate2, p2, out2, lambda h: conv(8))
            conv(4 * CW)
            dve.wait_ge(s_mus, 1)
            v.tensor_scalar(mu, ps[:, 4, 0:NT], 1.0 / 512, None, ALU.mult).then_inc(s_mu, 1)
            b = afilled(dve, "lnm")
            for j in range(4):
                v.tensor_tensor(cacc[:, j, :], cacc[:, j, :], b, ALU.subtract).then_inc(s_ln if j < 3 else aevD, 1)
            norm(30, 512, 5)
            b = afilled(dve, "lnv")
            for j in range(4):
                v.tensor_tensor(cacc[:, j, :], cacc[:, j, :], b, ALU.mult).then_inc(s_ln2 if j < 3 else aevD, 1)
            for j in range(4):
                dve.wait_ge(s_mh, 12 + j + 1)
                v.tensor_tensor(Bl[:, 4 + j, :], cacc[:, j, :], Bh[:, 4 + j, :].bitcast(F32),
                                ALU.subtract).then_inc(s_ml, 1)
            lo(4)
            norm(38, D, 6)
            b = afilled(dve, "n6")

            def low2(k):
                dve.wait_ge(s_hh, 21 + k + 1)
                v.scalar_tensor_tensor(Bl[:, k, :], R[:, k, :], col("g_ffn_pre_2", k), Bh[:, k, :].bitcast(F32),
                                       ALU.mult, ALU.subtract).then_inc(s_hl, 1)

            for k in range(KD):
                ins = v.scalar_tensor_tensor(mix[:, k, :], mix[:, k, :], col("g_mix_post_2", k), b, ALU.mult, ALU.mult)
                if k < KD - 1:
                    link(ins)
                else:
                    ins.then_inc(aevD, 1)
                    atook(dve, "n6")
                v.tensor_tensor(R[:, k, :], R[:, k, :], mix[:, k, :], ALU.add).then_inc(s_h2, 1)
                dve.wait_ge(s_h2, k + 1)
                if k:
                    low2(k - 1)
            low2(KD - 1)
            norm(46, D, 7)
            atook(dve, "n7")
            link(v.memset(zg[:, 0:16], 0.0))
            for j in range(NJ):
                c = cv[j % 2]
                if j:
                    dve.wait_ge(s_z, j)
                if j > 1:
                    dve.wait_ge(s_fl, j - 1)
                v.tensor_tensor(zg[:, 16:16 + T], filled(dve, "ffn", 2 * j), rBf, ALU.mult).then_inc(evD, 1)
                took(dve, "ffn", 2 * j)
                link(v.tensor_scalar(c, zg[:, 16:16 + T], col("ffn_dw_w_2", 2 * NJ + j), col("ffn_dw_b_2", j),
                                     ALU.mult, ALU.add))
                link(v.scalar_tensor_tensor(c, zg[:, 15:15 + T], col("ffn_dw_w_2", NJ + j), c, ALU.mult, ALU.add))
                v.scalar_tensor_tensor(c, zg[:, 14:14 + T], col("ffn_dw_w_2", j), c, ALU.mult,
                                       ALU.add).then_inc(s_z, 1)
                if j:
                    dve.wait_ge(s_fd, j)
                v.tensor_tensor(up, filled(dve, "ffn", 2 * j + 1), rBf, ALU.mult).then_inc(evD, 1)
                dve.wait_ge(s_gl, j + 1)
                took(dve, "ffn", 2 * j + 1)
                v.tensor_tensor(c, c, up, ALU.mult).then_inc(s_fd, 1)
                lo(1)
                dve.wait_ge(s_fh, j + 1)
                v.tensor_tensor(fl[:, j, :], c, fh[:, j, :].bitcast(F32), ALU.subtract).then_inc(s_fl, 1)
            for e in range(KD):
                lo(1)
                if e == 0:
                    for k in range(2):
                        dve.wait_ge(s_pTh, k + 1)
                        v.tensor_tensor(pTl[:, k, :], pTf[:, k, :], pTh[:, k, :].bitcast(F32),
                                        ALU.subtract).then_inc(s_pTl, 1)
                lo(1)
            norm(54, D, 8)
            b = afilled(dve, "n8")

            def low3(k):
                dve.wait_ge(s_hh, 29 + k + 1)
                v.tensor_tensor(h3l[:, k, :], R[:, k, :], h3h[:, k, :].bitcast(F32), ALU.subtract).then_inc(s_hl, 1)

            for k in range(KD):
                ins = v.scalar_tensor_tensor(fo[:, k, :], fo[:, k, :], col("g_ffn_post_2", k), b, ALU.mult, ALU.mult)
                if k < KD - 1:
                    link(ins)
                else:
                    ins.then_inc(aevD, 1)
                    atook(dve, "n8")
                v.tensor_tensor(R[:, k, :], R[:, k, :], fo[:, k, :], ALU.add).then_inc(s_h3, 1)
                dve.wait_ge(s_h3, k + 1)
                if k == 2:
                    lo(1)
                if k:
                    low3(k - 1)
            low3(KD - 1)
            took(dve, "e", 7)
            link(v.tensor_tensor(mu, sse[:, :, 0], sse[:, :, 1], ALU.add))
            variance(mu, D)
            link(rstd(keep[:, 72:76]))
            dve.wait_ge(s_grow, 16)
            for t in range(NT):
                link(v.scalar_tensor_tensor(etok[:, t, :], etok[:, t, :], keep[:, 72 + t:73 + t], grow, ALU.mult,
                                            ALU.mult))
            for i in range(8):
                t, hf = i // 2, i % 2
                v.tensor_copy(htok[:, t, 512 * hf:512 * hf + 512], filled(dve, "h3", i)).then_inc(evD, 1)
            took(dve, "h3", 7)
            for i in range(16):
                c, t = i // 4, i % 4
                if i % 4 == 0 and c < 2:
                    lo(1)
                took(dve, *(("plg", i) if i < 4 else ("plh", i - 4)))
                cl = slice(c * 256, (c + 1) * 256)
                link(v.tensor_tensor(otok[:, t, cl], otok[:, t, cl], etok[:, t, cl], ALU.mult))
                v.tensor_tensor(otok[:, t, cl], otok[:, t, cl], htok[:, t, cl], ALU.add).then_inc(s_ot, 1)
            assert lw[0] == len(wchunk), (lw[0], len(wchunk))
            assert tk[0] == 3 * TOPK // 8


def kernel(**inputs):
    import concourse.bacc as _bacc
    from concourse import mybir as _mybir
    from concourse.bass_utils import run_bass_kernel_spmd as _run

    get = {name: np.ascontiguousarray(v) for name, v in inputs.items()}
    arrays = {}
    arrays["xT"] = np.ascontiguousarray(get["x"][0].T).reshape(KD, P, T)
    arrays["pT"] = np.ascontiguousarray(get["p_2"][0, 0].T).reshape(2, P, T)
    rows = []
    for name, n in VECS:
        v = get[name].reshape(-1)
        if name in ("q_norm_w", "k_norm_w"):
            v = np.concatenate([v, v])
        rows.append(v.reshape(n, P))
    arrays["vecs"] = np.ascontiguousarray(np.concatenate(rows).T)
    pieces = []
    for _, parts in stream():
        tiles = [get[name][0][r0:r1][:, cols].reshape((r1 - r0) // P, P, len(cols)) for name, r0, r1, cols in parts]
        pieces.append(np.concatenate(tiles, axis=2).transpose(1, 0, 2).reshape(-1))
    arrays["stream"] = np.concatenate(pieces)
    arrays["con"] = constants()
    for name in ("w_pool", "positions_2", "g_ple_2"):
        arrays[name] = get[name]
    nc = _bacc.Bacc("TRN2", target_bir_lowering=False, num_devices=1)
    args = {name: nc.dram_tensor(f"in_{name}_dram", v.shape, _mybir.dt.from_np(v.dtype), kind="ExternalInput").ap()
            for name, v in arrays.items()}
    out = nc.dram_tensor("out_0_dram", (1, T, D), _mybir.dt.float32, kind="ExternalOutput").ap()
    build(nc, args, out)
    r = _run(nc, [{f"in_{name}_dram": v for name, v in arrays.items()}], core_ids=[0])
    return r.results[0]["out_0_dram"]
```

```python
from contextlib import ExitStack

import concourse.bass as bass
import numpy as np
from concourse import mybir

ALU = mybir.AluOpType
ACT = mybir.ActivationFunctionType
F32 = mybir.dt.float32
F32R = mybir.dt.float32r
I32 = mybir.dt.int32

P = 128
T = 512
NT = T // P
D = 1024
KD = D // P
EPS = 1e-6
NEG = -1e30
TAKEN = -3e38
HD = 64
TOPK = min(256, T // 4)
FF = 2816
NJ = FF // P
CW = 31
CP = 32
SCALE1 = HD ** -0.5
SCALE2 = 96 ** -0.5

GATE, VALUE = (0, 1, 10, 11), (2, 3, 12, 13)
DVE_CONV = 3
RAWS = 3
HIS = 3
QORD = (3, 2, 0, 1)
SOFF = {3: 0, 2: 512, 0: 896, 1: 1024}
TOFF = {0: 0, 1: 512, 3: 896, 2: 1024}
QB = (("n", 0), ("n", 1), ("r", 0), ("n", 2), ("n", 3), ("r", 1))
INV2PI = float(np.float32(1 / (2 * np.pi)))
ROUND = 1.5 * 2 ** 23
_c1 = 6.28125
TWOPI = (_c1, float(np.uint32(np.float32(2 * np.pi - _c1).view(np.uint32) & 0xFFFFF000).view(np.float32)))
TWOPI = TWOPI + (float(np.float32(2 * np.pi - TWOPI[0] - TWOPI[1])),)
PI32 = float(np.nextafter(np.float32(np.pi), np.float32(0)))

U0, GP0, Q0, K0, V0, GA0, QI0, KI0, WI0, E1 = 0, 512, 1024, 1536, 1664, 1792, 2304, 2816, 2880, 2888

C_ID, C_R64, C_R32, C_TRI, C_HS, C_ONE, C_FREQ, C_RC, C_COS, C_SIN, C_END = (
    0, 128, 256, 384, 896, 898, 900, 901, 917, 1429, 1941)

VECS = [("c", 8), ("norm_w", 8), ("b_ada", 24), ("pool_scale", 4), ("g_mix_pre_2", 8), ("g_mix_post_2", 8),
        ("g_ffn_pre_2", 8), ("g_ffn_post_2", 8), ("ffn_dw_b_2", 22), ("conv_b_2", 4), ("conv_ln_g_2", 4),
        ("conv_ln_b_2", 4), ("g_q_a_2", 3), ("g_kv_a_2", 2), ("q_norm_w", 1), ("k_norm_w", 1),
        ("ffn_dw_w_2", 66), ("conv_w_2", 124)]
NV = sum(n for _, n in VECS)


def stream():
    def cols(c0, c1):
        return np.arange(c0, c1)

    out = [("ada", [("w_ada", k * P, (k + 2) * P, np.concatenate([cols(c, c + 512), cols(D + c, D + c + 512)]))])
           for c in (0, 512) for k in range(0, KD, 2)]

    def w(name, rows, columns):
        out.append(("w", [(name, rows[0], rows[1], columns)]))

    w("w_in", (0, D), cols(KI0, E1))
    for c in (QI0, QI0 + 256, K0):
        w("w_in", (0, D), cols(c, c + 256))
    out.extend(("ada", [("w_ada", k * P, (k + 2) * P, cols(2 * D, 3 * D))]) for k in range(0, KD, 2))
    for c in (Q0, Q0 + 256, GA0, GA0 + 256, U0, U0 + 256, GP0, GP0 + 256):
        w("w_in", (0, D), cols(c, c + 256))
    for c in range(0, D, 256):
        w("w_out", (0, D), cols(c, c + 256))
    for c in (1184, 672, 0, 256):
        w("w_in_2", (0, D), cols(c, c + 256))
    w("w_in_2", (0, D), cols(512, 672))
    for c in (1440, 928):
        w("w_in_2", (0, D), cols(c, c + 256))
    for c in range(2):
        heads = np.arange(4 * c, 4 * c + 4)[:, None] * 96
        w("w_q_b_2", (0, 384), np.concatenate([(heads + np.arange(HD)).ravel(), (heads + np.arange(HD, 96)).ravel()]))
    heads = np.arange(8)[:, None] * P
    w("w_kv_b_2", (0, 256), np.concatenate([(heads + np.arange(HD)).ravel(), (heads + np.arange(HD, P)).ravel()]))
    for c in range(0, D, 256):
        w("w_o_2", (0, D), cols(c, c + 256))
    for j in range(NJ):
        out.append(("w", [(n, 0, D, cols(j * P, (j + 1) * P)) for n in ("w_ffn_gate_2", "w_ffn_up_2")]))
    for e in range(KD):
        for h in range(2):
            w("w_ffn_down_2", (h * 11 * P, (h + 1) * 11 * P), cols(e * P, (e + 1) * P))
    w("w_ple_proj_2", (0, 256), cols(0, D))
    for c in range(0, D, 256):
        w("w_ple_gate_2", (0, D), cols(c, c + 256))
    return out


def constants():
    c = np.zeros((P, C_END), np.float32)
    c[:, C_ID:C_ID + P] = np.eye(P)
    for base, w in ((C_R64, 64), (C_R32, 32)):
        for m in range(P):
            if m % w < w // 2:
                c[m + w // 2, base + m] = -1.0
            else:
                c[m - w // 2, base + m] = 1.0
    q, k = np.arange(P)[:, None], np.arange(P)[None, :]
    c[:, C_TRI + 384:C_TRI + 512] = np.where(k <= q, 0.0, NEG)
    c[0:64, C_HS] = 1.0
    c[64:128, C_HS + 1] = 1.0
    c[:, C_ONE:C_ONE + 2] = 1.0
    half = 16
    inv = (10000.0 ** (-np.arange(0, 32, 2, dtype=np.float32) / np.float32(32))).astype(np.float32)
    c[:, C_FREQ] = inv[np.arange(P) % half]
    c[:, C_RC:C_RC + 16] = 1.0 / np.arange(1, 17)
    freqs = (10000.0 ** (-np.arange(32, dtype=np.float32) / np.float32(32))).astype(np.float32)
    ang = (np.arange(T, dtype=np.float32)[None, :] * freqs[np.arange(P) % 32][:, None]).astype(np.float32)
    c[:, C_COS:C_COS + T] = np.cos(ang.astype(np.float64))
    c[:, C_SIN:C_SIN + T] = np.sin(ang.astype(np.float64))
    return c


def build(nc, a, out):
    ctx = ExitStack()
    with ctx:
        def sb(name, shape, dt=F32):
            return ctx.enter_context(nc.sbuf_tensor(name, shape, dt))

        def sem(name):
            return ctx.enter_context(nc.semaphore(name))

        spot = [(nc.sbuf_base + 63) // 64 * 64]

        def place(name, shape, dt=F32, at=None):
            size = int(np.prod(shape[1:])) * 4
            off = spot[0] if at is None else at
            if at is None:
                spot[0] += (size + 31) // 32 * 32
            return nc.alloc_sbuf_tensor_at(name, shape, dt, offset=off), off

        raw, raw_at = place("raw", [P, RAWS, 2048])
        wlo, _ = place("wlo", [P, RAWS, 2048], F32R, raw_at)
        whi, _ = place("whi", [P, HIS, 2048], F32R)
        R, _ = place("R", [P, KD, T])
        Bh, bh_at = place("Bh", [P, 8, T], F32R)
        Bl, bl_at = place("Bl", [P, 8, T], F32R)
        Bhf, _ = place("Bhf", [P, 8 * T], F32, bh_at)
        Blf, _ = place("Blf", [P, 8 * T], F32, bl_at)
        A, a_at = place("A", [P, 44 * T])
        Ar, _ = place("Ar", [P, 44 * T], F32R, a_at)
        M, _ = place("M", [P, 4 * T + 16])
        con, _ = place("con", [P, C_END])
        wpt, _ = place("wpt", [P, 4, P])
        vec, _ = place("vec", [P, NV])
        small, _ = place("small", [P, 400])
        nrm, _ = place("nrm", [P, 4, 40])
        assert spot[0] <= nc.sbuf_usable_end
        ps = ctx.enter_context(nc.psum_tensor("ps", [P, 8, 512], F32))

        def av(tile, n=1, w=T, of=A):
            lo = int(tile * T)
            return of[:, lo:lo + n * w].rearrange("p (n w) -> p n w", n=n)

        def ar(tile, n):
            return av(tile, n, of=Ar)

        ident = con[:, C_ID:C_ID + P]
        ones = con[:, C_ONE:C_ONE + 1]
        cosT, sinT = con[:, C_COS:C_COS + T], con[:, C_SIN:C_SIN + T]
        tri = con[:, C_TRI + 384:C_TRI + 512]
        rot64, rot32 = con[:, C_R64:C_R64 + P], con[:, C_R32:C_R32 + P]

        vat, at = {}, 0
        for name, n in VECS:
            vat[name] = at
            at += n

        def col(name, i=0, n=1):
            return vec[:, vat[name] + i:vat[name] + i + n]

        csil = small[:, 0:8]
        mcol = small[:, 8:16]
        gtcol = small[:, 24:32]
        mtmp = small[:, 32:48]
        wiT = small[:, 48:80].rearrange("p (t h) -> p t h", t=NT)
        m8 = small[:, 80:88]
        mx = small[:, 88:96].rearrange("p (b t) -> p b t", b=2)
        nb = small[:, 96:104].rearrange("p (b t) -> p b t", b=2)
        sm = small[:, 104:112].rearrange("p (b t) -> p b t", b=2)
        rsm = small[:, 112:120].rearrange("p (b t) -> p b t", b=2)
        rqs = small[:, 120:152].rearrange("p (t h) -> p t h", t=NT)
        mu = small[:, 152:156]
        sse = small[:, 168:176].rearrange("p (t h) -> p t h", t=NT)
        rqk = small[:, 176:216].rearrange("p (t h) -> p t h", t=NT)
        keep = small[:, 216:296]

        qiT, kid, kiw, sc = av(0, 4), av(4)[:, 0], av(5)[:, 0], av(6, 4)
        qT, kdup, vtok, gat = av(10, 4), av(14, 2), av(16)[:, 0], av(17, 4)
        uT, gp = av(21, 4), av(25, 4)
        kraw = uT[:, 3]
        aoh, aol = ar(21, 4), ar(25, 4)
        xr = av(29, 8)
        pmh, pml = ar(29, 4), ar(33, 4)
        pp = [A[:, 37 * T:37 * T + T + CP], A[:, 38 * T + CP:39 * T + 2 * CP]]
        acc = A[:, 40 * T:44 * T]
        gacc = M[:, 0:2 * T]
        t1, t2, rl = av(40)[:, 0], av(41)[:, 0], av(42, 2)
        kbx = av(43, 1)[:, 0].rearrange("p (t w) -> p t w", t=NT)
        vT, sqk = M[:, 2 * T:3 * T], M[:, 3 * T:4 * T]
        sqx = [vT, sqk]
        p1 = [A[:, 0:1280], A[:, 1280:2560], Blf[:, 4 * T:4 * T + 1280]]
        pT1 = [A[:, 37 * T + 1280 * i:37 * T + 1280 * (i + 1)] for i in range(2)]
        ao = av(42)[:, 0]
        sqy = [av(40)[:, 0], av(41)[:, 0]]
        cpad = A[:, 0:4 * (T + CP)].rearrange("p (n w) -> p n w", n=4)
        cacc = av(4.25, 4)
        gt2, qa, kva = av(8.25, 2), av(10.25, 3), av(13.25, 2)
        qnh, qnl, kvh, kvl = ar(15.25, 3), ar(18.25, 3), ar(21.25, 2), ar(23.25, 2)
        qno, qro, kno, kro = av(25.25, 4), av(29.25, 2), av(31.25, 4), av(35.25)[:, 0]
        v2 = av(36.25, 4)
        s2a, s2b, s2c = av(40.25)[:, 0], av(41.25)[:, 0], av(42.25)[:, 0]
        sq2 = [s2a, s2b]
        p2 = [A[:, at:at + 1280] for at in (int(8.25 * T), int(10.75 * T), int(18.25 * T))]
        pT2 = [A[:, int(13.25 * T) + 1280 * i:int(13.25 * T) + 1280 * (i + 1)] for i in range(2)]
        mix = av(25.25, 8)
        rB, tmpa = M[:, 0:T], M[:, T:2 * T]
        posi, posf = M[:, 2 * T:3 * T].bitcast(I32), M[:, 3 * T:4 * T]
        turns = M[:, 2 * T:3 * T]
        fh, fl = ar(0, NJ), ar(NJ, NJ)
        zg = M[:, 0:T + 16]
        cv = [M[:, T + 16:2 * T + 16], M[:, 2 * T + 16:3 * T + 16]]
        up = M[:, 3 * T + 16:4 * T + 16]
        rBf = sinT
        fo = Bhf[:, :].rearrange("p (n w) -> p n w", n=8)
        etok, htok, otok = av(0, 4, D), av(8, 4, D), av(32, 4, D)
        h3h, h3l = ar(16, 8), ar(24, 8)
        pTf = Blf[:, 0:2 * T].rearrange("p (k n) -> p k n", k=2)
        pTh, pTl = Bl[:, 2:4, :], Bl[:, 4:6, :]
        grow = Blf[:, 6 * T:8 * T]

        chunks, at = [], 0
        for kind, parts in stream():
            k, n = (parts[0][2] - parts[0][1]) // P, sum(len(x[3]) for x in parts)
            chunks.append((kind, a["stream"][at:at + P * k * n].rearrange("(p n) -> p n", p=P), k, n))
            at += P * k * n
        wchunk = [i for i, c in enumerate(chunks) if c[0] == "w"]
        wnum = {ci: w for w, ci in enumerate(wchunk)}
        W_FFN = len(wchunk) - NJ - 2 * KD - 5
        W_DOWN = W_FFN + NJ
        landed = [16 * (ci // RAWS + 1) for ci in range(len(chunks))]

        plan = ([("kiw", "A")] + [("qi", "A")] * 4 + [("k", "A"), ("vT", "A")] + [("q", "A")] * 4
                + [("ga", "A")] * 4 + [("u", "A")] * 4 + [("gp", "A")] * 4 + [("y", "D")] * 8
                + [("in2", "D")] * 14 + [("qb", "A")] * 6 + [("kn", "A")] * 4 + [("v2", "A")] * 4 + [("mix", "A")] * 8
                + [("ffn", "D")] * (2 * NJ) + [("down", "A")] * 8 + [("e", "A")] * 8 + [("plg", "A")] * 4
                + [("h3a", "D")] * 4 + [("plh", "A")] * 4 + [("h3b", "D")] * 4 + [("pli", "A")] * 8)
        aplan = ([("n0", "A"), ("mod", "D"), ("mod", "D"), ("kirot", "D"), ("wiT", "D")] + [("qirot", "D")] * 4
                 + [("idx", "A")] * 24 + [("gmod", "D"), ("krot", "D")] + [("qrot", "D")] * 4
                 + [("kb", "D"), ("vtok", "A")] + [("pool", "D")] * 4
                 + [("n2", "A"), ("krrot", "D"), ("n3", "D"), ("n4", "D")] + [("q2rot", "D")] * 2
                 + [("lnm", "D"), ("lnv", "D"), ("n6", "A"), ("n7", "A"), ("n8", "A")])

        def takers(order):
            first, done, count = {}, [], {"A": 0, "D": 0}
            for i, (name, e) in enumerate(order):
                first.setdefault(name, i)
                count[e] += 1
                done.append((e, count[e]))
            return first, done

        first, done_at = takers(plan)
        afirst, adone_at = takers(aplan)
        per_chunk = ([1] + [2] * 11 + [2] * 4 + [2] * 7 + [3, 3, 8] + [2] * 4 + [2] * NJ + [0, 1] * KD + [8, 4, 8, 8, 4])
        chunk_end = [int(x) for x in np.cumsum(per_chunk)]

        s_raw = [sem(f"s_raw{i}") for i in range(RAWS)]
        s_hi = sem("s_hi")
        s_lo = sem("s_lo")
        s_half = sem("s_half")
        s_blk = sem("s_blk")
        s_ev = {"A": sem("s_evA"), "D": sem("s_evD")}
        s_aux = sem("s_aux")
        s_aev = {"A": sem("s_aevA"), "D": sem("s_aevD")}
        s_con, s_trig, s_vec, s_wp = sem("s_con"), sem("s_trig"), sem("s_vec"), sem("s_wp")
        s_x = [sem(f"s_x{i}") for i in range(4)]
        s_pos, s_p, s_grow, s_out = sem("s_pos"), sem("s_p"), sem("s_grow"), sem("s_out")
        dch, ach, pch = sem("dve_chain"), sem("act_chain"), sem("pool_chain")
        s_csil = sem("s_csil")
        s_v, s_rt, s_rs = sem("s_v"), sem("s_rt"), sem("s_rs")
        s_sq, s_cs = sem("s_sq"), sem("s_cs")
        s_mod = sem("s_mod")
        s_xr = sem("s_xr")
        s_hh, s_hl = sem("s_hh"), sem("s_hl")
        s_ki, s_kid, s_qi = sem("s_ki"), sem("s_kid"), sem("s_qi")
        s_idx = sem("s_idx")
        s_kd, s_qr = sem("s_kd"), sem("s_qr")
        s_qh, s_ql = sem("s_qh"), sem("s_ql")
        s_pool, s_pld = sem("s_pool"), sem("s_pld")
        s_qk, s_msk, s_nb, s_exp = sem("s_qk"), sem("s_msk"), sem("s_nb"), sem("s_exp")
        s_pn, s_pt, s_pc, s_pv = sem("s_pn"), sem("s_pt"), sem("s_pc"), sem("s_pv")
        s_ao = sem("s_ao")
        s_mh, s_ml = sem("s_mh"), sem("s_ml")
        s_ang, s_tab, s_sg = sem("s_ang"), sem("s_tab"), sem("s_sg")
        s_cp, s_cvp = sem("s_cp"), sem("s_cvp")
        s_scaled = sem("s_scaled")
        s_cpz, s_qn, s_kr, s_kr4, s_q2 = sem("s_cpz"), sem("s_qn"), sem("s_kr"), sem("s_kr4"), sem("s_q2")
        s_cv, s_mus, s_mu, s_ln, s_ln2 = sem("s_cv"), sem("s_mus"), sem("s_mu"), sem("s_ln"), sem("s_ln2")
        s_h2, s_z, s_gl, s_fd, s_fh, s_fl = sem("s_h2"), sem("s_z"), sem("s_gl"), sem("s_fd"), sem("s_fh"), sem("s_fl")
        s_pTh, s_pTl, s_h3, s_ot = sem("s_pTh"), sem("s_pTl"), sem("s_h3"), sem("s_ot")

        def bank(name, i):
            return (first[name] + i) % 4

        def took(eng, name, i):
            e, v = done_at[first[name] + i]
            eng.wait_ge(s_ev[e], v)

        def abank(name, i=0):
            return 5 + (afirst[name] + i) % 3

        def atook(eng, name, i=0):
            e, v = adone_at[afirst[name] + i]
            eng.wait_ge(s_aev[e], v)

        def filled(eng, name, i):
            eng.wait_ge(s_blk, first[name] + i + 1)
            return ps[:, bank(name, i), :]

        def afilled(eng, name, i=0):
            eng.wait_ge(s_aux, afirst[name] + i + 1)
            return ps[:, abank(name, i), :]

        def used(eng, w):
            if W_DOWN <= w < W_DOWN + 2 * KD and (w - W_DOWN) % 2 == 0:
                eng.wait_ge(s_half, (w - W_DOWN) // 2 + 1)
            else:
                eng.wait_ge(s_blk, chunk_end[w])

        def gate_block(i):
            return ("plg", i) if i < 4 else ("plh", i - 4) if i < 8 else ("pli", i - 8)

        def obank(pair):
            return 3 if pair % 2 == 0 else 7

        block = ctx.enter_context(nc.Block())

        @block.sync
        def _(sp):
            sp.dma_start(vec[:, :], a["vecs"]).then_inc(s_vec, 16)
            for i in range(4):
                sp.dma_start(R[:, 2 * i:2 * i + 2, :], a["xT"][2 * i:2 * i + 2].rearrange("k p t -> p k t")) \
                    .then_inc(s_x[i], 16)
                if i == 0:
                    sp.dma_start(con[:, 0:C_COS], a["con"][:, 0:C_COS]).then_inc(s_con, 16)
            for ci, (kind, src, k, n) in enumerate(chunks):
                if ci == 10:
                    sp.dma_start(con[:, C_COS:C_END], a["con"][:, C_COS:C_END]).then_inc(s_trig, 16)
                if ci >= RAWS:
                    if chunks[ci - RAWS][0] == "w":
                        used(sp, wnum[ci - RAWS])
                    else:
                        sp.wait_ge(s_lo, ci - RAWS + 1)
                sp.dma_start(raw[:, ci % RAWS, 0:k * n], src).then_inc(s_raw[ci % RAWS], 16)
                if ci == 20:
                    sp.dma_start(wpt[:, :, :], a["w_pool"][0].rearrange("g c d -> c g d")).then_inc(s_wp, 16)
            for i in range(16):
                sp.wait_ge(s_ot, i + 1)
                c, t = i // 4, i % 4
                sp.dma_start(out[0, t * P:(t + 1) * P, c * 256:(c + 1) * 256],
                             otok[:, t, c * 256:(c + 1) * 256]).then_inc(s_out, 16)
            sp.wait_ge(s_out, 16 * 16)

        @block.gpsimd
        def _(g):
            pc = [0]

            def link(ins):
                pc[0] += 1
                ins.then_inc(pch, 1)
                g.wait_ge(pch, pc[0])

            g.wait_ge(s_aev["A"], 1)
            for k in range(KD):
                g.wait_ge(s_x[k // 2], 16)
                g.tensor_tensor(xr[:, k, :], R[:, k, :], rB, ALU.mult).then_inc(s_xr, 1)
            for i in range(2):
                ins = g.memset(pp[i][:, 0:CP], 0.0)
                link(ins)
            for grp in range(4):
                took(g, "u", grp)
                if grp:
                    g.wait_ge(s_pld, grp)
                link(g.tensor_copy(pp[0][:, CP:CP + 1], uT[:, grp, 0:1]))
                for step in range(grp + 1):
                    d = 1 << step
                    src, dst = pp[(step + 1) % 2], pp[step % 2]
                    if step == 0:
                        ins = g.tensor_tensor(dst[:, CP + 1:CP + T], uT[:, grp, 1:T], uT[:, grp, 0:T - 1], ALU.add)
                    else:
                        ins = g.tensor_tensor(dst[:, CP:CP + T], src[:, CP:CP + T], src[:, CP - d:CP - d + T], ALU.add)
                    if step < grp:
                        link(ins)
                ins.then_inc(s_pool, 1)
            took(g, "vT", 0)
            g.wait_ge(s_cs, 9)
            atook(g, "vtok")
            g.dma_start(posi, a["positions_2"].partition_broadcast(P)).then_inc(s_pos, 16)
            g.wait_ge(s_pos, 16)
            link(g.tensor_copy(posf, posi))
            link(g.tensor_scalar(posf, posf, con[:, C_FREQ:C_FREQ + 1], None, ALU.mult))
            g.wait_ge(s_qr, 4)
            atook(g, "gmod")
            for dst, quarter in ((sinT, 0.0), (cosT, 0.25)):
                link(g.tensor_scalar(turns, posf, INV2PI, quarter, ALU.mult, ALU.add))
                link(g.tensor_scalar(turns, turns, ROUND, None, ALU.add))
                link(g.tensor_scalar(turns, turns, -ROUND, None, ALU.add))
                src = posf
                for part in TWOPI:
                    link(g.tensor_scalar(tmpa, turns, -part, None, ALU.mult))
                    link(g.tensor_tensor(dst, src, tmpa, ALU.add))
                    src = dst
                link(g.tensor_scalar(dst, dst, quarter * 2 * np.pi, PI32, ALU.add, ALU.min))
                ins = g.tensor_scalar(dst, dst, -PI32, None, ALU.max)
                ins.then_inc(s_ang, 1)
            took(g, "y", 0)
            for j in range(4):
                ins = g.memset(cpad[:, j, 0:CP], 0.0)
                if j < 3:
                    link(ins)
            ins.then_inc(s_cpz, 1)
            for n, j in enumerate(range(DVE_CONV, 4)):
                g.wait_ge(s_cp, n + 1)
                for t in range(CW):
                    src = cpad[:, j, CP - (CW - 1) + t:CP - (CW - 1) + t + T]
                    wcol = col("conv_w_2", t * 4 + j)
                    if t == 0:
                        link(g.tensor_scalar(cacc[:, j, :], src, wcol, col("conv_b_2", j), ALU.mult, ALU.add))
                    else:
                        link(g.tensor_scalar(turns, src, wcol, None, ALU.mult))
                        ins = g.tensor_tensor(cacc[:, j, :], cacc[:, j, :], turns, ALU.add)
                        if t < CW - 1:
                            link(ins)
                        else:
                            ins.then_inc(s_cvp, 1)
            atook(g, "n6")
            for k in range(KD):
                g.tensor_tensor(mix[:, k, :], mix[:, k, :], rB, ALU.mult).then_inc(s_scaled, 1)
            g.wait_ge(s_blk, first["down"])
            g.dma_start(pTf, a["pT"].rearrange("k p t -> p k t")).then_inc(s_p, 16)
            g.dma_start(grow, a["g_ple_2"][0].partition_broadcast(P)).then_inc(s_grow, 16)
            atook(g, "n8")
            for k in range(KD):
                g.tensor_tensor(fo[:, k, :], fo[:, k, :], rBf, ALU.mult).then_inc(s_scaled, 1)

        @block.scalar
        def _(act):
            f = nc.scalar.activation
            ac, hw, sqn, rt = [0], [0], [0], [0]

            def link(ins):
                ac[0] += 1
                ins.then_inc(ach, 1)
                act.wait_ge(ach, ac[0])

            def hi(n=1):
                for _ in range(n):
                    w = hw[0]
                    ci = wchunk[w]
                    act.wait_ge(s_raw[ci % RAWS], landed[ci])
                    if w >= HIS:
                        used(act, w - HIS)
                    k, nn = chunks[ci][2:]
                    f(whi[:, w % HIS, 0:k * nn], raw[:, ci % RAWS, 0:k * nn], ACT.Copy).then_inc(s_hi, 1)
                    hw[0] += 1

            def square(tile, src, signal=None, depth=1):
                if sqn[0] >= depth:
                    act.wait_ge(s_cs, sqn[0] - depth + 1)
                sqn[0] += 1
                return f(tile, src, ACT.Square).then_inc(signal or s_sq, 1)

            def root(n=NT):
                rt[0] += 1
                act.wait_ge(s_v, rt[0])
                f(nrm[:, 1, 0:n], nrm[:, 0, 0:n], ACT.Sqrt).then_inc(s_rt, 1)

            evA = s_ev["A"]

            act.wait_ge(s_vec, 16)
            f(csil, col("c", 0, 8), ACT.Silu).then_inc(s_csil, 1)
            for k in range(KD):
                act.wait_ge(s_x[k // 2], 16)
                square(sqx[k % 2], R[:, k, :], depth=2)
            root()
            f(rB, afilled(act, "n0"), ACT.Copy).then_inc(s_aev["A"], 1)
            for k in range(KD):
                if k % 4 == 0:
                    act.wait_ge(s_mod, k // 4 + 1)
                act.wait_ge(s_xr, k + 1)
                link(f(xr[:, k, :], xr[:, k, :], ACT.Identity, scale=mcol[:, k:k + 1], bias=mtmp[:, k:k + 1]))
                f(Bh[:, k, :], xr[:, k, :], ACT.Copy).then_inc(s_hh, 1)
                if k == 3:
                    hi(2)
            hi(1)
            f(kiw[0:72, :], filled(act, "kiw", 0)[0:72, :], ACT.Copy).then_inc(evA, 1)
            for i in range(2):
                f(qiT[:, i, :], filled(act, "qi", i), ACT.Copy).then_inc(evA, 1)
            hi(1)
            act.wait_ge(s_ki, 1)
            f(kid[HD:P, :], kid[0:HD, :], ACT.Copy).then_inc(s_kid, 1)
            for i in range(2, 4):
                f(qiT[:, i, :], filled(act, "qi", i), ACT.Copy).then_inc(evA, 1)
            src = filled(act, "k", 0)
            link(f(kraw, src, ACT.Copy, scale=col("k_norm_w")))
            square(sqk, src, evA, depth=1)
            f(vT, filled(act, "vT", 0), ACT.Copy).then_inc(evA, 1)
            for n in range(24):
                w = (n // 8 + 2) * P
                src = afilled(act, "idx", n)
                if n >= 2:
                    act.wait_ge(s_idx, n - 1)
                f(rl[:, n % 2, 0:w], src[:, 0:w], ACT.Relu, scale=HD ** -0.5).then_inc(s_aev["A"], 1)
                if n in (15, 19):
                    hi(1)
            hi(1)
            for i in range(4):
                src = filled(act, "q", i)
                link(f(qT[:, i, :], src, ACT.Copy, scale=col("q_norm_w")))
                square(gat[:, i, :], src, evA, 99)
                if i % 2:
                    hi(1)
            for i in range(2):
                if i == 0:
                    act.wait_ge(s_cs, 11)
                f(gat[:, i, :], filled(act, "ga", i), ACT.Silu).then_inc(evA, 1)
            hi(1)
            root(40)
            for i in range(2, 4):
                f(gat[:, i, :], filled(act, "ga", i), ACT.Silu).then_inc(evA, 1)
            hi(1)
            atook(act, "kb")
            for i in range(2):
                for h in range(2):
                    f(kdup[h * HD:(h + 1) * HD, i, :], kraw[i * HD:(i + 1) * HD, :], ACT.Copy).then_inc(s_kd, 1)
            f(vtok, afilled(act, "vtok"), ACT.Copy).then_inc(s_aev["A"], 1)
            act.wait_ge(s_kd, 4)
            for i in range(4):
                f(uT[:, i, :], filled(act, "u", i), ACT.Copy).then_inc(evA, 1)
                if i % 2:
                    hi(1)
            for i in range(4):
                f(gp[:, i, :], filled(act, "gp", i), ACT.Silu).then_inc(evA, 1)
                if i % 2:
                    hi(1)
            act.wait_ge(s_kd, 4)
            for i in range(2):
                f(Bl[:, i, :], kdup[:, i, :], ACT.Copy).then_inc(s_qh, 1)
            act.wait_ge(s_qr, 4)
            for h in range(8):
                b0 = HD * (h % 2)
                f(Bh[b0:b0 + HD, h, :], qT[b0:b0 + HD, h // 2, :], ACT.Copy).then_inc(s_qh, 1)
            for i in range(4):
                atook(act, "pool", i)
                f(pmh[:, i, :], uT[:, i, :], ACT.Copy).then_inc(s_mh, 1)

            def attention(base, scale_of, p, pT, out_pair, between):
                def evac(h):
                    for b, wd in enumerate((512, 512, 256)):
                        act.wait_ge(s_pt, base * 24 + 3 * h + b + 1)
                        if b == 0 and h >= 2:
                            act.wait_ge(s_pv, base * 8 + h - 1)
                        f(pT[h % 2][:, 512 * b:512 * b + wd], ps[:, b, 0:wd], ACT.Copy).then_inc(s_pc, 1)

                for h in range(8):
                    act.wait_ge(s_nb, base * 8 + h + 1)
                    for qt in QORD:
                        o, w = SOFF[qt], (qt + 1) * P
                        f(p[h % 3][:, o:o + w], p[h % 3][:, o:o + w], ACT.Exp, bias=nb[:, h % 2, qt:qt + 1],
                          scale=scale_of(h, qt), accum_out=sm[:, h % 2, qt:qt + 1]).then_inc(s_exp, 1)
                    if h:
                        evac(h - 1)
                    if h >= 3 and h % 2:
                        out_pair(h // 2 - 1)
                    between(h)
                evac(7)
                out_pair(3)

            def out1(pair):
                act.wait_ge(s_ao, pair + 1)
                f(aoh[:, pair, :], ao, ACT.Copy).then_inc(s_mh, 1)

            attention(0, lambda h, qt: rqs[:, qt, h:h + 1], p1, pT1, out1, lambda h: None)
            act.wait_ge(s_ang, 2)
            f(sinT, sinT, ACT.Sin).then_inc(s_tab, 1)
            f(cosT, cosT, ACT.Sin).then_inc(s_tab, 1)
            for k in range(KD):
                took(act, "y", k)
                f(Bh[:, k, :], R[:, k, :], ACT.Copy, scale=col("g_mix_pre_2", k)).then_inc(s_hh, 1)
                square(sqy[k % 2], R[:, k, :], depth=2)
                if k % 2:
                    hi(1)
            root()
            f(rB, afilled(act, "n2"), ACT.Copy).then_inc(s_aev["A"], 1)
            def gates(j0):
                for j in (j0, j0 + 1):
                    took(act, "in2", GATE[j])
                    f(gt2[:, j % 2, :], gt2[:, j % 2, :], ACT.Sigmoid).then_inc(s_sg, 1)

            gates(0)
            hi(2)
            for i in range(2):
                took(act, "in2", 4 + i)
                square(sq2[i % 2], qa[:, i, :], depth=2)
            hi(1)
            took(act, "in2", 6)
            square(sq2[0], qa[:, 2, :], depth=2)
            took(act, "in2", 7)
            square(sq2[1], kva[:, 0, :], depth=2)
            hi(1)
            took(act, "in2", 8)
            square(sq2[0], kva[:, 1, :], depth=2)
            root()
            root()
            gates(2)
            hi(1)
            for i in range(3):
                act.wait_ge(s_qn, i + 1) if i < 2 else atook(act, "n3")
                f(qnh[:, i, :], qa[:, i, :], ACT.Copy).then_inc(s_hh, 1)
            for i in range(2):
                act.wait_ge(s_qn, 3) if i < 1 else atook(act, "n4")
                f(kvh[:, i, :], kva[:, i, :], ACT.Copy).then_inc(s_hh, 1)
            hi(2)
            act.wait_ge(s_kr, 1)
            for g4 in range(3):
                f(kro[g4 * 32:g4 * 32 + 32, :], kro[96:128, :], ACT.Copy).then_inc(s_kr4, 1)
            for i, (what, n) in enumerate(QB):
                f((qno if what == "n" else qro)[:, n, :], filled(act, "qb", i), ACT.Copy).then_inc(evA, 1)
                if i % 3 == 2:
                    hi(1)
            for i in range(4):
                f(kno[:, i, :], filled(act, "kn", i), ACT.Copy).then_inc(evA, 1)
            for i in range(4):
                f(v2[:, i, :], filled(act, "v2", i), ACT.Copy).then_inc(evA, 1)

            def out2(pair):
                act.wait_ge(s_pv, 8 + 2 * pair + 2)
                f(Bh[:, pair, :], ps[:, obank(pair), :], ACT.Copy).then_inc(s_mh, 1)

            attention(1, lambda h, qt: SCALE2, p2, pT2, out2, lambda h: hi(h == 2))
            for j in range(4):
                act.wait_ge(s_ln, j + 1) if j < 3 else atook(act, "lnm")
                square(sq2[j % 2], cacc[:, j, :], depth=2)
            root()
            for j in range(4):
                act.wait_ge(s_ln2, j + 1) if j < 3 else atook(act, "lnv")
                link(f(cacc[:, j, :], cacc[:, j, :], ACT.Silu, scale=col("conv_ln_g_2", j),
                       bias=col("conv_ln_b_2", j)))
                f(Bh[:, 4 + j, :], cacc[:, j, :], ACT.Copy).then_inc(s_mh, 1)
            for k in range(KD):
                link(f(mix[:, k, :], filled(act, "mix", k), ACT.Copy, scale=col("g_mix_post_2", k)))
                square(sq2[k % 2], ps[:, bank("mix", k), :], evA, 2)
                if k in (1, 3, 5):
                    hi(1)
            root()
            f(rB, afilled(act, "n6"), ACT.Copy).then_inc(s_aev["A"], 1)
            for k in range(KD):
                act.wait_ge(s_h2, k + 1)
                f(Bh[:, k, :], R[:, k, :], ACT.Copy, scale=col("g_ffn_pre_2", k)).then_inc(s_hh, 1)
                square(mix[:, k, :], R[:, k, :], depth=99)
            hi(1)
            root()
            f(rBf, afilled(act, "n7"), ACT.Copy).then_inc(s_aev["A"], 1)
            for j in range(NJ):
                act.wait_ge(s_z, j + 1)
                f(cv[j % 2], cv[j % 2], ACT.Gelu_apprx_tanh).then_inc(s_gl, 1)
                hi(1)
                act.wait_ge(s_fd, j + 1)
                f(fh[:, j, :], cv[j % 2], ACT.Copy).then_inc(s_fh, 1)
            for e in range(KD):
                hi(1)
                link(f(fo[:, e, :], filled(act, "down", e), ACT.Copy, scale=col("g_ffn_post_2", e)))
                square(cv[e % 2], ps[:, bank("down", e), :], evA, 2)
                if e == 0:
                    act.wait_ge(s_p, 16)
                    for k in range(2):
                        f(pTh[:, k, :], pTf[:, k, :], ACT.Copy).then_inc(s_pTh, 1)
                if e < KD - 1:
                    hi(1)
            root()

            def high3(k):
                act.wait_ge(s_h3, k + 1)
                f(h3h[:, k, :], R[:, k, :], ACT.Copy).then_inc(s_hh, 1)

            for i in range(8):
                t, hf = i // 2, i % 2
                f(etok[:, t, 512 * hf:512 * hf + 512], filled(act, "e", i), ACT.Copy).then_inc(evA, 1)
                if i == 1:
                    f(rBf, afilled(act, "n8"), ACT.Copy).then_inc(s_aev["A"], 1)
                if i >= 5:
                    high3(i - 5)
            for k in range(3, KD):
                high3(k)
            hi(1)
            for i in range(16):
                c, t = i // 4, i % 4
                if i == 4:
                    hi(1)
                    root()
                src = filled(act, *gate_block(i))
                f(otok[:, t, c * 256:(c + 1) * 256], src[:, 0:256], ACT.Sigmoid).then_inc(evA, 1)
                if i == 4:
                    hi(1)
            assert hw[0] == len(wchunk), (hw[0], len(wchunk))

        @block.tensor
        def _(pe):
            mm = nc.tensor.matmul
            an, bn = [0], [0]

            def begin(name, i):
                b = first[name] + i
                assert b == bn[0], (name, i, b, bn[0])
                bn[0] += 1
                if b >= 4:
                    e, v = done_at[b - 4]
                    pe.wait_ge(s_ev[e], v)
                return ps[:, b % 4, :]

            def abegin(name, i=0):
                b = afirst[name] + i
                assert b == an[0], (name, i, b, an[0])
                an[0] += 1
                if b >= 3:
                    e, v = adone_at[b - 3]
                    pe.wait_ge(s_aev[e], v)
                return ps[:, 5 + b % 3, :]

            def exact(dst, wh, wl, xh, xl, start, stop):
                mm(dst, wh, xh, start=start, stop=False)
                mm(dst, wh, xl, start=False, stop=False)
                return mm(dst, wl, xh, start=False, stop=stop)

            def weights(w, sel):
                ci = wchunk[w]
                k, n = chunks[ci][2:]
                pe.wait_ge(s_lo, ci + 1)
                h = whi[:, w % HIS, 0:k * n].rearrange("p (k n) -> p k n", k=k)
                lo = wlo[:, ci % RAWS, 0:k * n].rearrange("p (k n) -> p k n", k=k)
                return [(sel(h[:, i, :]), sel(lo[:, i, :])) for i in range(k)]

            def cols_of(c0, c1):
                return lambda v: v[:, c0:c1]

            def product(dst, wts, movers, k0=0, k1=None, start=True, stop=True):
                k1 = len(wts) if k1 is None else k1
                for k in range(k0, k1):
                    xh, xl, wait = movers[k]
                    if wait:
                        pe.wait_ge(*wait)
                    ins = exact(dst, *wts[k], xh, xl, start and k == k0, stop and k == k1 - 1)
                return ins

            def sums(tile, k, n):
                for t in range(NT):
                    ins = mm(ps[:, 4, t:t + 1], tile[:, t * P:(t + 1) * P], ones,
                             start=(k == 0 and t == 0), stop=(k == n - 1), skip_group_check=True)
                return ins

            def spread(name, rcol):
                dst = abegin(name)
                for t in range(NT):
                    ins = nc.tensor.transpose(dst[:, t * P:(t + 1) * P], rcol[:, t:t + 1].to_broadcast([P, P]), ident)
                ins.then_inc(s_aux, 1)

            def kcol(n):
                return keep[:, 8 * n:8 * n + NT]

            sqs = [0]

            def sum_sq(tile, k, n, free=None, via=None):
                if via is None:
                    sqs[0] += 1
                    pe.wait_ge(s_sq, sqs[0])
                else:
                    took(pe, *via)
                if free:
                    pe.wait_ge(*free)
                sums(tile, k, n).then_inc(s_cs, 1)

            pe.wait_ge(s_con, 16)
            for k in range(KD):
                sum_sq(sqx[k % 2], k, KD)
            pe.wait_ge(s_rs, 1)
            spread("n0", kcol(0))
            for g in range(2):
                pe.wait_ge(s_lo, 4 * g + 4)
                dst = abegin("mod", g)
                for c in range(8):
                    ins = mm(dst[:, c:c + 1], acc[:, (8 * g + c) * P:(8 * g + c + 1) * P], ones, start=True, stop=True)
                ins.then_inc(s_aux, 1)

            h1 = [(Bh[:, k, :], Bl[:, k, :], (s_hl, k + 1)) for k in range(KD)]
            w = [0]

            def chunk(names, movers=h1, step=P):
                for n, (name, i) in enumerate(names):
                    product(begin(name, i), weights(w[0], cols_of(n * step, (n + 1) * step)), movers) \
                        .then_inc(s_blk, 1)
                w[0] += 1

            group = [(begin("kiw", 0)[0:72, :], weights(0, cols_of(0, 72))),
                     (begin("qi", 0), weights(1, cols_of(0, P))), (begin("qi", 1), weights(1, cols_of(P, 2 * P)))]
            for k in range(KD):
                for dst, wts in group:
                    ins = product(dst, wts, h1, k, k + 1, start=(k == 0), stop=(k == KD - 1))
                    if k == KD - 1:
                        ins.then_inc(s_blk, 1)
            w[0] = 2
            took(pe, "kiw", 0)
            mm(abegin("kirot")[0:HD, :], rot64[0:HD, 0:HD], kiw[0:HD, :], start=True, stop=True).then_inc(s_aux, 1)
            dst = abegin("wiT")
            for t in range(NT):
                ins = nc.tensor.transpose(dst[:, 8 * t:8 * t + 8], kiw[64:72, t * P:(t + 1) * P], ident[64:72, 64:72])
            ins.then_inc(s_aux, 1)
            chunk([("qi", 2), ("qi", 3)])

            def turn(name, i, rot, src, of):
                took(pe, *of)
                mm(abegin(name, i), rot, src, start=True, stop=True).then_inc(s_aux, 1)

            for i in range(2):
                turn("qirot", i, rot64, qiT[:, i, :], ("qi", i))
            chunk([("k", 0), ("vT", 0)])
            for i in range(2, 4):
                turn("qirot", i, rot64, qiT[:, i, :], ("qi", i))
            pe.wait_ge(s_kid, 1)
            pe.wait_ge(s_qi, 4)
            for n in range(24):
                qt, h = n // 8 + 1, n % 8
                b0, wd = HD * (h % 2), (qt + 1) * P
                mm(abegin("idx", n)[:, 0:wd], qiT[b0:b0 + HD, h // 2, qt * P:(qt + 1) * P],
                   kid[b0:b0 + HD, 0:wd], start=True, stop=True).then_inc(s_aux, 1)
            chunk([("q", 0), ("q", 1)])
            chunk([("q", 2), ("q", 3)])

            def head_sums(i, tile, via):
                took(pe, *via)
                for t in range(NT):
                    ins = mm(ps[:, 4, t * 10 + 2 * i:t * 10 + 2 * i + 2], tile[:, t * P:(t + 1) * P],
                             con[:, C_HS:C_HS + 2], start=(i == 0 and t == 0), stop=True, skip_group_check=True)
                return ins

            pe.wait_ge(s_v, 1)
            head_sums(0, sqk, ("k", 0)).then_inc(s_cs, 1)
            for i in range(3):
                head_sums(1 + i, gat[:, i, :], ("q", i)).then_inc(s_cs, 1)
            chunk([("ga", 0), ("ga", 1)])
            head_sums(4, gat[:, 3, :], ("q", 3)).then_inc(s_cs, 1)
            pe.wait_ge(s_lo, 16)
            dst = abegin("gmod")
            for c in range(8):
                ins = mm(dst[:, c:c + 1], gacc[:, c * P:(c + 1) * P], ones, start=True, stop=True)
            ins.then_inc(s_aux, 1)
            turn("krot", 0, rot64, kraw, ("k", 0))
            turn("qrot", 0, rot64, qT[:, 0, :], ("q", 0))
            chunk([("ga", 2), ("ga", 3)])
            for i in range(1, 4):
                turn("qrot", i, rot64, qT[:, i, :], ("q", i))
            pe.wait_ge(s_rs, 2)
            dst = abegin("kb")
            for t in range(NT):
                ins = nc.tensor.transpose(dst[:, t * P:(t + 1) * P], kbx[:, t, :], ident)
            ins.then_inc(s_aux, 1)
            dst = abegin("vtok")
            took(pe, "vT", 0)
            for t in range(NT):
                ins = nc.tensor.transpose(dst[:, t * P:(t + 1) * P], vT[:, t * P:(t + 1) * P], ident)
            ins.then_inc(s_aux, 1)
            chunk([("u", 0), ("u", 1)])
            chunk([("u", 2), ("u", 3)])
            chunk([("gp", 0), ("gp", 1)])
            pe.wait_ge(s_wp, 16)

            def pool(i):
                pe.wait_ge(s_pld, i + 1)
                mm(abegin("pool", i), wpt[:, i, :], uT[:, i, :], start=True, stop=True).then_inc(s_aux, 1)

            pool(0)
            chunk([("gp", 2), ("gp", 3)])
            for i in range(1, 4):
                pool(i)

            def attention(base, scores, values, p, pT, pair_free):
                def qk(h):
                    for n, qt in enumerate(QORD):
                        b = (4, 5, 5, 6)[n]
                        if h and n != 2:
                            pe.wait_ge(s_msk, base * 32 + 4 * (h - 1) + (1, 3, 3, 4)[n])
                        o = SOFF[qt] % 512
                        scores(h, qt, ps[:, b, o:o + (qt + 1) * P]).then_inc(s_qk, 1)

                def turn_p(h):
                    pe.wait_ge(s_pn, base * 32 + 4 * h + 4)
                    for b, kts in enumerate(((0,), (1, 3), (2,))):
                        if h:
                            pe.wait_ge(s_pc, base * 24 + 3 * (h - 1) + b + 1)
                        for kt in kts:
                            for qt in range(kt, NT):
                                o = TOFF[kt] % 512 + P * (qt - kt)
                                s = SOFF[qt] + P * kt
                                ins = nc.tensor.transpose(ps[:, b, o:o + P], p[h % 3][:, s:s + P], ident)
                        ins.then_inc(s_pt, 1)

                def pv(h):
                    if h % 2 == 0 and h >= 4:
                        pe.wait_ge(*pair_free(h // 2 - 2))
                    pe.wait_ge(s_pc, base * 24 + 3 * h + 3)
                    for kt in range(NT):
                        ins = mm(ps[HD * (h % 2):HD * (h % 2) + HD, obank(h // 2), P * kt:T], values(h, kt),
                                 pT[h % 2][:, TOFF[kt]:TOFF[kt] + T - P * kt], start=(kt == 0), stop=(kt == NT - 1),
                                 skip_group_check=True)
                    ins.then_inc(s_pv, 1)

                qk(0)
                qk(1)
                for h in range(8):
                    if h < 6:
                        qk(h + 2)
                    if h:
                        pv(h - 1)
                    turn_p(h)
                pv(7)

            def scores1(h, qt, dst):
                b0, n = HD * (h % 2), (qt + 1) * P
                pe.wait_ge(s_ql, 2 + h + 1)
                mm(dst, Bh[:, h, qt * P:n], Bl[:, h // 4, 0:n], start=True, stop=False)
                return mm(dst, Bh[b0:b0 + HD, h, qt * P:n], Bl[b0:b0 + HD, 2 + h // 4, 0:n], start=False, stop=True)

            for i in range(4):
                took(pe, "gp", i)
            for i in range(2, 4):
                atook(pe, "pool", i)
            attention(0, scores1, lambda h, kt: vtok[:, kt * P + HD * (h // 4):kt * P + HD * (h // 4) + HD], p1, pT1,
                      lambda pair: (s_ao, pair + 1))
            mixer1 = ([(pmh[:, k, :], pml[:, k, :], (s_ml, k + 1)) for k in range(4)]
                      + [(aoh[:, k, :], aol[:, k, :], (s_ml, k + 5)) for k in range(4)])
            for i in range(0, 8, 2):
                chunk([("y", i), ("y", i + 1)], mixer1)
                if i:
                    for j in (i - 2, i - 1):
                        sum_sq(sqy[j % 2], j, KD, (s_v, 2) if j == 0 else None)
            hg = [(Bh[:, k, :], Bl[:, k, :], (s_hl, 8 + k + 1)) for k in range(KD)]
            product(begin("in2", 0), weights(w[0], cols_of(0, P)), hg).then_inc(s_blk, 1)
            for j in (6, 7):
                sum_sq(sqy[j % 2], j, KD)
            product(begin("in2", 1), weights(w[0], cols_of(P, 2 * P)), hg).then_inc(s_blk, 1)
            w[0] += 1
            pe.wait_ge(s_rs, 3)
            spread("n2", kcol(2))
            for i in range(2, 8, 2):
                chunk([("in2", i), ("in2", i + 1)], hg)
            for i in range(2):
                sum_sq(sq2[i % 2], i, 3, (s_v, 3))
            product(begin("in2", 8), weights(w[0], cols_of(0, P)), hg).then_inc(s_blk, 1)
            sum_sq(sq2[0], 2, 3)
            product(begin("in2", 9), weights(w[0], cols_of(32, 160)), hg).then_inc(s_blk, 1)
            w[0] += 1
            sum_sq(sq2[1], 0, 2, (s_v, 4))
            sum_sq(sq2[0], 1, 2)
            product(begin("in2", 10), weights(w[0], cols_of(0, P)), hg).then_inc(s_blk, 1)
            turn("krrot", 0, rot32, kro, ("in2", 9))
            pe.wait_ge(s_rs, 4)
            spread("n3", kcol(3))
            pe.wait_ge(s_rs, 5)
            spread("n4", kcol(4))
            product(begin("in2", 11), weights(w[0], cols_of(P, 2 * P)), hg).then_inc(s_blk, 1)
            w[0] += 1
            chunk([("in2", 12), ("in2", 13)], hg)
            qn = [(qnh[:, k, :], qnl[:, k, :], (s_hl, 16 + k + 1)) for k in range(3)]
            kvn = [(kvh[:, k, :], kvl[:, k, :], (s_hl, 19 + k + 1)) for k in range(2)]

            for c in range(2):
                chunk([("qb", 3 * c + n) for n in range(3)], qn)
            for i in range(4):
                product(begin("kn", i), weights(w[0], cols_of(P * i, P * i + P)), kvn).then_inc(s_blk, 1)
            for i in range(2):
                turn("q2rot", i, rot32, qro[:, i, :], ("qb", 3 * i + 2))
            for t in range(NT):
                wts = weights(w[0], cols_of(512, 1024))
                dst = begin("v2", t)
                for k in range(2):
                    sl = slice(t * P, (t + 1) * P)
                    (wh, wl), (xh, xl, _) = wts[k], kvn[k]
                    mm(dst, xh[:, sl], wh, start=(k == 0), stop=False)
                    mm(dst, xh[:, sl], wl, start=False, stop=False)
                    ins = mm(dst, xl[:, sl], wh, start=False, stop=(k == 1))
                ins.then_inc(s_blk, 1)
            w[0] += 1

            def scores2(h, qt, dst):
                b0, r0 = HD * (h % 2), 32 * (h % 4)
                q0, n = qt * P, (qt + 1) * P
                mm(dst, qno[b0:b0 + HD, h // 2, q0:q0 + P], kno[b0:b0 + HD, h // 2, 0:n], start=True, stop=False)
                return mm(dst, qro[r0:r0 + 32, h // 4, q0:q0 + P], kro[r0:r0 + 32, 0:n], start=False, stop=True,
                          tile_position=(r0, 0))

            for i in range(4):
                took(pe, "v2", i)
            atook(pe, "q2rot", 1)
            pe.wait_ge(s_kr4, 3)
            pe.wait_ge(s_q2, 2)
            attention(1, scores2, lambda h, kt: v2[:, kt, HD * h:HD * h + HD], p2, pT2,
                      lambda pair: (s_ml, 8 + pair + 1))
            mixer2 = [(Bh[:, k, :], Bl[:, k, :], (s_ml, 8 + k + 1)) for k in range(KD)]
            pe.wait_ge(s_ml, 12)
            pe.wait_ge(s_v, 5)
            for j in range(4):
                pe.wait_ge(s_cv, j + 1) if j < DVE_CONV else pe.wait_ge(s_cvp, j - DVE_CONV + 1)
                ins = sums(cacc[:, j, :], j, 4)
            ins.then_inc(s_mus, 1)
            halves = []
            for i in range(4):
                dst = begin("mix", i)
                wts = weights(w[0] + i // 2, cols_of(P * (i % 2), P * (i % 2) + P))
                halves.append((dst, wts))
                product(dst, wts, mixer2, 0, 4, stop=False)
                if i == 1:
                    pe.wait_ge(s_mu, 1)
                    spread("lnm", mu)
            for j in range(4):
                sum_sq(sq2[j % 2], j, 4)
            pe.wait_ge(s_rs, 6)
            spread("lnv", kcol(5))
            for i in range(4):
                product(*halves[i], mixer2, 4, 8, start=False).then_inc(s_blk, 1)
                if i >= 2:
                    sum_sq(sq2[i % 2], i - 2, KD, (s_v, 6), via=("mix", i - 2))
            w[0] += 2
            for i in range(4, 8, 2):
                chunk([("mix", i), ("mix", i + 1)], mixer2)
                for j in (i - 2, i - 1):
                    sum_sq(sq2[j % 2], j, KD, via=("mix", j))
            for j in (6, 7):
                sum_sq(sq2[j % 2], j, KD, via=("mix", j))
            pe.wait_ge(s_rs, 7)
            spread("n6", kcol(6))
            h2 = [(Bh[:, k, :], Bl[:, k, :], (s_hl, 21 + k + 1)) for k in range(KD)]
            pair = [(begin("ffn", i), weights(w[0], cols_of(P * i, P * i + P))) for i in range(2)]
            for k in range(KD):
                for i in range(2):
                    ins = product(*pair[i], h2, k, k + 1, start=(k == 0), stop=(k == KD - 1))
                    if k == KD - 1:
                        ins.then_inc(s_blk, 1)
            for k in range(KD):
                sum_sq(mix[:, k, :], k, KD, (s_v, 7))
            w[0] += 1
            pe.wait_ge(s_rs, 8)
            spread("n7", kcol(7))
            for j in range(1, NJ):
                chunk([("ffn", 2 * j), ("ffn", 2 * j + 1)], h2)
            ff = [(fh[:, k, :], fl[:, k, :], (s_fl, k + 1)) for k in range(NJ)]
            for e in range(KD):
                dst = begin("down", e)
                product(dst, weights(w[0], cols_of(0, P)), ff[0:11], stop=False).then_inc(s_half, 1)
                product(dst, weights(w[0] + 1, cols_of(0, P)), ff[11:22], start=False).then_inc(s_blk, 1)
                w[0] += 2
                if e:
                    sum_sq(cv[(e - 1) % 2], e - 1, KD, (s_v, 8), via=("down", e - 1))
            sum_sq(cv[1], 7, KD, via=("down", 7))
            pe.wait_ge(s_pTl, 2)
            for i in range(8):
                t, hf = i // 2, i % 2
                wts = weights(w[0], cols_of(512 * hf, 512 * hf + 512))
                dst = begin("e", i)
                for k in range(2):
                    sl = slice(t * P, (t + 1) * P)
                    wh, wl = wts[k]
                    mm(dst, pTh[:, k, sl], wh, start=(k == 0), stop=False)
                    mm(dst, pTh[:, k, sl], wl, start=False, stop=False)
                    ins = mm(dst, pTl[:, k, sl], wh, start=False, stop=(k == 1))
                ins.then_inc(s_blk, 1)
                if i == 1:
                    pe.wait_ge(s_rs, 9)
                    spread("n8", kcol(8))
            w[0] += 1

            def gate(dst, t, k):
                sl = slice(t * P, (t + 1) * P)
                wh, wl = wts[k]
                mm(dst, h3h[:, k, sl], wh, start=(k == 0), stop=False)
                mm(dst, h3h[:, k, sl], wl, start=False, stop=False)
                return mm(dst, h3l[:, k, sl], wh, start=False, stop=(k == KD - 1))

            for c in range(4):
                wts = weights(w[0], cols_of(0, 256))
                if c == 0:
                    dsts = [begin(*gate_block(t))[:, 0:256] for t in range(NT)]
                    for k in range(KD):
                        pe.wait_ge(s_hl, 29 + k + 1)
                        for t in range(NT):
                            ins = gate(dsts[t], t, k)
                            if k == KD - 1:
                                ins.then_inc(s_blk, 1)
                else:
                    for t in range(NT):
                        dst = begin(*gate_block(4 * c + t))[:, 0:256]
                        for k in range(KD):
                            ins = gate(dst, t, k)
                        ins.then_inc(s_blk, 1)
                w[0] += 1
                if c < 2:
                    for i in range(4 * c, 4 * c + 4):
                        t, hf = i % 4, i // 4
                        dst = begin(("h3a", "h3b")[hf], t)
                        for k in range(4):
                            ins = nc.tensor.transpose(dst[:, k * P:(k + 1) * P], R[:, 4 * hf + k, t * P:(t + 1) * P],
                                                      ident)
                        ins.then_inc(s_blk, 1)
            assert w[0] == len(wchunk) and an[0] == len(aplan) and bn[0] == len(plan)

        @block.vector
        def _(dve):
            v = nc.vector
            dc, lw, ci_at, nn = [0], [0], [0], [0]
            evD, aevD = s_ev["D"], s_aev["D"]

            def link(ins):
                dc[0] += 1
                ins.then_inc(dch, 1)
                dve.wait_ge(dch, dc[0])

            def lo(n=1):
                for _ in range(n):
                    w = lw[0]
                    ci = wchunk[w]
                    assert ci == ci_at[0], (ci, ci_at[0])
                    dve.wait_ge(s_hi, w + 1)
                    k, m = chunks[ci][2:]
                    src = raw[:, ci % RAWS, 0:k * m]
                    v.tensor_tensor(wlo[:, ci % RAWS, 0:k * m], src, whi[:, w % HIS, 0:k * m].bitcast(F32),
                                    ALU.subtract).then_inc(s_lo, 1)
                    lw[0] += 1
                    ci_at[0] += 1

            def ada(dst, k0, parts, width, cont):
                ci = ci_at[0]
                dve.wait_ge(s_raw[ci % RAWS], landed[ci])
                for i in range(parts):
                    src = raw[:, ci % RAWS, i * width:(i + 1) * width]
                    c = csil[:, k0 + i:k0 + i + 1]
                    if i == 0 and not cont:
                        ins = v.tensor_scalar(dst, src, c, None, ALU.mult)
                    else:
                        ins = v.scalar_tensor_tensor(dst, src, c, dst, ALU.mult, ALU.add)
                    if i < parts - 1:
                        link(ins)
                ins.then_inc(s_lo, 1)
                ci_at[0] += 1
                dve.wait_ge(s_lo, ci_at[0])

            def variance(src, n, count=NT):
                v.tensor_scalar(nrm[:, 0, 0:count], src, 1.0 / n, EPS, ALU.mult, ALU.add).then_inc(s_v, 1)

            def rstd(dst, count=NT):
                nn[0] += 1
                dve.wait_ge(s_rt, nn[0])
                va, ro, r, tt = (nrm[:, i, 0:count] for i in range(4))
                link(v.reciprocal(r, ro))
                link(v.tensor_tensor(tt, r, r, ALU.mult))
                link(v.tensor_tensor(tt, tt, va, ALU.mult))
                link(v.tensor_scalar(tt, tt, -0.5, 1.5, ALU.mult, ALU.add))
                return v.tensor_tensor(dst, r, tt, ALU.mult)

            def norm(summed, count, idx):
                dve.wait_ge(s_cs, summed)
                variance(ps[:, 4, 0:NT], count)
                rstd(keep[:, 8 * idx:8 * idx + NT]).then_inc(s_rs, 1)

            def rope(dst, src, name, i, parts=P, cos=cosT, sin=sinT, tmp=(t1, t2)):
                rot = afilled(dve, name, i)
                link(v.tensor_tensor(tmp[0][0:parts, :], src, cos[0:parts, :], ALU.mult))
                v.tensor_tensor(tmp[1][0:parts, :], rot[0:parts, :], sin[0:parts, :], ALU.mult).then_inc(aevD, 1)
                atook(dve, name, i)
                return v.tensor_tensor(dst, tmp[0][0:parts, :], tmp[1][0:parts, :], ALU.add)

            dve.wait_ge(s_con, 16)
            dve.wait_ge(s_vec, 16)
            dve.wait_ge(s_csil, 1)
            def halves(x):
                return x.rearrange("p (a g c) -> p g a c", a=2, g=2)

            def modulation(g):
                mod = afilled(dve, "mod", g)
                v.tensor_tensor(halves(mtmp)[:, g], mod[:, 0:8].rearrange("p (a c) -> p a c", a=2),
                                halves(col("b_ada", 0, 16))[:, g], ALU.add).then_inc(aevD, 1)
                atook(dve, "mod", g)
                v.scalar_tensor_tensor(mcol[:, 4 * g:4 * g + 4], mtmp[:, 8 + 4 * g:12 + 4 * g], 1.0,
                                       col("norm_w", 4 * g, 4), ALU.add, ALU.mult).then_inc(s_mod, 1)

            def low1(k):
                dve.wait_ge(s_hh, k + 1)
                v.tensor_tensor(Bl[:, k, :], xr[:, k, :], Bh[:, k, :].bitcast(F32), ALU.subtract).then_inc(s_hl, 1)

            for g in range(2):
                for k in range(0, KD, 2):
                    ada(acc[:, g * D:(g + 1) * D], k, 2, D, k > 0)
                    if g == 0 and k == 2:
                        norm(8, D, 0)
                    if g == 1 and k == 2:
                        modulation(0)
                    if g == 1 and k >= 4:
                        low1(k - 4)
                        low1(k - 3)
            modulation(1)
            lo(2)
            for k in range(4, KD):
                low1(k)
            lo(1)
            dve.wait_ge(s_trig, 16)
            took(dve, "kiw", 0)
            rope(kid[0:HD, :], kiw[0:HD, :], "kirot", 0, HD).then_inc(s_ki, 1)
            v.tensor_scalar(small[:, 48:80], afilled(dve, "wiT")[:, 0:32], 8 ** -0.5, None, ALU.mult).then_inc(aevD, 1)
            atook(dve, "wiT")
            lo(1)
            for i in range(4):
                took(dve, "qi", i)
                if i:
                    dve.wait_ge(s_qi, i)
                rope(qiT[:, i, :], qiT[:, i, :], "qirot", i).then_inc(s_qi, 1)
                if i == 1:
                    ada(gacc, 0, 2, D, False)
            ada(gacc, 2, 2, D, True)
            tk = [0]

            def topk(n):
                for _ in range(n):
                    qt, r = tk[0] // (TOPK // 8) + 1, tk[0] % (TOPK // 8)
                    s = sc[:, qt, 0:(qt + 1) * P]
                    link(v.max(m8, s))
                    link(v.match_replace(s, m8, s, TAKEN))
                    if r == TOPK // 8 - 1:
                        link(v.tensor_scalar(s, s, -2e38, NEG, ALU.is_gt, ALU.mult))
                    tk[0] += 1

            for n in range(24):
                qt, h = n // 8 + 1, n % 8
                wd = (qt + 1) * P
                atook(dve, "idx", n)
                dst, r, wcol = sc[:, qt, 0:wd], rl[:, n % 2, 0:wd], wiT[:, qt, h:h + 1]
                if h == 0:
                    v.tensor_scalar(dst, r, wcol, None, ALU.mult).then_inc(s_idx, 1)
                else:
                    dve.wait_ge(s_idx, n)
                    v.scalar_tensor_tensor(dst, r, wcol, dst, ALU.mult, ALU.add).then_inc(s_idx, 1)
                if n in (8, 12):
                    ada(gacc, n // 2, 2, D, True)
                if n in (16, 20):
                    lo(1)
                elif n > 16 and n != 23:
                    topk(1)
                if h == 7:
                    dve.wait_ge(s_idx, n + 1)
                    diag = sc[:, qt, qt * P:wd]
                    link(v.tensor_tensor(diag, diag, tri, ALU.add))
            lo(1)
            topk(9)
            lo(1)
            topk(11)
            lo(1)
            topk(2)
            gm = afilled(dve, "gmod")
            v.tensor_tensor(gtcol, gm[:, 0:8], col("b_ada", 16, 8), ALU.add).then_inc(aevD, 1)
            took(dve, "k", 0)
            link(rope(kraw, kraw, "krot", 0))
            took(dve, "q", 0)
            rope(qT[:, 0, :], qT[:, 0, :], "qrot", 0).then_inc(s_qr, 1)
            dve.wait_ge(s_cs, 13)
            variance(ps[:, 4, 0:40], HD, 40)
            topk(2)
            link(rstd(small[:, 176:216], 40))
            link(v.tensor_scalar(rqs, rqk[:, :, 2:10], SCALE1, None, ALU.mult))
            for h in range(2):
                ins = v.tensor_copy(kbx[:, :, h * HD:(h + 1) * HD], rqk[:, :, h:h + 1].to_broadcast([P, NT, HD]))
                if h == 0:
                    link(ins)
            ins.then_inc(s_rs, 1)
            for i in range(1, 4):
                dve.wait_ge(s_qr, i)
                took(dve, "q", i)
                rope(qT[:, i, :], qT[:, i, :], "qrot", i).then_inc(s_qr, 1)
            v.tensor_tensor(kraw, kraw, afilled(dve, "kb"), ALU.mult).then_inc(aevD, 1)
            lo(1)
            topk(5)
            lo(1)
            topk(2)

            def pooled(g):
                wdw = 2 << g
                S = pp[g % 2][:, CP:CP + T]
                dve.wait_ge(s_pool, g + 1)
                took(dve, "u", g)
                link(v.tensor_tensor(t1[:, 0:wdw], S[:, 0:wdw], con[:, C_RC:C_RC + wdw], ALU.mult))
                link(v.tensor_tensor(uT[:, g, 0:wdw], t1[:, 0:wdw], uT[:, g, 0:wdw], ALU.subtract))
                v.scalar_tensor_tensor(uT[:, g, wdw:T], S[:, wdw:T], 1.0 / wdw, uT[:, g, wdw:T], ALU.mult,
                                       ALU.subtract).then_inc(s_pld, 1)

            def mixed(g):
                dve.wait_ge(s_pld, g + 1)
                m = afilled(dve, "pool", g)
                took(dve, "gp", g)
                v.scalar_tensor_tensor(uT[:, g, :], m, col("pool_scale", g), gp[:, g, :], ALU.mult,
                                       ALU.mult).then_inc(aevD, 1)

            pooled(0)
            topk(1)
            lo(1)
            topk(2)
            pooled(1)
            pooled(2)
            topk(3)
            lo(1)
            pooled(3)
            topk(3 * TOPK // 8 - tk[0])
            lo(1)
            for g in range(4):
                mixed(g)
            for g in range(4):
                dve.wait_ge(s_mh, g + 1)
                v.tensor_tensor(pml[:, g, :], uT[:, g, :], pmh[:, g, :].bitcast(F32), ALU.subtract).then_inc(s_ml, 1)

            def attention(base, mask, negate, p, take_pair, out_pair, between):
                def masked(h):
                    if h >= 3:
                        dve.wait_ge(s_pt, base * 24 + 3 * (h - 2))
                    for n, qt in enumerate(QORD):
                        o, wd = SOFF[qt], (qt + 1) * P
                        dve.wait_ge(s_qk, base * 32 + 4 * h + (1, 3, 3, 4)[n])
                        b = (4, 5, 5, 6)[n]
                        v.tensor_tensor_reduce(out=p[h % 3][:, o:o + wd], in0=ps[:, b, o % 512:o % 512 + wd],
                                               in1=mask(qt), scale=1.0, scalar=-3e38, op0=ALU.add, op1=ALU.max,
                                               accum_out=mx[:, h % 2, qt:qt + 1]).then_inc(s_msk, 1)
                    dve.wait_ge(s_msk, base * 32 + 4 * h + 4)
                    negate(h).then_inc(s_nb, 1)

                def normalised(h):
                    dve.wait_ge(s_exp, base * 32 + 4 * h + 4)
                    link(v.reciprocal(rsm[:, h % 2, :], sm[:, h % 2, :]))
                    for qt in QORD:
                        o, wd = SOFF[qt], (qt + 1) * P
                        s = p[h % 3][:, o:o + wd]
                        v.tensor_scalar(s, s, rsm[:, h % 2, qt:qt + 1], None, ALU.mult).then_inc(s_pn, 1)

                masked(0)
                for h in range(8):
                    if h < 7:
                        masked(h + 1)
                    if h >= 3 and h % 2:
                        take_pair(h // 2 - 1)
                    normalised(h)
                    between(h)
                    if h >= 3 and h % 2:
                        out_pair(h // 2 - 1)
                take_pair(3)
                out_pair(3)

            def negate1(h):
                return v.scalar_tensor_tensor(nb[:, h % 2, :], mx[:, h % 2, :], -1.0, rqs[:, :, h], ALU.mult, ALU.mult)

            def low_q(h):
                b0 = HD * (h % 2)
                dve.wait_ge(s_qh, 2 + h + 1)
                v.tensor_tensor(Bh[HD - b0:2 * HD - b0, h, :], qT[b0:b0 + HD, h // 2, :],
                                Bh[b0:b0 + HD, h, :].bitcast(F32), ALU.subtract).then_inc(s_ql, 1)

            for i in range(2):
                dve.wait_ge(s_qh, i + 1)
                v.tensor_tensor(Bl[:, 2 + i, :], kdup[:, i, :], Bl[:, i, :].bitcast(F32),
                                ALU.subtract).then_inc(s_ql, 1)
            for h in range(3):
                low_q(h)

            def between1(h):
                if h < 5:
                    low_q(h + 3)
                lo(h == 2)

            def take1(pair):
                dve.wait_ge(s_pv, 2 * pair + 2)
                if pair:
                    dve.wait_ge(s_ml, 4 + pair)
                v.tensor_tensor(ao, ps[:, obank(pair), :], gat[:, pair, :], ALU.mult).then_inc(s_ao, 1)

            def out1(pair):
                dve.wait_ge(s_mh, 4 + pair + 1)
                v.tensor_tensor(aol[:, pair, :], ao, aoh[:, pair, :].bitcast(F32), ALU.subtract).then_inc(s_ml, 1)

            attention(0, lambda qt: tri if qt == 0 else sc[:, qt, 0:(qt + 1) * P], negate1, p1, take1, out1, between1)
            for k in range(KD):
                v.scalar_tensor_tensor(R[:, k, :], filled(dve, "y", k), gtcol[:, k:k + 1], R[:, k, :], ALU.mult,
                                       ALU.add).then_inc(evD, 1)
                took(dve, "y", k)
                dve.wait_ge(s_hh, 8 + k + 1)
                v.scalar_tensor_tensor(Bl[:, k, :], R[:, k, :], col("g_mix_pre_2", k), Bh[:, k, :].bitcast(F32),
                                       ALU.mult, ALU.subtract).then_inc(s_hl, 1)
                if k % 2:
                    lo(1)
            norm(21, D, 2)
            atook(dve, "n2")

            def tmul(dst, i, signal):
                v.tensor_tensor(dst, filled(dve, "in2", i), rB, ALU.mult).then_inc(signal, 1)

            cs, tap_at = [0], [0] * 4
            taps = [(j, t) for t in range(10) for j in range(2)]
            taps += [(j, t + (10 if j < 2 else 0)) for t in range(CW) for j in range(DVE_CONV) if j == 2 or t + 10 < CW]

            def conv(n):
                for _ in range(min(n, len(taps) - cs[0])):
                    j, t = taps[cs[0]]
                    src = cpad[:, j, CP - (CW - 1) + t:CP - (CW - 1) + t + T]
                    wcol = col("conv_w_2", t * 4 + j)
                    if t == 0:
                        ins = v.tensor_scalar(cacc[:, j, :], src, wcol, col("conv_b_2", j), ALU.mult, ALU.add)
                    else:
                        dve.wait_ge(dch, tap_at[j])
                        ins = v.scalar_tensor_tensor(cacc[:, j, :], src, wcol, cacc[:, j, :], ALU.mult, ALU.add)
                    if t < CW - 1:
                        ins.then_inc(dch, 1)
                        dc[0] += 1
                        tap_at[j] = dc[0]
                    else:
                        ins.then_inc(s_cv, 1)
                    cs[0] += 1

            dve.wait_ge(s_cpz, 1)
            def gates(j0):
                for j in (j0, j0 + 1):
                    tmul(gt2[:, j % 2, :], GATE[j], evD)

            def gated(j0):
                for j in (j0, j0 + 1):
                    tmul(tmpa, VALUE[j], evD)
                    took(dve, "in2", VALUE[j])
                    dve.wait_ge(s_sg, j + 1)
                    ins = v.tensor_tensor(cpad[:, j, CP:CP + T], tmpa, gt2[:, j % 2, :], ALU.mult)
                    if j < DVE_CONV:
                        link(ins)
                    else:
                        ins.then_inc(s_cp, 1)
                        dve.wait_ge(s_cp, j - DVE_CONV + 1)

            gates(0)
            lo(1)
            gated(0)
            lo(1)
            conv(6)
            for i in range(2):
                tmul(qa[:, i, :], 4 + i, evD)
            lo(1)
            conv(8)
            tmul(qa[:, 2, :], 6, evD)
            tmul(kva[:, 0, :], 7, evD)
            lo(1)
            conv(6)
            tmul(kva[:, 1, :], 8, evD)
            tmul(kro, 9, evD)
            took(dve, "in2", 9)
            norm(24, 384, 3)
            norm(26, 256, 4)
            gates(2)
            lo(1)
            dve.wait_ge(s_tab, 2)
            rope(kro, kro, "krrot", 0, tmp=(s2c, tmpa)).then_inc(s_kr, 1)
            b = afilled(dve, "n3")
            for i in range(3):
                v.scalar_tensor_tensor(qa[:, i, :], qa[:, i, :], col("g_q_a_2", i), b, ALU.mult, ALU.mult) \
                    .then_inc(s_qn if i < 2 else aevD, 1)
            b = afilled(dve, "n4")
            for i in range(2):
                v.scalar_tensor_tensor(kva[:, i, :], kva[:, i, :], col("g_kv_a_2", i), b, ALU.mult, ALU.mult) \
                    .then_inc(s_qn if i < 1 else aevD, 1)
            for i in range(3):
                dve.wait_ge(s_hh, 16 + i + 1)
                v.tensor_tensor(qnl[:, i, :], qa[:, i, :], qnh[:, i, :].bitcast(F32), ALU.subtract).then_inc(s_hl, 1)
            for i in range(2):
                dve.wait_ge(s_hh, 19 + i + 1)
                v.tensor_tensor(kvl[:, i, :], kva[:, i, :], kvh[:, i, :].bitcast(F32), ALU.subtract).then_inc(s_hl, 1)
            lo(1)
            gated(2)
            lo(1)
            conv(2)
            lo(1)
            conv(6)
            for i in range(2):
                took(dve, "qb", 3 * i + 2)
                rope(qro[:, i, :], qro[:, i, :], "q2rot", i, tmp=(s2c, tmpa)).then_inc(s_q2, 1)
                if i == 0:
                    lo(1)
                dve.wait_ge(s_q2, i + 1)
            conv(3)

            def negate2(h):
                return v.tensor_scalar(nb[:, h % 2, :], mx[:, h % 2, :], -SCALE2, None, ALU.mult)

            def out2(pair):
                dve.wait_ge(s_mh, 8 + pair + 1)
                v.tensor_tensor(Bl[:, pair, :], ps[:, obank(pair), :], Bh[:, pair, :].bitcast(F32),
                                ALU.subtract).then_inc(s_ml, 1)

            attention(1, lambda qt: con[:, C_TRI + 384 - P * qt:C_TRI + 512], negate2, p2, lambda pair: None, out2,
                      lambda h: (conv(7), lo(h == 3)))
            conv(len(taps))
            dve.wait_ge(s_mus, 1)
            v.tensor_scalar(mu, ps[:, 4, 0:NT], 1.0 / 512, None, ALU.mult).then_inc(s_mu, 1)
            b = afilled(dve, "lnm")
            for j in range(4):
                v.tensor_tensor(cacc[:, j, :], cacc[:, j, :], b, ALU.subtract).then_inc(s_ln if j < 3 else aevD, 1)
            norm(30, 512, 5)
            b = afilled(dve, "lnv")
            for j in range(4):
                v.tensor_tensor(cacc[:, j, :], cacc[:, j, :], b, ALU.mult).then_inc(s_ln2 if j < 3 else aevD, 1)
            for j in range(4):
                dve.wait_ge(s_mh, 12 + j + 1)
                v.tensor_tensor(Bl[:, 4 + j, :], cacc[:, j, :], Bh[:, 4 + j, :].bitcast(F32),
                                ALU.subtract).then_inc(s_ml, 1)
            lo(3)
            norm(38, D, 6)

            def low2(k):
                dve.wait_ge(s_hh, 21 + k + 1)
                v.scalar_tensor_tensor(Bl[:, k, :], R[:, k, :], col("g_ffn_pre_2", k), Bh[:, k, :].bitcast(F32),
                                       ALU.mult, ALU.subtract).then_inc(s_hl, 1)

            for k in range(KD):
                dve.wait_ge(s_scaled, k + 1)
                v.tensor_tensor(R[:, k, :], R[:, k, :], mix[:, k, :], ALU.add).then_inc(s_h2, 1)
                dve.wait_ge(s_h2, k + 1)
                if k:
                    low2(k - 1)
            low2(KD - 1)
            lo(1)
            norm(46, D, 7)
            atook(dve, "n7")
            link(v.memset(zg[:, 0:16], 0.0))
            for j in range(NJ):
                c = cv[j % 2]
                if j:
                    dve.wait_ge(s_z, j)
                if j > 1:
                    dve.wait_ge(s_fl, j - 1)
                v.tensor_tensor(zg[:, 16:16 + T], filled(dve, "ffn", 2 * j), rBf, ALU.mult).then_inc(evD, 1)
                took(dve, "ffn", 2 * j)
                link(v.tensor_scalar(c, zg[:, 16:16 + T], col("ffn_dw_w_2", 2 * NJ + j), col("ffn_dw_b_2", j),
                                     ALU.mult, ALU.add))
                link(v.scalar_tensor_tensor(c, zg[:, 15:15 + T], col("ffn_dw_w_2", NJ + j), c, ALU.mult, ALU.add))
                v.scalar_tensor_tensor(c, zg[:, 14:14 + T], col("ffn_dw_w_2", j), c, ALU.mult,
                                       ALU.add).then_inc(s_z, 1)
                if j:
                    dve.wait_ge(s_fd, j)
                v.tensor_tensor(up, filled(dve, "ffn", 2 * j + 1), rBf, ALU.mult).then_inc(evD, 1)
                dve.wait_ge(s_gl, j + 1)
                took(dve, "ffn", 2 * j + 1)
                v.tensor_tensor(c, c, up, ALU.mult).then_inc(s_fd, 1)
                lo(1)
                dve.wait_ge(s_fh, j + 1)
                v.tensor_tensor(fl[:, j, :], c, fh[:, j, :].bitcast(F32), ALU.subtract).then_inc(s_fl, 1)
            for e in range(KD):
                lo(1)
                if e == 0:
                    for k in range(2):
                        dve.wait_ge(s_pTh, k + 1)
                        v.tensor_tensor(pTl[:, k, :], pTf[:, k, :], pTh[:, k, :].bitcast(F32),
                                        ALU.subtract).then_inc(s_pTl, 1)
                if e < KD - 1:
                    lo(1)
            norm(54, D, 8)

            def square_e(i):
                t, hf = i // 2, i % 2
                took(dve, "e", i)
                src = etok[:, t, 512 * hf:512 * hf + 512]
                link(v.tensor_tensor_reduce(out=cosT, in0=src, in1=src, scale=1.0, scalar=0.0, op0=ALU.mult,
                                            op1=ALU.add, accum_out=sse[:, t, hf:hf + 1]))

            for i in range(3):
                square_e(i)

            def low3(k):
                dve.wait_ge(s_hh, 29 + k + 1)
                v.tensor_tensor(h3l[:, k, :], R[:, k, :], h3h[:, k, :].bitcast(F32), ALU.subtract).then_inc(s_hl, 1)

            for k in range(KD):
                dve.wait_ge(s_scaled, KD + k + 1)
                v.tensor_tensor(R[:, k, :], R[:, k, :], fo[:, k, :], ALU.add).then_inc(s_h3, 1)
                dve.wait_ge(s_h3, k + 1)
                if k:
                    low3(k - 1)
            low3(KD - 1)
            lo(1)
            for i in range(3, 8):
                square_e(i)
            link(v.tensor_tensor(mu, sse[:, :, 0], sse[:, :, 1], ALU.add))
            variance(mu, D)
            def token_major(hf):
                for t in range(NT):
                    v.tensor_copy(htok[:, t, 512 * hf:512 * hf + 512],
                                  filled(dve, ("h3a", "h3b")[hf], t)).then_inc(evD, 1)
                took(dve, ("h3a", "h3b")[hf], 3)

            token_major(0)
            lo(1)
            link(rstd(keep[:, 72:76]))
            dve.wait_ge(s_grow, 16)
            for t in range(NT):
                link(v.scalar_tensor_tensor(etok[:, t, :], etok[:, t, :], keep[:, 72 + t:73 + t], grow, ALU.mult,
                                            ALU.mult))
            for i in range(16):
                c, t = i // 4, i % 4
                if i == 4:
                    token_major(1)
                    lo(1)
                took(dve, *gate_block(i))
                cl = slice(c * 256, (c + 1) * 256)
                link(v.tensor_tensor(otok[:, t, cl], otok[:, t, cl], etok[:, t, cl], ALU.mult))
                v.tensor_tensor(otok[:, t, cl], otok[:, t, cl], htok[:, t, cl], ALU.add).then_inc(s_ot, 1)
            assert lw[0] == len(wchunk), (lw[0], len(wchunk))
            assert tk[0] == 3 * TOPK // 8


def kernel(**inputs):
    import concourse.bacc as _bacc
    from concourse import mybir as _mybir
    from concourse.bass_utils import run_bass_kernel_spmd as _run

    get = {name: np.ascontiguousarray(v) for name, v in inputs.items()}
    arrays = {}
    arrays["xT"] = np.ascontiguousarray(get["x"][0].T).reshape(KD, P, T)
    arrays["pT"] = np.ascontiguousarray(get["p_2"][0, 0].T).reshape(2, P, T)
    rows = []
    for name, n in VECS:
        v = get[name].reshape(-1)
        if name in ("q_norm_w", "k_norm_w"):
            v = np.concatenate([v, v])
        rows.append(v.reshape(n, P))
    arrays["vecs"] = np.ascontiguousarray(np.concatenate(rows).T)
    pieces = []
    for _, parts in stream():
        tiles = [get[name][0][r0:r1][:, cols].reshape((r1 - r0) // P, P, len(cols)) for name, r0, r1, cols in parts]
        pieces.append(np.concatenate(tiles, axis=2).transpose(1, 0, 2).reshape(-1))
    arrays["stream"] = np.concatenate(pieces)
    arrays["con"] = constants()
    for name in ("w_pool", "positions_2", "g_ple_2"):
        arrays[name] = get[name]
    nc = _bacc.Bacc("TRN2", target_bir_lowering=False, num_devices=1)
    args = {name: nc.dram_tensor(f"in_{name}_dram", v.shape, _mybir.dt.from_np(v.dtype), kind="ExternalInput").ap()
            for name, v in arrays.items()}
    out = nc.dram_tensor("out_0_dram", (1, T, D), _mybir.dt.float32, kind="ExternalOutput").ap()
    build(nc, args, out)
    r = _run(nc, [{f"in_{name}_dram": v for name, v in arrays.items()}], core_ids=[0])
    return r.results[0]["out_0_dram"]
```

```python
from contextlib import ExitStack

import concourse.bass as bass
import numpy as np
from concourse import mybir

ALU = mybir.AluOpType
ACT = mybir.ActivationFunctionType
F32 = mybir.dt.float32
F32R = mybir.dt.float32r
I32 = mybir.dt.int32

P = 128
T = 512
NT = T // P
D = 1024
KD = D // P
EPS = 1e-6
NEG = -1e30
TAKEN = -3e38
HD = 64
TOPK = min(256, T // 4)
FF = 2816
NJ = FF // P
CW = 31
CP = 32
SCALE1 = HD ** -0.5
SCALE2 = 96 ** -0.5

GATE, VALUE = (0, 1, 10, 11), (2, 3, 12, 13)
DVE_CONV = 3
RAWS = 3
HIS = 3
QORD = (3, 2, 0, 1)
SOFF = {3: 0, 2: 512, 0: 896, 1: 1024}
TOFF = {0: 0, 1: 512, 3: 896, 2: 1024}
QB = (("n", 0), ("n", 1), ("r", 0), ("n", 2), ("n", 3), ("r", 1))
INV2PI = float(np.float32(1 / (2 * np.pi)))
ROUND = 1.5 * 2 ** 23
_c1 = 6.28125
TWOPI = (_c1, float(np.uint32(np.float32(2 * np.pi - _c1).view(np.uint32) & 0xFFFFF000).view(np.float32)))
TWOPI = TWOPI + (float(np.float32(2 * np.pi - TWOPI[0] - TWOPI[1])),)
PI32 = float(np.nextafter(np.float32(np.pi), np.float32(0)))

U0, GP0, Q0, K0, V0, GA0, QI0, KI0, WI0, E1 = 0, 512, 1024, 1536, 1664, 1792, 2304, 2816, 2880, 2888

C_ID, C_R64, C_R32, C_HS, C_ONE, C_FREQ, C_RC, C_TRI, C_COS, C_SIN, C_END = (
    0, 128, 256, 384, 386, 388, 389, 405, 917, 1429, 1941)

VECS = [("c", 8), ("norm_w", 8), ("b_ada", 24), ("pool_scale", 4), ("g_mix_pre_2", 8), ("g_mix_post_2", 8),
        ("g_ffn_pre_2", 8), ("g_ffn_post_2", 8), ("ffn_dw_b_2", 22), ("conv_b_2", 4), ("conv_ln_g_2", 4),
        ("conv_ln_b_2", 4), ("g_q_a_2", 3), ("g_kv_a_2", 2), ("q_norm_w", 1), ("k_norm_w", 1),
        ("ffn_dw_w_2", 66), ("conv_w_2", 124)]
NV = sum(n for _, n in VECS)


def stream():
    def cols(c0, c1):
        return np.arange(c0, c1)

    out = [("ada", [("w_ada", k * P, (k + 2) * P, np.concatenate([cols(c, c + 512), cols(D + c, D + c + 512)]))])
           for c in (0, 512) for k in range(0, KD, 2)]

    def w(name, rows, columns):
        out.append(("w", [(name, rows[0], rows[1], columns)]))

    w("w_in", (0, D), cols(KI0, E1))
    for c in (QI0, QI0 + 256, K0):
        w("w_in", (0, D), cols(c, c + 256))

    for c in (Q0, Q0 + 256, GA0, GA0 + 256, U0, U0 + 256, GP0, GP0 + 256):
        w("w_in", (0, D), cols(c, c + 256))
    for c in range(0, D, 256):
        w("w_out", (0, D), cols(c, c + 256))
    for c in (1184, 672, 0, 256):
        w("w_in_2", (0, D), cols(c, c + 256))
    w("w_in_2", (0, D), cols(512, 672))
    for c in (1440, 928):
        w("w_in_2", (0, D), cols(c, c + 256))
    for c in range(2):
        heads = np.arange(4 * c, 4 * c + 4)[:, None] * 96
        w("w_q_b_2", (0, 384), np.concatenate([(heads + np.arange(HD)).ravel(), (heads + np.arange(HD, 96)).ravel()]))
    heads = np.arange(8)[:, None] * P
    w("w_kv_b_2", (0, 256), np.concatenate([(heads + np.arange(HD)).ravel(), (heads + np.arange(HD, P)).ravel()]))
    for c in range(0, D, 256):
        w("w_o_2", (0, D), cols(c, c + 256))
    for j in range(NJ):
        out.append(("w", [(n, 0, D, cols(j * P, (j + 1) * P)) for n in ("w_ffn_gate_2", "w_ffn_up_2")]))
    for e in range(KD):
        for h in range(2):
            w("w_ffn_down_2", (h * 11 * P, (h + 1) * 11 * P), cols(e * P, (e + 1) * P))
    w("w_ple_proj_2", (0, 256), cols(0, D))
    for c in range(0, D, 256):
        w("w_ple_gate_2", (0, D), cols(c, c + 256))
    return out


def constants():
    c = np.zeros((P, C_END), np.float32)
    c[:, C_ID:C_ID + P] = np.eye(P)
    for base, w in ((C_R64, 64), (C_R32, 32)):
        for m in range(P):
            if m % w < w // 2:
                c[m + w // 2, base + m] = -1.0
            else:
                c[m - w // 2, base + m] = 1.0
    q, k = np.arange(P)[:, None], np.arange(P)[None, :]
    c[:, C_TRI + 384:C_TRI + 512] = np.where(k <= q, 0.0, NEG)
    c[0:64, C_HS] = 1.0
    c[64:128, C_HS + 1] = 1.0
    c[:, C_ONE:C_ONE + 2] = 1.0
    half = 16
    inv = (10000.0 ** (-np.arange(0, 32, 2, dtype=np.float32) / np.float32(32))).astype(np.float32)
    c[:, C_FREQ] = inv[np.arange(P) % half]
    c[:, C_RC:C_RC + 16] = 1.0 / np.arange(1, 17)
    freqs = (10000.0 ** (-np.arange(32, dtype=np.float32) / np.float32(32))).astype(np.float32)
    ang = (np.arange(T, dtype=np.float32)[None, :] * freqs[np.arange(P) % 32][:, None]).astype(np.float32)
    c[:, C_COS:C_COS + T] = np.cos(ang.astype(np.float64))
    c[:, C_SIN:C_SIN + T] = np.sin(ang.astype(np.float64))
    return c


def build(nc, a, out):
    ctx = ExitStack()
    with ctx:


        def sem(name):
            return ctx.enter_context(nc.semaphore(name))

        spot = [(nc.sbuf_base + 63) // 64 * 64]

        def place(name, shape, dt=F32, at=None):
            size = int(np.prod(shape[1:])) * 4
            off = spot[0] if at is None else at
            if at is None:
                spot[0] += (size + 31) // 32 * 32
            return nc.alloc_sbuf_tensor_at(name, shape, dt, offset=off), off

        raw, raw_at = place("raw", [P, RAWS, 2048])
        wlo, _ = place("wlo", [P, RAWS, 2048], F32R, raw_at)
        whi, _ = place("whi", [P, HIS, 2048], F32R)
        R, _ = place("R", [P, KD, T])
        Bh, bh_at = place("Bh", [P, 8, T], F32R)
        Bl, bl_at = place("Bl", [P, 8, T], F32R)
        Bhf, _ = place("Bhf", [P, 8 * T], F32, bh_at)
        Blf, _ = place("Blf", [P, 8 * T], F32, bl_at)
        A, a_at = place("A", [P, 44 * T])
        Ar, _ = place("Ar", [P, 44 * T], F32R, a_at)
        M, _ = place("M", [P, 4 * T + 16])
        con, _ = place("con", [P, C_END])
        wpt, _ = place("wpt", [P, 4, P])
        vec, _ = place("vec", [P, NV])
        small, _ = place("small", [P, 400])
        nrm, _ = place("nrm", [P, 4, 40])
        assert spot[0] <= nc.sbuf_usable_end
        ps = ctx.enter_context(nc.psum_tensor("ps", [P, 8, 512], F32))

        def av(tile, n=1, w=T, of=A):
            lo = int(tile * T)
            return of[:, lo:lo + n * w].rearrange("p (n w) -> p n w", n=n)

        def ar(tile, n):
            return av(tile, n, of=Ar)

        ident = con[:, C_ID:C_ID + P]
        ones = con[:, C_ONE:C_ONE + 1]
        cosT, sinT = con[:, C_COS:C_COS + T], con[:, C_SIN:C_SIN + T]
        tri = con[:, C_TRI + 384:C_TRI + 512]
        rot64, rot32 = con[:, C_R64:C_R64 + P], con[:, C_R32:C_R32 + P]

        vat, at = {}, 0
        for name, n in VECS:
            vat[name] = at
            at += n

        def col(name, i=0, n=1):
            return vec[:, vat[name] + i:vat[name] + i + n]

        csil = small[:, 0:8]
        mcol = small[:, 8:16]
        gtcol = small[:, 24:32]
        mtmp = small[:, 32:48]
        wiT = small[:, 48:80].rearrange("p (t h) -> p t h", t=NT)
        m8 = small[:, 296:320].rearrange("p (t n) -> p t n", t=3)
        mx = small[:, 88:96].rearrange("p (b t) -> p b t", b=2)
        nb = small[:, 96:104].rearrange("p (b t) -> p b t", b=2)
        sm = small[:, 104:112].rearrange("p (b t) -> p b t", b=2)
        rsm = small[:, 112:120].rearrange("p (b t) -> p b t", b=2)
        rqs = small[:, 120:152].rearrange("p (t h) -> p t h", t=NT)
        mu = small[:, 152:156]
        sse = small[:, 168:176].rearrange("p (t h) -> p t h", t=NT)
        rqk = small[:, 176:216].rearrange("p (t h) -> p t h", t=NT)
        keep = small[:, 216:296]

        qiT, kid, kiw, sc = av(0, 4), av(4)[:, 0], av(5)[:, 0], av(6, 4)
        qT, kdup, vtok, gat = av(10, 4), av(14, 2), av(16)[:, 0], av(17, 4)
        uT, gp = av(21, 4), av(25, 4)
        kraw = uT[:, 3]
        aoh, aol = ar(21, 4), ar(25, 4)
        xr = av(29, 8)
        pmh, pml = ar(29, 4), ar(33, 4)
        qs, kh, kl = ar(29, 8), ar(14, 1)[:, 0], ar(15, 1)[:, 0]
        gbuf = [A[:, 17 * T:21 * T], A[:, 25 * T:29 * T]]
        pp = [A[:, 37 * T:37 * T + T + CP], A[:, 38 * T + CP:39 * T + 2 * CP]]
        acc = A[:, 40 * T:44 * T]
        gacc = M[:, 0:2 * T]
        t1, t2, rl = av(40)[:, 0], av(41)[:, 0], av(42, 2)
        kbx = av(43, 1)[:, 0].rearrange("p (t w) -> p t w", t=NT)
        vT, sqk = M[:, 2 * T:3 * T], M[:, 3 * T:4 * T]
        sqx = [vT, sqk]
        p1 = [A[:, 0:1280], A[:, 1280:2560], Blf[:, 4 * T:4 * T + 1280]]
        pT1 = [A[:, 37 * T + 1280 * i:37 * T + 1280 * (i + 1)] for i in range(2)]
        ao = av(42)[:, 0]
        sqy = [av(40)[:, 0], av(41)[:, 0]]
        cpad = A[:, 0:4 * (T + CP)].rearrange("p (n w) -> p n w", n=4)
        cacc = av(4.25, 4)
        gt2, qa, kva = av(8.25, 2), av(10.25, 3), av(13.25, 2)
        qnh, qnl, kvh, kvl = ar(15.25, 3), ar(18.25, 3), ar(21.25, 2), ar(23.25, 2)
        qno, qro, kno, kro = av(25.25, 4), av(29.25, 2), av(31.25, 4), av(35.25)[:, 0]
        v2 = av(36.25, 4)
        s2a, s2b, s2c = av(40.25)[:, 0], av(41.25)[:, 0], av(42.25)[:, 0]
        sq2 = [s2a, s2b]
        p2 = [A[:, o:o + 1280] for o in (int(8.25 * T), int(10.75 * T), int(18.25 * T))]
        pT2 = [A[:, int(13.25 * T) + 1280 * i:int(13.25 * T) + 1280 * (i + 1)] for i in range(2)]
        mix = av(25.25, 8)
        rB, tmpa = M[:, 0:T], M[:, T:2 * T]
        posi, posf = M[:, 2 * T:3 * T].bitcast(I32), M[:, 3 * T:4 * T]
        turns = M[:, 2 * T:3 * T]
        fh, fl = ar(0, NJ), ar(NJ, NJ)
        zg = M[:, 0:T + 16]
        cv = [M[:, T + 16:2 * T + 16], M[:, 2 * T + 16:3 * T + 16]]
        up = M[:, 3 * T + 16:4 * T + 16]
        rBf = sinT
        fo = Bhf[:, :].rearrange("p (n w) -> p n w", n=8)
        etok, htok, otok = av(0, 4, D), av(8, 4, D), av(32, 4, D)
        h3h, h3l = ar(16, 8), ar(24, 8)
        pTf = Blf[:, 0:2 * T].rearrange("p (k n) -> p k n", k=2)
        pTh, pTl = Bl[:, 2:4, :], Bl[:, 4:6, :]
        grow = Blf[:, 6 * T:8 * T]

        chunks, at = [], 0
        for kind, parts in stream():
            k, n = (parts[0][2] - parts[0][1]) // P, sum(len(x[3]) for x in parts)
            chunks.append((kind, a["stream"][at:at + P * k * n].rearrange("(p n) -> p n", p=P), k, n))
            at += P * k * n
        wchunk = [i for i, c in enumerate(chunks) if c[0] == "w"]
        wnum = {ci: w for w, ci in enumerate(wchunk)}
        W_FFN = len(wchunk) - NJ - 2 * KD - 5
        W_DOWN = W_FFN + NJ
        landed = [16 * (ci // RAWS + 1) for ci in range(len(chunks))]

        plan = ([("kiw", "A")] + [("qi", "A")] * 4 + [("k", "A"), ("vT", "A")] + [("q", "A")] * 4
                + [("ga", "A")] * 4 + [("u", "A")] * 4 + [("gp", "A")] * 4 + [("y", "D")] * 8
                + [("in2", "D")] * 14 + [("qb", "A")] * 6 + [("kn", "A")] * 4 + [("v2", "A")] * 4 + [("mix", "A")] * 8
                + [("ffn", "D")] * (2 * NJ) + [("down", "A")] * 8 + [("e", "A")] * 8 + [("plg", "A")] * 4
                + [("h3a", "D")] * 4 + [("plh", "A")] * 4 + [("h3b", "D")] * 4 + [("pli", "A")] * 8)
        aplan = ([("n0", "A"), ("mod", "D"), ("mod", "D"), ("kirot", "D"), ("wiT", "D")] + [("qirot", "D")] * 4
                 + [("idx", "A")] * 24 + [("gmod", "D"), ("krot", "D")] + [("qrot", "D")] * 4
                 + [("kb", "D"), ("vtok", "A")] + [("pool", "D")] * 4
                 + [("n2", "A"), ("krrot", "D"), ("n3", "D"), ("n4", "D")] + [("q2rot", "D")] * 2
                 + [("lnm", "D"), ("lnv", "D"), ("n6", "A"), ("n7", "A"), ("n8", "A")])

        def takers(order):
            first, done, count = {}, [], {"A": 0, "D": 0}
            for i, (name, e) in enumerate(order):
                first.setdefault(name, i)
                count[e] += 1
                done.append((e, count[e]))
            return first, done

        first, done_at = takers(plan)
        afirst, adone_at = takers(aplan)
        per_chunk = ([1] + [2] * 11 + [2] * 4 + [2] * 7 + [3, 3, 8] + [2] * 4 + [2] * NJ + [0, 1] * KD
                     + [8, 4, 8, 8, 4])
        chunk_end = [int(x) for x in np.cumsum(per_chunk)]

        s_raw = [sem(f"s_raw{i}") for i in range(RAWS)]
        s_hi = sem("s_hi")
        s_lo = sem("s_lo")
        s_half = sem("s_half")
        s_blk = sem("s_blk")
        s_ev = {"A": sem("s_evA"), "D": sem("s_evD")}
        s_aux = sem("s_aux")
        s_aev = {"A": sem("s_aevA"), "D": sem("s_aevD")}
        s_con, s_trig, s_vec, s_wp = sem("s_con"), sem("s_trig"), sem("s_vec"), sem("s_wp")
        s_x = [sem(f"s_x{i}") for i in range(4)]
        s_pos, s_p, s_grow, s_out = sem("s_pos"), sem("s_p"), sem("s_grow"), sem("s_out")
        dch, ach, pch = sem("dve_chain"), sem("act_chain"), sem("pool_chain")
        s_csil = sem("s_csil")
        s_v, s_rt, s_rs = sem("s_v"), sem("s_rt"), sem("s_rs")
        s_sq, s_cs = sem("s_sq"), sem("s_cs")
        s_mod = sem("s_mod")
        s_xr = sem("s_xr")
        s_hh, s_hl = sem("s_hh"), sem("s_hl")
        s_ki, s_qi = sem("s_ki"), sem("s_qi")
        s_idx = sem("s_idx")
        s_gr, s_ga = [sem("s_gr0"), sem("s_gr1")], sem("s_ga")
        s_kh, s_kl, s_qsh, s_qs = sem("s_kh"), sem("s_kl"), sem("s_qsh"), sem("s_qs")
        s_kd, s_qr = sem("s_kd"), sem("s_qr")
        s_qh, s_ql = sem("s_qh"), sem("s_ql")
        s_pool, s_pld = sem("s_pool"), sem("s_pld")
        s_qk, s_msk, s_nb, s_exp = sem("s_qk"), sem("s_msk"), sem("s_nb"), sem("s_exp")
        s_pn, s_pt, s_pc, s_pv = sem("s_pn"), sem("s_pt"), sem("s_pc"), sem("s_pv")
        s_ao = sem("s_ao")
        s_mh, s_ml = sem("s_mh"), sem("s_ml")
        s_ang, s_tab = sem("s_ang"), sem("s_tab")
        s_sg = sem("s_sg")
        s_cp, s_cvp = sem("s_cp"), sem("s_cvp")
        s_cpz, s_cv = sem("s_cpz"), sem("s_cv")
        s_scaled = sem("s_scaled")
        s_qn = sem("s_qn")
        s_kr, s_kr4 = sem("s_kr"), sem("s_kr4")
        s_q2 = sem("s_q2")
        s_mus, s_mu = sem("s_mus"), sem("s_mu")
        s_ln, s_ln2 = sem("s_ln"), sem("s_ln2")
        s_h2, s_h3 = sem("s_h2"), sem("s_h3")
        s_z, s_gl, s_fd = sem("s_z"), sem("s_gl"), sem("s_fd")
        s_fh, s_fl = sem("s_fh"), sem("s_fl")
        s_pTh, s_pTl = sem("s_pTh"), sem("s_pTl")
        s_ot = sem("s_ot")

        def bank(name, i):
            return (first[name] + i) % 4

        def took(eng, name, i):
            e, v = done_at[first[name] + i]
            eng.wait_ge(s_ev[e], v)

        def abank(name, i=0):
            return 5 + (afirst[name] + i) % 3

        def atook(eng, name, i=0):
            e, v = adone_at[afirst[name] + i]
            eng.wait_ge(s_aev[e], v)

        def filled(eng, name, i):
            eng.wait_ge(s_blk, first[name] + i + 1)
            return ps[:, bank(name, i), :]

        def afilled(eng, name, i=0):
            eng.wait_ge(s_aux, afirst[name] + i + 1)
            return ps[:, abank(name, i), :]

        def used(eng, w):
            if W_DOWN <= w < W_DOWN + 2 * KD and (w - W_DOWN) % 2 == 0:
                eng.wait_ge(s_half, (w - W_DOWN) // 2 + 1)
            else:
                eng.wait_ge(s_blk, chunk_end[w])

        def idx_item(n):
            return n % 12 // 4 + 1, 4 * (n // 12) + n % 4

        def gate_block(i):
            return ("plg", i) if i < 4 else ("plh", i - 4) if i < 8 else ("pli", i - 8)

        def obank(pair):
            return 3 if pair % 2 == 0 else 7

        block = ctx.enter_context(nc.Block())

        @block.sync
        def _(sp):
            sp.dma_start(vec[:, :], a["vecs"]).then_inc(s_vec, 16)
            for i in range(4):
                sp.dma_start(R[:, 2 * i:2 * i + 2, :], a["xT"][2 * i:2 * i + 2].rearrange("k p t -> p k t")) \
                    .then_inc(s_x[i], 16)
                if i == 0:
                    sp.dma_start(con[:, 0:C_TRI], a["con"][:, 0:C_TRI]).then_inc(s_con, 16)
            for ci, (kind, src, k, n) in enumerate(chunks):
                if ci == 10:
                    sp.dma_start(con[:, C_TRI:C_END], a["con"][:, C_TRI:C_END]).then_inc(s_trig, 16)
                if ci >= RAWS:
                    if chunks[ci - RAWS][0] == "w":
                        used(sp, wnum[ci - RAWS])
                    else:
                        sp.wait_ge(s_lo, ci - RAWS + 1)
                sp.dma_start(raw[:, ci % RAWS, 0:k * n], src).then_inc(s_raw[ci % RAWS], 16)
                if ci == 10:
                    for g in range(2):
                        sp.dma_start(gbuf[g], a["gate"][g]).then_inc(s_gr[g], 16)
                if ci == 11:
                    for g in range(2, 4):
                        sp.wait_ge(s_ga, g - 1)
                        sp.dma_start(gbuf[g - 2], a["gate"][g]).then_inc(s_gr[g - 2], 16)
                if ci == 20:
                    sp.dma_start(wpt[:, :, :], a["w_pool"][0].rearrange("g c d -> c g d")).then_inc(s_wp, 16)
            for i in range(16):
                sp.wait_ge(s_ot, i + 1)
                c, t = i // 4, i % 4
                sp.dma_start(out[0, t * P:(t + 1) * P, c * 256:(c + 1) * 256],
                             otok[:, t, c * 256:(c + 1) * 256]).then_inc(s_out, 16)
            sp.wait_ge(s_out, 16 * 16)

        @block.gpsimd
        def _(g):
            pc = [0]

            def link(ins):
                pc[0] += 1
                ins.then_inc(pch, 1)
                g.wait_ge(pch, pc[0])

            g.wait_ge(s_aev["A"], 1)
            for k in range(KD):
                g.wait_ge(s_x[k // 2], 16)
                g.tensor_tensor(xr[:, k, :], R[:, k, :], rB, ALU.mult).then_inc(s_xr, 1)
            for i in range(2):
                ins = g.memset(pp[i][:, 0:CP], 0.0)
                link(ins)
            for grp in range(4):
                took(g, "u", grp)
                if grp:
                    g.wait_ge(s_pld, grp)
                link(g.tensor_copy(pp[0][:, CP:CP + 1], uT[:, grp, 0:1]))
                for step in range(grp + 1):
                    d = 1 << step
                    src, dst = pp[(step + 1) % 2], pp[step % 2]
                    if step == 0:
                        ins = g.tensor_tensor(dst[:, CP + 1:CP + T], uT[:, grp, 1:T], uT[:, grp, 0:T - 1], ALU.add)
                    else:
                        ins = g.tensor_tensor(dst[:, CP:CP + T], src[:, CP:CP + T], src[:, CP - d:CP - d + T], ALU.add)
                    if step < grp:
                        link(ins)
                ins.then_inc(s_pool, 1)
            took(g, "vT", 0)
            g.wait_ge(s_cs, 9)
            atook(g, "vtok")
            g.dma_start(posi, a["positions_2"].partition_broadcast(P)).then_inc(s_pos, 16)
            g.wait_ge(s_pos, 16)
            link(g.tensor_copy(posf, posi))
            link(g.tensor_scalar(posf, posf, con[:, C_FREQ:C_FREQ + 1], None, ALU.mult))
            g.wait_ge(s_qr, 4)
            atook(g, "gmod")
            for dst, quarter in ((sinT, 0.0), (cosT, 0.25)):
                link(g.tensor_scalar(turns, posf, INV2PI, quarter, ALU.mult, ALU.add))
                link(g.tensor_scalar(turns, turns, ROUND, None, ALU.add))
                link(g.tensor_scalar(turns, turns, -ROUND, None, ALU.add))
                src = posf
                for part in TWOPI:
                    link(g.tensor_scalar(tmpa, turns, -part, None, ALU.mult))
                    link(g.tensor_tensor(dst, src, tmpa, ALU.add))
                    src = dst
                link(g.tensor_scalar(dst, dst, quarter * 2 * np.pi, PI32, ALU.add, ALU.min))
                ins = g.tensor_scalar(dst, dst, -PI32, None, ALU.max)
                ins.then_inc(s_ang, 1)
            took(g, "y", 0)
            for j in range(4):
                ins = g.memset(cpad[:, j, 0:CP], 0.0)
                if j < 3:
                    link(ins)
            ins.then_inc(s_cpz, 1)
            for n, j in enumerate(range(DVE_CONV, 4)):
                g.wait_ge(s_cp, n + 1)
                for t in range(CW):
                    src = cpad[:, j, CP - (CW - 1) + t:CP - (CW - 1) + t + T]
                    wcol = col("conv_w_2", t * 4 + j)
                    if t == 0:
                        link(g.tensor_scalar(cacc[:, j, :], src, wcol, col("conv_b_2", j), ALU.mult, ALU.add))
                    else:
                        link(g.tensor_scalar(turns, src, wcol, None, ALU.mult))
                        ins = g.tensor_tensor(cacc[:, j, :], cacc[:, j, :], turns, ALU.add)
                        if t < CW - 1:
                            link(ins)
                        else:
                            ins.then_inc(s_cvp, 1)
            atook(g, "n6")
            for k in range(1, KD):
                g.tensor_tensor(mix[:, k, :], mix[:, k, :], rB, ALU.mult).then_inc(s_scaled, 1)
            g.wait_ge(s_blk, first["down"])
            g.dma_start(pTf, a["pT"].rearrange("k p t -> p k t")).then_inc(s_p, 16)
            g.dma_start(grow, a["g_ple_2"][0].partition_broadcast(P)).then_inc(s_grow, 16)
            atook(g, "n8")
            for k in range(KD):
                g.tensor_tensor(fo[:, k, :], fo[:, k, :], rBf, ALU.mult).then_inc(s_scaled, 1)

        @block.scalar
        def _(act):
            f = nc.scalar.activation
            ac, hw, sqn, rt = [0], [0], [0], [0]

            def link(ins):
                ac[0] += 1
                ins.then_inc(ach, 1)
                act.wait_ge(ach, ac[0])

            def hi(n=1):
                for _ in range(n):
                    w = hw[0]
                    ci = wchunk[w]
                    act.wait_ge(s_raw[ci % RAWS], landed[ci])
                    if w >= HIS:
                        used(act, w - HIS)
                    k, nn = chunks[ci][2:]
                    f(whi[:, w % HIS, 0:k * nn], raw[:, ci % RAWS, 0:k * nn], ACT.Copy).then_inc(s_hi, 1)
                    hw[0] += 1

            def square(tile, src, signal=None, depth=1):
                if sqn[0] >= depth:
                    act.wait_ge(s_cs, sqn[0] - depth + 1)
                sqn[0] += 1
                return f(tile, src, ACT.Square).then_inc(signal or s_sq, 1)

            def root(n=NT):
                rt[0] += 1
                act.wait_ge(s_v, rt[0])
                f(nrm[:, 1, 0:n], nrm[:, 0, 0:n], ACT.Sqrt).then_inc(s_rt, 1)

            evA = s_ev["A"]

            act.wait_ge(s_vec, 16)
            f(csil, col("c", 0, 8), ACT.Silu).then_inc(s_csil, 1)
            for k in range(KD):
                act.wait_ge(s_x[k // 2], 16)
                square(sqx[k % 2], R[:, k, :], depth=2)
            root()
            f(rB, afilled(act, "n0"), ACT.Copy).then_inc(s_aev["A"], 1)
            for k in range(KD):
                if k % 4 == 0:
                    act.wait_ge(s_mod, k // 4 + 1)
                act.wait_ge(s_xr, k + 1)
                link(f(xr[:, k, :], xr[:, k, :], ACT.Identity, scale=mcol[:, k:k + 1], bias=mtmp[:, k:k + 1]))
                f(Bh[:, k, :], xr[:, k, :], ACT.Copy).then_inc(s_hh, 1)
                if k == 3:
                    hi(2)
            hi(1)
            f(kiw[0:72, :], filled(act, "kiw", 0)[0:72, :], ACT.Copy).then_inc(evA, 1)
            for i in range(2):
                f(qiT[:, i, :], filled(act, "qi", i), ACT.Copy).then_inc(evA, 1)
            hi(1)
            act.wait_ge(s_ki, 1)
            link(f(kid[HD:P, :], kid[0:HD, :], ACT.Copy))
            f(kh, kid, ACT.Copy).then_inc(s_kh, 1)

            def high_qi(i):
                act.wait_ge(s_qi, i + 1)
                for h in (2 * i, 2 * i + 1):
                    b0 = HD * (h % 2)
                    f(qs[b0:b0 + HD, h, :], qiT[b0:b0 + HD, i, :], ACT.Copy).then_inc(s_qsh, 1)

            def relus(n0, n1):
                for n in range(n0, n1):
                    wd = (idx_item(n)[0] + 1) * P
                    src = afilled(act, "idx", n)
                    if n >= 2:
                        act.wait_ge(s_idx, n - 1)
                    f(rl[:, n % 2, 0:wd], src[:, 0:wd], ACT.Relu, scale=HD ** -0.5).then_inc(s_aev["A"], 1)

            def q_out(i):
                src = filled(act, "q", i)
                link(f(qT[:, i, :], src, ACT.Copy, scale=col("q_norm_w")))
                square(gat[:, i, :], src, evA, 99)

            high_qi(0)
            high_qi(1)
            hi(1)
            for i in range(2, 4):
                f(qiT[:, i, :], filled(act, "qi", i), ACT.Copy).then_inc(evA, 1)
            hi(1)
            relus(0, 6)
            src = filled(act, "k", 0)
            link(f(kraw, src, ACT.Copy, scale=col("k_norm_w")))
            square(sqk, src, evA, depth=1)
            high_qi(2)
            high_qi(3)
            relus(6, 12)
            f(vT, filled(act, "vT", 0), ACT.Copy).then_inc(evA, 1)
            relus(12, 18)
            hi(1)
            act.wait_ge(s_ga, 4)
            q_out(0)
            relus(18, 24)
            q_out(1)
            hi(1)
            q_out(2)
            q_out(3)
            hi(1)
            for i in range(2):
                if i == 0:
                    act.wait_ge(s_cs, 11)
                f(gat[:, i, :], filled(act, "ga", i), ACT.Silu).then_inc(evA, 1)
            hi(1)
            root(40)
            for i in range(2, 4):
                f(gat[:, i, :], filled(act, "ga", i), ACT.Silu).then_inc(evA, 1)
            hi(1)
            atook(act, "kb")
            for i in range(2):
                for h in range(2):
                    f(kdup[h * HD:(h + 1) * HD, i, :], kraw[i * HD:(i + 1) * HD, :], ACT.Copy).then_inc(s_kd, 1)
            f(vtok, afilled(act, "vtok"), ACT.Copy).then_inc(s_aev["A"], 1)
            act.wait_ge(s_kd, 4)
            for i in range(4):
                f(uT[:, i, :], filled(act, "u", i), ACT.Copy).then_inc(evA, 1)
                if i % 2:
                    hi(1)
            for i in range(4):
                f(gp[:, i, :], filled(act, "gp", i), ACT.Silu).then_inc(evA, 1)
                if i == 1:
                    hi(1)
            act.wait_ge(s_kd, 4)
            for i in range(2):
                f(Bl[:, i, :], kdup[:, i, :], ACT.Copy).then_inc(s_qh, 1)
            act.wait_ge(s_qr, 4)
            def high_q(h):
                b0 = HD * (h % 2)
                f(Bh[b0:b0 + HD, h, :], qT[b0:b0 + HD, h // 2, :], ACT.Copy).then_inc(s_qh, 1)

            for h in range(4):
                high_q(h)
            for i in range(4):
                atook(act, "pool", i)
                f(pmh[:, i, :], uT[:, i, :], ACT.Copy).then_inc(s_mh, 1)

            def attention(base, scale_of, p, pT, out_pair, late, between):
                def evac(h):
                    for b, wd in enumerate((512, 512, 256)):
                        act.wait_ge(s_pt, base * 24 + 3 * h + b + 1)
                        if b == 0 and h >= 2:
                            act.wait_ge(s_pv, base * 8 + h - 1)
                        f(pT[h % 2][:, 512 * b:512 * b + wd], ps[:, b, 0:wd], ACT.Copy).then_inc(s_pc, 1)

                for h in range(8):
                    act.wait_ge(s_nb, base * 8 + h + 1)
                    for qt in QORD:
                        o, w = SOFF[qt], (qt + 1) * P
                        f(p[h % 3][:, o:o + w], p[h % 3][:, o:o + w], ACT.Exp, bias=nb[:, h % 2, qt:qt + 1],
                          scale=scale_of(h, qt), accum_out=sm[:, h % 2, qt:qt + 1]).then_inc(s_exp, 1)
                    if h:
                        evac(h - 1)
                    if h >= 3 + late and (h - late) % 2:
                        out_pair((h - late) // 2 - 1)
                    between(h)
                evac(7)
                for pair in range(3 - late, 4):
                    out_pair(pair)

            def out1(pair):
                act.wait_ge(s_ao, pair + 1)
                f(aoh[:, pair, :], ao, ACT.Copy).then_inc(s_mh, 1)

            def between1(h):
                if h < 4:
                    high_q(h + 4)
                if h == 1:
                    hi(1)

            attention(0, lambda h, qt: rqs[:, qt, h:h + 1], p1, pT1, out1, 1, between1)
            act.wait_ge(s_ang, 2)
            f(sinT, sinT, ACT.Sin).then_inc(s_tab, 1)
            f(cosT, cosT, ACT.Sin).then_inc(s_tab, 1)
            for k in range(KD):
                took(act, "y", k)
                f(Bh[:, k, :], R[:, k, :], ACT.Copy, scale=col("g_mix_pre_2", k)).then_inc(s_hh, 1)
                square(sqy[k % 2], R[:, k, :], depth=2)
                if k % 2:
                    hi(1)
            root()
            f(rB, afilled(act, "n2"), ACT.Copy).then_inc(s_aev["A"], 1)
            def gates(j0):
                for j in (j0, j0 + 1):
                    took(act, "in2", GATE[j])
                    f(gt2[:, j % 2, :], gt2[:, j % 2, :], ACT.Sigmoid).then_inc(s_sg, 1)

            gates(0)
            hi(2)
            for i in range(2):
                took(act, "in2", 4 + i)
                square(sq2[i % 2], qa[:, i, :], depth=2)
            hi(1)
            took(act, "in2", 6)
            square(sq2[0], qa[:, 2, :], depth=2)
            took(act, "in2", 7)
            square(sq2[1], kva[:, 0, :], depth=2)
            hi(1)
            took(act, "in2", 8)
            square(sq2[0], kva[:, 1, :], depth=2)
            root()
            root()
            gates(2)
            hi(1)
            for i in range(3):
                if i < 2:
                    act.wait_ge(s_qn, i + 1)
                else:
                    atook(act, "n3")
                f(qnh[:, i, :], qa[:, i, :], ACT.Copy).then_inc(s_hh, 1)
            for i in range(2):
                if i < 1:
                    act.wait_ge(s_qn, 3)
                else:
                    atook(act, "n4")
                f(kvh[:, i, :], kva[:, i, :], ACT.Copy).then_inc(s_hh, 1)
            hi(2)
            act.wait_ge(s_kr, 1)
            for g4 in range(3):
                f(kro[g4 * 32:g4 * 32 + 32, :], kro[96:128, :], ACT.Copy).then_inc(s_kr4, 1)
            for i, (what, n) in enumerate(QB):
                f((qno if what == "n" else qro)[:, n, :], filled(act, "qb", i), ACT.Copy).then_inc(evA, 1)
                if i % 3 == 2:
                    hi(1)
            for i in range(4):
                f(kno[:, i, :], filled(act, "kn", i), ACT.Copy).then_inc(evA, 1)
            for i in range(4):
                f(v2[:, i, :], filled(act, "v2", i), ACT.Copy).then_inc(evA, 1)

            def out2(pair):
                act.wait_ge(s_pv, 8 + 2 * pair + 2)
                f(Bh[:, pair, :], ps[:, obank(pair), :], ACT.Copy).then_inc(s_mh, 1)

            def between2(h):
                if h == 2:
                    hi(1)

            attention(1, lambda h, qt: SCALE2, p2, pT2, out2, 0, between2)
            for j in range(4):
                if j < 3:
                    act.wait_ge(s_ln, j + 1)
                else:
                    atook(act, "lnm")
                square(v2[:, j, :], cacc[:, j, :], depth=99)
            root()
            for j in range(4):
                if j < 3:
                    act.wait_ge(s_ln2, j + 1)
                else:
                    atook(act, "lnv")
                link(f(cacc[:, j, :], cacc[:, j, :], ACT.Silu, scale=col("conv_ln_g_2", j),
                       bias=col("conv_ln_b_2", j)))
                f(Bh[:, 4 + j, :], cacc[:, j, :], ACT.Copy).then_inc(s_mh, 1)
            for k in range(KD):
                link(f(mix[:, k, :], filled(act, "mix", k), ACT.Copy, scale=col("g_mix_post_2", k)))
                square(sq2[k % 2], ps[:, bank("mix", k), :], evA, 2)
                if k in (1, 3, 5):
                    hi(1)
            root()
            f(rB, afilled(act, "n6"), ACT.Copy).then_inc(s_aev["A"], 1)
            for k in range(KD):
                act.wait_ge(s_h2, k + 1)
                f(Bh[:, k, :], R[:, k, :], ACT.Copy, scale=col("g_ffn_pre_2", k)).then_inc(s_hh, 1)
                square(mix[:, k, :], R[:, k, :], depth=99)
            hi(1)
            root()
            f(rBf, afilled(act, "n7"), ACT.Copy).then_inc(s_aev["A"], 1)
            for j in range(NJ):
                act.wait_ge(s_z, j + 1)
                f(cv[j % 2], cv[j % 2], ACT.Gelu_apprx_tanh).then_inc(s_gl, 1)
                hi(1)
                act.wait_ge(s_fd, j + 1)
                f(fh[:, j, :], cv[j % 2], ACT.Copy).then_inc(s_fh, 1)
            for e in range(KD):
                hi(1)
                link(f(fo[:, e, :], filled(act, "down", e), ACT.Copy, scale=col("g_ffn_post_2", e)))
                square(cv[e % 2], ps[:, bank("down", e), :], evA, 2)
                if e == 0:
                    act.wait_ge(s_p, 16)
                    for k in range(2):
                        f(pTh[:, k, :], pTf[:, k, :], ACT.Copy).then_inc(s_pTh, 1)
                if e < KD - 1:
                    hi(1)
            root()

            def high3(k):
                act.wait_ge(s_h3, k + 1)
                f(h3h[:, k, :], R[:, k, :], ACT.Copy).then_inc(s_hh, 1)

            for i in range(8):
                t, hf = i // 2, i % 2
                f(etok[:, t, 512 * hf:512 * hf + 512], filled(act, "e", i), ACT.Copy).then_inc(evA, 1)
                if i == 1:
                    f(rBf, afilled(act, "n8"), ACT.Copy).then_inc(s_aev["A"], 1)
                if i >= 5:
                    high3(i - 5)
            for k in range(3, KD):
                high3(k)
            hi(1)
            for i in range(16):
                c, t = i // 4, i % 4
                if i == 4:
                    hi(2)
                    root()
                src = filled(act, *gate_block(i))
                f(otok[:, t, c * 256:(c + 1) * 256], src[:, 0:256], ACT.Sigmoid).then_inc(evA, 1)
            assert hw[0] == len(wchunk), (hw[0], len(wchunk))

        @block.tensor
        def _(pe):
            mm = nc.tensor.matmul
            an, bn = [0], [0]

            def begin(name, i):
                b = first[name] + i
                assert b == bn[0], (name, i, b, bn[0])
                bn[0] += 1
                if b >= 4:
                    e, v = done_at[b - 4]
                    pe.wait_ge(s_ev[e], v)
                return ps[:, b % 4, :]

            def abegin(name, i=0):
                b = afirst[name] + i
                assert b == an[0], (name, i, b, an[0])
                an[0] += 1
                if b >= 3:
                    e, v = adone_at[b - 3]
                    pe.wait_ge(s_aev[e], v)
                return ps[:, 5 + b % 3, :]

            def exact(dst, wh, wl, xh, xl, start, stop):
                mm(dst, wh, xh, start=start, stop=False)
                mm(dst, wh, xl, start=False, stop=False)
                return mm(dst, wl, xh, start=False, stop=stop)

            def weights(w, sel):
                ci = wchunk[w]
                k, n = chunks[ci][2:]
                pe.wait_ge(s_lo, ci + 1)
                h = whi[:, w % HIS, 0:k * n].rearrange("p (k n) -> p k n", k=k)
                lo = wlo[:, ci % RAWS, 0:k * n].rearrange("p (k n) -> p k n", k=k)
                return [(sel(h[:, i, :]), sel(lo[:, i, :])) for i in range(k)]

            def cols_of(c0, c1):
                return lambda v: v[:, c0:c1]

            def product(dst, wts, movers, k0=0, k1=None, start=True, stop=True):
                k1 = len(wts) if k1 is None else k1
                for k in range(k0, k1):
                    xh, xl, wait = movers[k]
                    if wait:
                        pe.wait_ge(*wait)
                    ins = exact(dst, *wts[k], xh, xl, start and k == k0, stop and k == k1 - 1)
                return ins

            def sums(tile, k, n):
                for t in range(NT):
                    ins = mm(ps[:, 4, t:t + 1], tile[:, t * P:(t + 1) * P], ones,
                             start=(k == 0 and t == 0), stop=(k == n - 1), skip_group_check=True)
                return ins

            def spread(name, rcol):
                dst = abegin(name)
                for t in range(NT):
                    ins = nc.tensor.transpose(dst[:, t * P:(t + 1) * P], rcol[:, t:t + 1].to_broadcast([P, P]), ident)
                ins.then_inc(s_aux, 1)

            def kcol(n):
                return keep[:, 8 * n:8 * n + NT]

            sqs = [0]

            def sum_sq(tile, k, n, free=None, via=None):
                if via is None:
                    sqs[0] += 1
                    pe.wait_ge(s_sq, sqs[0])
                else:
                    took(pe, *via)
                if free:
                    pe.wait_ge(*free)
                sums(tile, k, n).then_inc(s_cs, 1)

            pe.wait_ge(s_con, 16)
            for k in range(KD):
                sum_sq(sqx[k % 2], k, KD)
            pe.wait_ge(s_rs, 1)
            spread("n0", kcol(0))
            for g in range(2):
                pe.wait_ge(s_lo, 4 * g + 4)
                dst = abegin("mod", g)
                for c in range(8):
                    ins = mm(dst[:, c:c + 1], acc[:, (8 * g + c) * P:(8 * g + c + 1) * P], ones, start=True, stop=True)
                ins.then_inc(s_aux, 1)

            h1 = [(Bh[:, k, :], Bl[:, k, :], (s_hl, k + 1)) for k in range(KD)]
            w = [0]

            def chunk(names, movers=h1, step=P):
                for n, (name, i) in enumerate(names):
                    product(begin(name, i), weights(w[0], cols_of(n * step, (n + 1) * step)), movers) \
                        .then_inc(s_blk, 1)
                w[0] += 1

            group = [(begin("kiw", 0)[0:72, :], weights(0, cols_of(0, 72)))]
            product(*group[0], h1, 0, 4, stop=False)
            for i in range(2):
                group.append((begin("qi", i), weights(1, cols_of(P * i, P * i + P))))
                product(*group[1 + i], h1, 0, 4, stop=False)
            for k in range(4, KD):
                for dst, wts in group:
                    ins = product(dst, wts, h1, k, k + 1, start=False, stop=(k == KD - 1))
                    if k == KD - 1:
                        ins.then_inc(s_blk, 1)
            w[0] = 2
            took(pe, "kiw", 0)
            mm(abegin("kirot")[0:HD, :], rot64[0:HD, 0:HD], kiw[0:HD, :], start=True, stop=True).then_inc(s_aux, 1)
            dst = abegin("wiT")
            for t in range(NT):
                ins = nc.tensor.transpose(dst[:, 8 * t:8 * t + 8], kiw[64:72, t * P:(t + 1) * P], ident[64:72, 64:72])
            ins.then_inc(s_aux, 1)

            def turn(name, i, rot, src, of):
                took(pe, *of)
                mm(abegin(name, i), rot, src, start=True, stop=True).then_inc(s_aux, 1)

            for i in range(2):
                turn("qirot", i, rot64, qiT[:, i, :], ("qi", i))
            chunk([("qi", 2), ("qi", 3)])
            for i in range(2, 4):
                turn("qirot", i, rot64, qiT[:, i, :], ("qi", i))

            def woven(names, n):
                for b, (name, i) in enumerate(names):
                    dst, wts = begin(name, i), weights(w[0], cols_of(b * P, (b + 1) * P))
                    for k in range(KD):
                        ins = product(dst, wts, h1, k, k + 1, start=(k == 0), stop=(k == KD - 1))
                        if k == KD - 1:
                            ins.then_inc(s_blk, 1)
                        if k < 6:
                            qt, h = idx_item(n)
                            b0, wd = HD * (h % 2), (qt + 1) * P
                            to = abegin("idx", n)[:, 0:wd]
                            pe.wait_ge(s_qs, h + 1)
                            mm(to, qs[:, h, qt * P:wd], kh[:, 0:wd], start=True, stop=False)
                            mm(to, qs[b0:b0 + HD, h, qt * P:wd], kl[b0:b0 + HD, 0:wd], start=False,
                               stop=True).then_inc(s_aux, 1)
                            n += 1
                w[0] += 1

            pe.wait_ge(s_kl, 1)
            woven([("k", 0), ("vT", 0)], 0)
            woven([("q", 0), ("q", 1)], 12)
            chunk([("q", 2), ("q", 3)])

            def head_sums(i, tile, via):
                took(pe, *via)
                for t in range(NT):
                    ins = mm(ps[:, 4, t * 10 + 2 * i:t * 10 + 2 * i + 2], tile[:, t * P:(t + 1) * P],
                             con[:, C_HS:C_HS + 2], start=(i == 0 and t == 0), stop=True, skip_group_check=True)
                return ins

            pe.wait_ge(s_v, 1)
            head_sums(0, sqk, ("k", 0)).then_inc(s_cs, 1)
            for i in range(3):
                head_sums(1 + i, gat[:, i, :], ("q", i)).then_inc(s_cs, 1)
            chunk([("ga", 0), ("ga", 1)])
            head_sums(4, gat[:, 3, :], ("q", 3)).then_inc(s_cs, 1)
            pe.wait_ge(s_ga, 4)
            dst = abegin("gmod")
            for c in range(8):
                ins = mm(dst[:, c:c + 1], gacc[:, c * P:(c + 1) * P], ones, start=True, stop=True)
            ins.then_inc(s_aux, 1)
            turn("krot", 0, rot64, kraw, ("k", 0))
            turn("qrot", 0, rot64, qT[:, 0, :], ("q", 0))
            chunk([("ga", 2), ("ga", 3)])
            for i in range(1, 4):
                turn("qrot", i, rot64, qT[:, i, :], ("q", i))
            pe.wait_ge(s_rs, 2)
            dst = abegin("kb")
            for t in range(NT):
                ins = nc.tensor.transpose(dst[:, t * P:(t + 1) * P], kbx[:, t, :], ident)
            ins.then_inc(s_aux, 1)
            dst = abegin("vtok")
            took(pe, "vT", 0)
            for t in range(NT):
                ins = nc.tensor.transpose(dst[:, t * P:(t + 1) * P], vT[:, t * P:(t + 1) * P], ident)
            ins.then_inc(s_aux, 1)
            chunk([("u", 0), ("u", 1)])
            chunk([("u", 2), ("u", 3)])
            chunk([("gp", 0), ("gp", 1)])
            pe.wait_ge(s_wp, 16)

            def pool(i):
                pe.wait_ge(s_pld, i + 1)
                mm(abegin("pool", i), wpt[:, i, :], uT[:, i, :], start=True, stop=True).then_inc(s_aux, 1)

            pool(0)
            chunk([("gp", 2), ("gp", 3)])
            for i in range(1, 4):
                pool(i)

            def attention(base, scores, values, p, pT, pair_free):
                def qk(h):
                    for n, qt in enumerate(QORD):
                        b = (4, 5, 5, 6)[n]
                        if h and n != 2:
                            pe.wait_ge(s_msk, base * 32 + 4 * (h - 1) + (1, 3, 3, 4)[n])
                        o = SOFF[qt] % 512
                        scores(h, qt, ps[:, b, o:o + (qt + 1) * P]).then_inc(s_qk, 1)

                def turn_p(h):
                    pe.wait_ge(s_pn, base * 32 + 4 * h + 4)
                    for b, kts in enumerate(((0,), (1, 3), (2,))):
                        if h:
                            pe.wait_ge(s_pc, base * 24 + 3 * (h - 1) + b + 1)
                        for kt in kts:
                            for qt in range(kt, NT):
                                o = TOFF[kt] % 512 + P * (qt - kt)
                                s = SOFF[qt] + P * kt
                                ins = nc.tensor.transpose(ps[:, b, o:o + P], p[h % 3][:, s:s + P], ident)
                        ins.then_inc(s_pt, 1)

                def pv(h):
                    if h % 2 == 0 and h >= 4:
                        pe.wait_ge(*pair_free(h // 2 - 2))
                    pe.wait_ge(s_pc, base * 24 + 3 * h + 3)
                    for kt in range(NT):
                        ins = mm(ps[HD * (h % 2):HD * (h % 2) + HD, obank(h // 2), P * kt:T], values(h, kt),
                                 pT[h % 2][:, TOFF[kt]:TOFF[kt] + T - P * kt], start=(kt == 0), stop=(kt == NT - 1),
                                 skip_group_check=True)
                    ins.then_inc(s_pv, 1)

                qk(0)
                qk(1)
                for h in range(8):
                    if h < 6:
                        qk(h + 2)
                    if h:
                        pv(h - 1)
                    turn_p(h)
                pv(7)

            def scores1(h, qt, dst):
                b0, n = HD * (h % 2), (qt + 1) * P
                pe.wait_ge(s_ql, 2 + h + 1)
                mm(dst, Bh[:, h, qt * P:n], Bl[:, h // 4, 0:n], start=True, stop=False)
                return mm(dst, Bh[b0:b0 + HD, h, qt * P:n], Bl[b0:b0 + HD, 2 + h // 4, 0:n], start=False, stop=True)

            for i in range(4):
                took(pe, "gp", i)
            for i in range(2, 4):
                atook(pe, "pool", i)
            attention(0, scores1, lambda h, kt: vtok[:, kt * P + HD * (h // 4):kt * P + HD * (h // 4) + HD], p1, pT1,
                      lambda pair: (s_ao, pair + 1))
            mixer1 = ([(pmh[:, k, :], pml[:, k, :], (s_ml, k + 1)) for k in range(4)]
                      + [(aoh[:, k, :], aol[:, k, :], (s_ml, k + 5)) for k in range(4)])
            for i in range(0, 8, 2):
                chunk([("y", i), ("y", i + 1)], mixer1)
                if i:
                    for j in (i - 2, i - 1):
                        sum_sq(sqy[j % 2], j, KD, (s_v, 2) if j == 0 else None)
            hg = [(Bh[:, k, :], Bl[:, k, :], (s_hl, 8 + k + 1)) for k in range(KD)]
            product(begin("in2", 0), weights(w[0], cols_of(0, P)), hg).then_inc(s_blk, 1)
            for j in (6, 7):
                sum_sq(sqy[j % 2], j, KD)
            product(begin("in2", 1), weights(w[0], cols_of(P, 2 * P)), hg).then_inc(s_blk, 1)
            w[0] += 1
            pe.wait_ge(s_rs, 3)
            spread("n2", kcol(2))
            for i in range(2, 8, 2):
                chunk([("in2", i), ("in2", i + 1)], hg)
            for i in range(2):
                sum_sq(sq2[i % 2], i, 3, (s_v, 3))
            product(begin("in2", 8), weights(w[0], cols_of(0, P)), hg).then_inc(s_blk, 1)
            sum_sq(sq2[0], 2, 3)
            product(begin("in2", 9), weights(w[0], cols_of(32, 160)), hg).then_inc(s_blk, 1)
            w[0] += 1
            product(begin("in2", 10), weights(w[0], cols_of(0, P)), hg).then_inc(s_blk, 1)
            sum_sq(sq2[1], 0, 2, (s_v, 4))
            sum_sq(sq2[0], 1, 2)
            turn("krrot", 0, rot32, kro, ("in2", 9))
            product(begin("in2", 11), weights(w[0], cols_of(P, 2 * P)), hg).then_inc(s_blk, 1)
            w[0] += 1
            pe.wait_ge(s_rs, 4)
            spread("n3", kcol(3))
            pe.wait_ge(s_rs, 5)
            spread("n4", kcol(4))
            chunk([("in2", 12), ("in2", 13)], hg)
            qn = [(qnh[:, k, :], qnl[:, k, :], (s_hl, 16 + k + 1)) for k in range(3)]
            kvn = [(kvh[:, k, :], kvl[:, k, :], (s_hl, 19 + k + 1)) for k in range(2)]

            for c in range(2):
                chunk([("qb", 3 * c + n) for n in range(3)], qn)
            for i in range(4):
                product(begin("kn", i), weights(w[0], cols_of(P * i, P * i + P)), kvn).then_inc(s_blk, 1)
            for i in range(2):
                turn("q2rot", i, rot32, qro[:, i, :], ("qb", 3 * i + 2))
            for t in range(NT):
                wts = weights(w[0], cols_of(512, 1024))
                dst = begin("v2", t)
                for k in range(2):
                    sl = slice(t * P, (t + 1) * P)
                    (wh, wl), (xh, xl, _) = wts[k], kvn[k]
                    mm(dst, xh[:, sl], wh, start=(k == 0), stop=False)
                    mm(dst, xh[:, sl], wl, start=False, stop=False)
                    ins = mm(dst, xl[:, sl], wh, start=False, stop=(k == 1))
                ins.then_inc(s_blk, 1)
            w[0] += 1

            def scores2(h, qt, dst):
                b0, r0 = HD * (h % 2), 32 * (h % 4)
                q0, n = qt * P, (qt + 1) * P
                mm(dst, qno[b0:b0 + HD, h // 2, q0:q0 + P], kno[b0:b0 + HD, h // 2, 0:n], start=True, stop=False)
                return mm(dst, qro[r0:r0 + 32, h // 4, q0:q0 + P], kro[r0:r0 + 32, 0:n], start=False, stop=True,
                          tile_position=(r0, 0))

            for i in range(4):
                took(pe, "v2", i)
            atook(pe, "q2rot", 1)
            pe.wait_ge(s_kr4, 3)
            pe.wait_ge(s_q2, 2)
            attention(1, scores2, lambda h, kt: v2[:, kt, HD * h:HD * h + HD], p2, pT2,
                      lambda pair: (s_ml, 8 + pair + 1))
            mixer2 = [(Bh[:, k, :], Bl[:, k, :], (s_ml, 8 + k + 1)) for k in range(KD)]
            pe.wait_ge(s_ml, 11)
            halves = []
            for i in range(4):
                halves.append((begin("mix", i), weights(w[0] + i // 2, cols_of(P * (i % 2), P * (i % 2) + P))))
                if i == 1:
                    product(*halves[1], mixer2, 0, 2, stop=False)
                    pe.wait_ge(s_v, 5)
                    for j in range(4):
                        if j < DVE_CONV:
                            pe.wait_ge(s_cv, j + 1)
                        else:
                            pe.wait_ge(s_cvp, j - DVE_CONV + 1)
                        ins = sums(cacc[:, j, :], j, 4)
                    ins.then_inc(s_mus, 1)
                    product(*halves[1], mixer2, 2, 4, start=False, stop=False)
                    pe.wait_ge(s_mu, 1)
                    spread("lnm", mu)
                elif i < 3:
                    product(*halves[i], mixer2, 0, 4, stop=False)
            for j in range(4):
                sum_sq(v2[:, j, :], j, 4)
            product(*halves[3], mixer2, 0, 1, stop=False)
            pe.wait_ge(s_rs, 6)
            spread("lnv", kcol(5))
            product(*halves[3], mixer2, 1, 4, start=False, stop=False)
            for i in range(4):
                product(*halves[i], mixer2, 4, 8, start=False).then_inc(s_blk, 1)
                if i >= 2:
                    sum_sq(sq2[i % 2], i - 2, KD, (s_v, 6), via=("mix", i - 2))
            w[0] += 2
            for i in range(4, 8, 2):
                chunk([("mix", i), ("mix", i + 1)], mixer2)
                for j in (i - 2, i - 1):
                    sum_sq(sq2[j % 2], j, KD, via=("mix", j))
            for j in (6, 7):
                sum_sq(sq2[j % 2], j, KD, via=("mix", j))
            pe.wait_ge(s_rs, 7)
            spread("n6", kcol(6))
            h2 = [(Bh[:, k, :], Bl[:, k, :], (s_hl, 21 + k + 1)) for k in range(KD)]
            pair = [(begin("ffn", i), weights(w[0], cols_of(P * i, P * i + P))) for i in range(2)]
            for k in range(KD):
                for i in range(2):
                    ins = product(*pair[i], h2, k, k + 1, start=(k == 0), stop=(k == KD - 1))
                    if k == KD - 1:
                        ins.then_inc(s_blk, 1)
            for k in range(KD):
                sum_sq(mix[:, k, :], k, KD, (s_v, 7))
            w[0] += 1
            product(begin("ffn", 2), weights(w[0], cols_of(0, P)), h2).then_inc(s_blk, 1)
            pe.wait_ge(s_rs, 8)
            spread("n7", kcol(7))
            product(begin("ffn", 3), weights(w[0], cols_of(P, 2 * P)), h2).then_inc(s_blk, 1)
            w[0] += 1
            for j in range(2, NJ):
                chunk([("ffn", 2 * j), ("ffn", 2 * j + 1)], h2)
            ff = [(fh[:, k, :], fl[:, k, :], (s_fl, k + 1)) for k in range(NJ)]
            for e in range(KD):
                dst = begin("down", e)
                product(dst, weights(w[0], cols_of(0, P)), ff[0:11], stop=False).then_inc(s_half, 1)
                product(dst, weights(w[0] + 1, cols_of(0, P)), ff[11:22], start=False).then_inc(s_blk, 1)
                w[0] += 2
                if e:
                    sum_sq(cv[(e - 1) % 2], e - 1, KD, (s_v, 8), via=("down", e - 1))
            sum_sq(cv[1], 7, KD, via=("down", 7))
            pe.wait_ge(s_pTl, 2)
            for i in range(8):
                t, hf = i // 2, i % 2
                wts = weights(w[0], cols_of(512 * hf, 512 * hf + 512))
                dst = begin("e", i)
                for k in range(2):
                    sl = slice(t * P, (t + 1) * P)
                    wh, wl = wts[k]
                    mm(dst, pTh[:, k, sl], wh, start=(k == 0), stop=False)
                    mm(dst, pTh[:, k, sl], wl, start=False, stop=False)
                    ins = mm(dst, pTl[:, k, sl], wh, start=False, stop=(k == 1))
                ins.then_inc(s_blk, 1)
                if i == 1:
                    pe.wait_ge(s_rs, 9)
                    spread("n8", kcol(8))
            w[0] += 1
            def gate(dst, t, k):
                sl = slice(t * P, (t + 1) * P)
                wh, wl = wts[k]
                mm(dst, h3h[:, k, sl], wh, start=(k == 0), stop=False)
                mm(dst, h3h[:, k, sl], wl, start=False, stop=False)
                return mm(dst, h3l[:, k, sl], wh, start=False, stop=(k == KD - 1))

            for c in range(4):
                wts = weights(w[0], cols_of(0, 256))
                if c == 0:
                    dsts = [begin(*gate_block(t))[:, 0:256] for t in range(NT)]
                    for k in range(KD):
                        pe.wait_ge(s_hl, 29 + k + 1)
                        for t in range(NT):
                            ins = gate(dsts[t], t, k)
                            if k == KD - 1:
                                ins.then_inc(s_blk, 1)
                else:
                    for t in range(NT):
                        dst = begin(*gate_block(4 * c + t))[:, 0:256]
                        for k in range(KD):
                            ins = gate(dst, t, k)
                        ins.then_inc(s_blk, 1)
                w[0] += 1
                if c < 2:
                    for i in range(4 * c, 4 * c + 4):
                        t, hf = i % 4, i // 4
                        dst = begin(("h3a", "h3b")[hf], t)
                        for k in range(4):
                            ins = nc.tensor.transpose(dst[:, k * P:(k + 1) * P], R[:, 4 * hf + k, t * P:(t + 1) * P],
                                                      ident)
                        ins.then_inc(s_blk, 1)
            assert w[0] == len(wchunk) and an[0] == len(aplan) and bn[0] == len(plan)

        @block.vector
        def _(dve):
            v = nc.vector
            dc, lw, ci_at, nn = [0], [0], [0], [0]
            evD, aevD = s_ev["D"], s_aev["D"]

            def link(ins):
                dc[0] += 1
                ins.then_inc(dch, 1)
                dve.wait_ge(dch, dc[0])

            def lo(n=1):
                for _ in range(n):
                    w = lw[0]
                    ci = wchunk[w]
                    assert ci == ci_at[0], (ci, ci_at[0])
                    dve.wait_ge(s_hi, w + 1)
                    k, m = chunks[ci][2:]
                    src = raw[:, ci % RAWS, 0:k * m]
                    v.tensor_tensor(wlo[:, ci % RAWS, 0:k * m], src, whi[:, w % HIS, 0:k * m].bitcast(F32),
                                    ALU.subtract).then_inc(s_lo, 1)
                    lw[0] += 1
                    ci_at[0] += 1

            def ada(dst, k0, parts, width, cont):
                ci = ci_at[0]
                dve.wait_ge(s_raw[ci % RAWS], landed[ci])
                for i in range(parts):
                    src = raw[:, ci % RAWS, i * width:(i + 1) * width]
                    c = csil[:, k0 + i:k0 + i + 1]
                    if i == 0 and not cont:
                        ins = v.tensor_scalar(dst, src, c, None, ALU.mult)
                    else:
                        ins = v.scalar_tensor_tensor(dst, src, c, dst, ALU.mult, ALU.add)
                    if i < parts - 1:
                        link(ins)
                ins.then_inc(s_lo, 1)
                ci_at[0] += 1
                dve.wait_ge(s_lo, ci_at[0])

            def variance(src, n, count=NT):
                v.tensor_scalar(nrm[:, 0, 0:count], src, 1.0 / n, EPS, ALU.mult, ALU.add).then_inc(s_v, 1)

            def rstd(dst, count=NT):
                nn[0] += 1
                dve.wait_ge(s_rt, nn[0])
                va, ro, r, tt = (nrm[:, i, 0:count] for i in range(4))
                link(v.reciprocal(r, ro))
                link(v.tensor_tensor(tt, r, r, ALU.mult))
                link(v.tensor_tensor(tt, tt, va, ALU.mult))
                link(v.tensor_scalar(tt, tt, -0.5, 1.5, ALU.mult, ALU.add))
                return v.tensor_tensor(dst, r, tt, ALU.mult)

            def norm(summed, count, idx):
                dve.wait_ge(s_cs, summed)
                variance(ps[:, 4, 0:NT], count)
                rstd(keep[:, 8 * idx:8 * idx + NT]).then_inc(s_rs, 1)

            def rope(dst, src, name, i, parts=P, cos=cosT, sin=sinT, tmp=(t1, t2)):
                rot = afilled(dve, name, i)
                link(v.tensor_tensor(tmp[0][0:parts, :], src, cos[0:parts, :], ALU.mult))
                v.tensor_tensor(tmp[1][0:parts, :], rot[0:parts, :], sin[0:parts, :], ALU.mult).then_inc(aevD, 1)
                atook(dve, name, i)
                return v.tensor_tensor(dst, tmp[0][0:parts, :], tmp[1][0:parts, :], ALU.add)

            dve.wait_ge(s_con, 16)
            dve.wait_ge(s_vec, 16)
            dve.wait_ge(s_csil, 1)

            def by_group(x):
                return x.rearrange("p (a g c) -> p g a c", a=2, g=2)

            def modulation(g):
                mod = afilled(dve, "mod", g)
                v.tensor_tensor(by_group(mtmp)[:, g], mod[:, 0:8].rearrange("p (a c) -> p a c", a=2),
                                by_group(col("b_ada", 0, 16))[:, g], ALU.add).then_inc(aevD, 1)
                atook(dve, "mod", g)
                v.scalar_tensor_tensor(mcol[:, 4 * g:4 * g + 4], mtmp[:, 8 + 4 * g:12 + 4 * g], 1.0,
                                       col("norm_w", 4 * g, 4), ALU.add, ALU.mult).then_inc(s_mod, 1)

            def low1(k):
                dve.wait_ge(s_hh, k + 1)
                v.tensor_tensor(Bl[:, k, :], xr[:, k, :], Bh[:, k, :].bitcast(F32), ALU.subtract).then_inc(s_hl, 1)

            for g in range(2):
                for k in range(0, KD, 2):
                    ada(acc[:, g * D:(g + 1) * D], k, 2, D, k > 0)
                    if g == 0 and k == 4:
                        norm(8, D, 0)
                    if g == 1 and k == 2:
                        modulation(0)
            for k in range(4):
                low1(k)
            lo(1)
            modulation(1)
            lo(1)
            for k in range(4, KD):
                low1(k)
            lo(1)

            def gate_ada(g):
                dve.wait_ge(s_gr[g % 2], 16 * (g // 2 + 1))
                if g:
                    dve.wait_ge(s_ga, g)
                for i in range(2):
                    src, c = gbuf[g % 2][:, i * D:(i + 1) * D], csil[:, 2 * g + i:2 * g + i + 1]
                    if g == i == 0:
                        ins = v.tensor_scalar(gacc, src, c, None, ALU.mult)
                    else:
                        ins = v.scalar_tensor_tensor(gacc, src, c, gacc, ALU.mult, ALU.add)
                    if i == 0:
                        link(ins)
                ins.then_inc(s_ga, 1)

            gate_ada(0)
            gate_ada(1)
            dve.wait_ge(s_trig, 16)
            took(dve, "kiw", 0)
            rope(kid[0:HD, :], kiw[0:HD, :], "kirot", 0, HD).then_inc(s_ki, 1)
            v.tensor_scalar(small[:, 48:80], afilled(dve, "wiT")[:, 0:32], 8 ** -0.5, None, ALU.mult).then_inc(aevD, 1)
            atook(dve, "wiT")

            def rope_qi(i):
                took(dve, "qi", i)
                if i:
                    dve.wait_ge(s_qi, i)
                rope(qiT[:, i, :], qiT[:, i, :], "qirot", i).then_inc(s_qi, 1)

            def low_qi(h):
                b0 = HD * (h % 2)
                dve.wait_ge(s_qsh, h + 1)
                v.tensor_tensor(qs[HD - b0:2 * HD - b0, h, :], qiT[b0:b0 + HD, h // 2, :],
                                qs[b0:b0 + HD, h, :].bitcast(F32), ALU.subtract).then_inc(s_qs, 1)

            rope_qi(0)
            rope_qi(1)
            lo(1)
            dve.wait_ge(s_kh, 1)
            v.tensor_tensor(kl, kid, kh.bitcast(F32), ALU.subtract).then_inc(s_kl, 1)
            for h in range(4):
                low_qi(h)
            gate_ada(2)
            gate_ada(3)
            rope_qi(2)
            rope_qi(3)
            rounds, marked = [0], [0] * 3

            def topk(n):
                for _ in range(n):
                    seen = []
                    for qt in range(1, NT):
                        if rounds[0]:
                            dve.wait_ge(dch, marked[qt - 1])
                        v.max(m8[:, qt - 1, :], sc[:, qt, 0:(qt + 1) * P]).then_inc(dch, 1)
                        dc[0] += 1
                        seen.append(dc[0])
                    for qt in range(1, NT):
                        s = sc[:, qt, 0:(qt + 1) * P]
                        dve.wait_ge(dch, seen[qt - 1])
                        v.match_replace(s, m8[:, qt - 1, :], s, TAKEN).then_inc(dch, 1)
                        dc[0] += 1
                        marked[qt - 1] = dc[0]
                    rounds[0] += 1
                    if rounds[0] == TOPK // 8:
                        for qt in range(1, NT):
                            s = sc[:, qt, 0:(qt + 1) * P]
                            dve.wait_ge(dch, marked[qt - 1])
                            link(v.tensor_scalar(s, s, -2e38, NEG, ALU.is_gt, ALU.mult))

            for n in range(24):
                qt, h = idx_item(n)
                wd = (qt + 1) * P
                atook(dve, "idx", n)
                dst, r, wcol = sc[:, qt, 0:wd], rl[:, n % 2, 0:wd], wiT[:, qt, h:h + 1]
                if h == 0:
                    v.tensor_scalar(dst, r, wcol, None, ALU.mult).then_inc(s_idx, 1)
                else:
                    dve.wait_ge(s_idx, n)
                    v.scalar_tensor_tensor(dst, r, wcol, dst, ALU.mult, ALU.add).then_inc(s_idx, 1)
                if n == 5:
                    for hh in range(4, 8):
                        low_qi(hh)
                if n in (3, 13, 20):
                    lo(1)
                if h == 7:
                    dve.wait_ge(s_idx, n + 1)
                    diag = sc[:, qt, qt * P:wd]
                    link(v.tensor_tensor(diag, diag, tri, ALU.add))
            topk(3)
            lo(1)
            topk(4)
            lo(1)
            topk(1)
            gm = afilled(dve, "gmod")
            v.tensor_tensor(gtcol, gm[:, 0:8], col("b_ada", 16, 8), ALU.add).then_inc(aevD, 1)
            took(dve, "k", 0)
            link(rope(kraw, kraw, "krot", 0))
            took(dve, "q", 0)
            rope(qT[:, 0, :], qT[:, 0, :], "qrot", 0).then_inc(s_qr, 1)
            dve.wait_ge(s_cs, 13)
            variance(ps[:, 4, 0:40], HD, 40)
            link(rstd(small[:, 176:216], 40))
            link(v.tensor_scalar(rqs, rqk[:, :, 2:10], SCALE1, None, ALU.mult))
            for h in range(2):
                ins = v.tensor_copy(kbx[:, :, h * HD:(h + 1) * HD], rqk[:, :, h:h + 1].to_broadcast([P, NT, HD]))
                if h == 0:
                    link(ins)
            ins.then_inc(s_rs, 1)
            for i in range(1, 4):
                dve.wait_ge(s_qr, i)
                took(dve, "q", i)
                rope(qT[:, i, :], qT[:, i, :], "qrot", i).then_inc(s_qr, 1)
            v.tensor_tensor(kraw, kraw, afilled(dve, "kb"), ALU.mult).then_inc(aevD, 1)
            lo(1)
            topk(2)
            lo(1)
            topk(1)

            def pooled(g):
                wdw = 2 << g
                S = pp[g % 2][:, CP:CP + T]
                dve.wait_ge(s_pool, g + 1)
                took(dve, "u", g)
                link(v.tensor_tensor(t1[:, 0:wdw], S[:, 0:wdw], con[:, C_RC:C_RC + wdw], ALU.mult))
                link(v.tensor_tensor(uT[:, g, 0:wdw], t1[:, 0:wdw], uT[:, g, 0:wdw], ALU.subtract))
                v.scalar_tensor_tensor(uT[:, g, wdw:T], S[:, wdw:T], 1.0 / wdw, uT[:, g, wdw:T], ALU.mult,
                                       ALU.subtract).then_inc(s_pld, 1)

            def mixed(g):
                dve.wait_ge(s_pld, g + 1)
                m = afilled(dve, "pool", g)
                took(dve, "gp", g)
                v.scalar_tensor_tensor(uT[:, g, :], m, col("pool_scale", g), gp[:, g, :], ALU.mult,
                                       ALU.mult).then_inc(aevD, 1)

            pooled(0)
            topk(1)
            lo(1)
            topk(1)
            pooled(1)
            topk(1)
            pooled(2)
            lo(1)
            topk(1)
            pooled(3)
            topk(TOPK // 8 - rounds[0])
            lo(1)
            for i in range(2):
                dve.wait_ge(s_qh, i + 1)
                v.tensor_tensor(Bl[:, 2 + i, :], kdup[:, i, :], Bl[:, i, :].bitcast(F32),
                                ALU.subtract).then_inc(s_ql, 1)
            for g in range(4):
                mixed(g)


            def attention(base, mask, negate, p, take_pair, out_pair, between):
                def masked(h):
                    if h >= 3:
                        dve.wait_ge(s_pt, base * 24 + 3 * (h - 2))
                    for n, qt in enumerate(QORD):
                        o, wd = SOFF[qt], (qt + 1) * P
                        dve.wait_ge(s_qk, base * 32 + 4 * h + (1, 3, 3, 4)[n])
                        b = (4, 5, 5, 6)[n]
                        v.tensor_tensor_reduce(out=p[h % 3][:, o:o + wd], in0=ps[:, b, o % 512:o % 512 + wd],
                                               in1=mask(qt), scale=1.0, scalar=-3e38, op0=ALU.add, op1=ALU.max,
                                               accum_out=mx[:, h % 2, qt:qt + 1]).then_inc(s_msk, 1)
                    dve.wait_ge(s_msk, base * 32 + 4 * h + 4)
                    negate(h).then_inc(s_nb, 1)

                def normalised(h):
                    dve.wait_ge(s_exp, base * 32 + 4 * h + 4)
                    link(v.reciprocal(rsm[:, h % 2, :], sm[:, h % 2, :]))
                    for qt in QORD:
                        o, wd = SOFF[qt], (qt + 1) * P
                        s = p[h % 3][:, o:o + wd]
                        v.tensor_scalar(s, s, rsm[:, h % 2, qt:qt + 1], None, ALU.mult).then_inc(s_pn, 1)

                masked(0)
                for h in range(8):
                    if h < 7:
                        masked(h + 1)
                    if take_pair and h >= 3 and h % 2:
                        take_pair(h // 2 - 1)
                    normalised(h)
                    between(h)
                    if out_pair and h >= 4 and h % 2 == 0:
                        out_pair(h // 2 - 2)
                if out_pair:
                    out_pair(2)
                    take_pair(3)
                    out_pair(3)

            def negate1(h):
                return v.scalar_tensor_tensor(nb[:, h % 2, :], mx[:, h % 2, :], -1.0, rqs[:, :, h], ALU.mult, ALU.mult)

            def low_q(h):
                b0 = HD * (h % 2)
                dve.wait_ge(s_qh, 2 + h + 1)
                v.tensor_tensor(Bh[HD - b0:2 * HD - b0, h, :], qT[b0:b0 + HD, h // 2, :],
                                Bh[b0:b0 + HD, h, :].bitcast(F32), ALU.subtract).then_inc(s_ql, 1)

            for h in range(3):
                low_q(h)

            def between1(h):
                if h < 5:
                    low_q(h + 3)
                if h < 4:
                    dve.wait_ge(s_mh, h + 1)
                    v.tensor_tensor(pml[:, h, :], uT[:, h, :], pmh[:, h, :].bitcast(F32),
                                    ALU.subtract).then_inc(s_ml, 1)
                if h == 2:
                    lo(1)

            def take1(pair):
                dve.wait_ge(s_pv, 2 * pair + 2)
                if pair:
                    dve.wait_ge(s_ml, 4 + pair)
                v.tensor_tensor(ao, ps[:, obank(pair), :], gat[:, pair, :], ALU.mult).then_inc(s_ao, 1)

            def out1(pair):
                dve.wait_ge(s_mh, 4 + pair + 1)
                v.tensor_tensor(aol[:, pair, :], ao, aoh[:, pair, :].bitcast(F32), ALU.subtract).then_inc(s_ml, 1)

            attention(0, lambda qt: tri if qt == 0 else sc[:, qt, 0:(qt + 1) * P], negate1, p1, take1, out1, between1)
            for k in range(KD):
                v.scalar_tensor_tensor(R[:, k, :], filled(dve, "y", k), gtcol[:, k:k + 1], R[:, k, :], ALU.mult,
                                       ALU.add).then_inc(evD, 1)
                took(dve, "y", k)
                dve.wait_ge(s_hh, 8 + k + 1)
                v.scalar_tensor_tensor(Bl[:, k, :], R[:, k, :], col("g_mix_pre_2", k), Bh[:, k, :].bitcast(F32),
                                       ALU.mult, ALU.subtract).then_inc(s_hl, 1)
                if k % 2:
                    lo(1)
            norm(21, D, 2)
            atook(dve, "n2")

            def tmul(dst, i, signal):
                v.tensor_tensor(dst, filled(dve, "in2", i), rB, ALU.mult).then_inc(signal, 1)

            cs, tap_at = [0], [0] * 4
            taps = [(j, t) for t in range(10) for j in range(2)]
            taps += [(j, t + (10 if j < 2 else 0)) for t in range(CW) for j in range(DVE_CONV) if j == 2 or t + 10 < CW]

            def conv(n):
                for _ in range(min(n, len(taps) - cs[0])):
                    j, t = taps[cs[0]]
                    src = cpad[:, j, CP - (CW - 1) + t:CP - (CW - 1) + t + T]
                    wcol = col("conv_w_2", t * 4 + j)
                    if t == 0:
                        ins = v.tensor_scalar(cacc[:, j, :], src, wcol, col("conv_b_2", j), ALU.mult, ALU.add)
                    else:
                        dve.wait_ge(dch, tap_at[j])
                        ins = v.scalar_tensor_tensor(cacc[:, j, :], src, wcol, cacc[:, j, :], ALU.mult, ALU.add)
                    if t < CW - 1:
                        ins.then_inc(dch, 1)
                        dc[0] += 1
                        tap_at[j] = dc[0]
                    else:
                        ins.then_inc(s_cv, 1)
                    cs[0] += 1

            dve.wait_ge(s_cpz, 1)

            def gates(j0):
                for j in (j0, j0 + 1):
                    tmul(gt2[:, j % 2, :], GATE[j], evD)

            def gated(j0):
                for j in (j0, j0 + 1):
                    tmul(tmpa, VALUE[j], evD)
                    took(dve, "in2", VALUE[j])
                    dve.wait_ge(s_sg, j + 1)
                    ins = v.tensor_tensor(cpad[:, j, CP:CP + T], tmpa, gt2[:, j % 2, :], ALU.mult)
                    if j < DVE_CONV:
                        link(ins)
                    else:
                        ins.then_inc(s_cp, 1)
                        dve.wait_ge(s_cp, j - DVE_CONV + 1)

            gates(0)
            lo(1)
            gated(0)
            lo(1)
            conv(6)
            for i in range(2):
                tmul(qa[:, i, :], 4 + i, evD)
            lo(1)
            conv(8)
            tmul(qa[:, 2, :], 6, evD)
            tmul(kva[:, 0, :], 7, evD)
            lo(1)
            conv(2)
            tmul(kva[:, 1, :], 8, evD)
            tmul(kro, 9, evD)
            took(dve, "in2", 9)
            norm(24, 384, 3)
            conv(4)
            norm(26, 256, 4)
            gates(2)
            lo(1)
            dve.wait_ge(s_tab, 2)
            rope(kro, kro, "krrot", 0, tmp=(s2c, tmpa)).then_inc(s_kr, 1)
            b = afilled(dve, "n3")
            for i in range(3):
                v.scalar_tensor_tensor(qa[:, i, :], qa[:, i, :], col("g_q_a_2", i), b, ALU.mult, ALU.mult) \
                    .then_inc(s_qn if i < 2 else aevD, 1)
            b = afilled(dve, "n4")
            for i in range(2):
                v.scalar_tensor_tensor(kva[:, i, :], kva[:, i, :], col("g_kv_a_2", i), b, ALU.mult, ALU.mult) \
                    .then_inc(s_qn if i < 1 else aevD, 1)
            for i in range(3):
                dve.wait_ge(s_hh, 16 + i + 1)
                v.tensor_tensor(qnl[:, i, :], qa[:, i, :], qnh[:, i, :].bitcast(F32), ALU.subtract).then_inc(s_hl, 1)
            for i in range(2):
                dve.wait_ge(s_hh, 19 + i + 1)
                v.tensor_tensor(kvl[:, i, :], kva[:, i, :], kvh[:, i, :].bitcast(F32), ALU.subtract).then_inc(s_hl, 1)
            lo(1)
            gated(2)
            lo(1)
            conv(2)
            lo(1)
            conv(6)
            for i in range(2):
                took(dve, "qb", 3 * i + 2)
                rope(qro[:, i, :], qro[:, i, :], "q2rot", i, tmp=(s2c, tmpa)).then_inc(s_q2, 1)
                if i == 0:
                    lo(1)
                dve.wait_ge(s_q2, i + 1)
            conv(3)

            def negate2(h):
                return v.tensor_scalar(nb[:, h % 2, :], mx[:, h % 2, :], -SCALE2, None, ALU.mult)

            def out2(pair):
                dve.wait_ge(s_mh, 8 + pair + 1)
                v.tensor_tensor(Bl[:, pair, :], ps[:, obank(pair), :], Bh[:, pair, :].bitcast(F32),
                                ALU.subtract).then_inc(s_ml, 1)

            def between2(h):
                if h >= 3 and h % 2:
                    out2(h // 2 - 1)
                conv(7)
                if h == 3:
                    lo(1)

            attention(1, lambda qt: con[:, C_TRI + 384 - P * qt:C_TRI + 512], negate2, p2, None, None, between2)
            out2(3)
            conv(len(taps))
            dve.wait_ge(s_mus, 1)
            v.tensor_scalar(mu, ps[:, 4, 0:NT], 1.0 / 512, None, ALU.mult).then_inc(s_mu, 1)
            b = afilled(dve, "lnm")
            for j in range(4):
                v.tensor_tensor(cacc[:, j, :], cacc[:, j, :], b, ALU.subtract).then_inc(s_ln if j < 3 else aevD, 1)
            norm(30, 512, 5)
            b = afilled(dve, "lnv")
            for j in range(4):
                v.tensor_tensor(cacc[:, j, :], cacc[:, j, :], b, ALU.mult).then_inc(s_ln2 if j < 3 else aevD, 1)
            for j in range(4):
                dve.wait_ge(s_mh, 12 + j + 1)
                v.tensor_tensor(Bl[:, 4 + j, :], cacc[:, j, :], Bh[:, 4 + j, :].bitcast(F32),
                                ALU.subtract).then_inc(s_ml, 1)
            lo(3)
            norm(38, D, 6)

            def low2(k):
                dve.wait_ge(s_hh, 21 + k + 1)
                v.scalar_tensor_tensor(Bl[:, k, :], R[:, k, :], col("g_ffn_pre_2", k), Bh[:, k, :].bitcast(F32),
                                       ALU.mult, ALU.subtract).then_inc(s_hl, 1)

            atook(dve, "n6")
            link(v.tensor_tensor(mix[:, 0, :], mix[:, 0, :], rB, ALU.mult))
            for k in range(KD):
                if k:
                    dve.wait_ge(s_scaled, k)
                v.tensor_tensor(R[:, k, :], R[:, k, :], mix[:, k, :], ALU.add).then_inc(s_h2, 1)
                dve.wait_ge(s_h2, k + 1)
                if k:
                    low2(k - 1)
            low2(KD - 1)
            lo(1)
            norm(46, D, 7)
            atook(dve, "n7")
            link(v.memset(zg[:, 0:16], 0.0))
            for j in range(NJ):
                c = cv[j % 2]
                if j:
                    dve.wait_ge(s_z, j)
                if j > 1:
                    dve.wait_ge(s_fl, j - 1)
                v.tensor_tensor(zg[:, 16:16 + T], filled(dve, "ffn", 2 * j), rBf, ALU.mult).then_inc(evD, 1)
                took(dve, "ffn", 2 * j)
                link(v.tensor_scalar(c, zg[:, 16:16 + T], col("ffn_dw_w_2", 2 * NJ + j), col("ffn_dw_b_2", j),
                                     ALU.mult, ALU.add))
                link(v.scalar_tensor_tensor(c, zg[:, 15:15 + T], col("ffn_dw_w_2", NJ + j), c, ALU.mult, ALU.add))
                v.scalar_tensor_tensor(c, zg[:, 14:14 + T], col("ffn_dw_w_2", j), c, ALU.mult,
                                       ALU.add).then_inc(s_z, 1)
                if j:
                    dve.wait_ge(s_fd, j)
                v.tensor_tensor(up, filled(dve, "ffn", 2 * j + 1), rBf, ALU.mult).then_inc(evD, 1)
                dve.wait_ge(s_gl, j + 1)
                took(dve, "ffn", 2 * j + 1)
                v.tensor_tensor(c, c, up, ALU.mult).then_inc(s_fd, 1)
                lo(1)
                dve.wait_ge(s_fh, j + 1)
                v.tensor_tensor(fl[:, j, :], c, fh[:, j, :].bitcast(F32), ALU.subtract).then_inc(s_fl, 1)
            for e in range(KD):
                lo(1)
                if e == 0:
                    for k in range(2):
                        dve.wait_ge(s_pTh, k + 1)
                        v.tensor_tensor(pTl[:, k, :], pTf[:, k, :], pTh[:, k, :].bitcast(F32),
                                        ALU.subtract).then_inc(s_pTl, 1)
                if e < KD - 1:
                    lo(1)
            norm(54, D, 8)

            def square_e(i):
                t, hf = i // 2, i % 2
                took(dve, "e", i)
                src = etok[:, t, 512 * hf:512 * hf + 512]
                link(v.tensor_tensor_reduce(out=cosT, in0=src, in1=src, scale=1.0, scalar=0.0, op0=ALU.mult,
                                            op1=ALU.add, accum_out=sse[:, t, hf:hf + 1]))

            for i in range(3):
                square_e(i)

            def low3(k):
                dve.wait_ge(s_hh, 29 + k + 1)
                v.tensor_tensor(h3l[:, k, :], R[:, k, :], h3h[:, k, :].bitcast(F32), ALU.subtract).then_inc(s_hl, 1)

            for k in range(KD):
                dve.wait_ge(s_scaled, KD + k)
                v.tensor_tensor(R[:, k, :], R[:, k, :], fo[:, k, :], ALU.add).then_inc(s_h3, 1)
                dve.wait_ge(s_h3, k + 1)
                if k:
                    low3(k - 1)
            low3(KD - 1)
            lo(1)
            def token_major(hf):
                for t in range(NT):
                    v.tensor_copy(htok[:, t, 512 * hf:512 * hf + 512],
                                  filled(dve, ("h3a", "h3b")[hf], t)).then_inc(evD, 1)
                took(dve, ("h3a", "h3b")[hf], 3)

            square_e(3)
            token_major(0)
            lo(1)
            for i in range(4, 8):
                square_e(i)
            link(v.tensor_tensor(mu, sse[:, :, 0], sse[:, :, 1], ALU.add))
            variance(mu, D)
            link(rstd(keep[:, 72:76]))
            dve.wait_ge(s_grow, 16)
            for t in range(NT):
                link(v.scalar_tensor_tensor(etok[:, t, :], etok[:, t, :], keep[:, 72 + t:73 + t], grow, ALU.mult,
                                            ALU.mult))
                if t == 0:
                    lo(1)
                    token_major(1)
            for i in range(16):
                c, t = i // 4, i % 4
                took(dve, *gate_block(i))
                cl = slice(c * 256, (c + 1) * 256)
                link(v.tensor_tensor(otok[:, t, cl], otok[:, t, cl], etok[:, t, cl], ALU.mult))
                v.tensor_tensor(otok[:, t, cl], otok[:, t, cl], htok[:, t, cl], ALU.add).then_inc(s_ot, 1)
            assert lw[0] == len(wchunk), (lw[0], len(wchunk))
            assert rounds[0] == TOPK // 8


def kernel(**inputs):
    import concourse.bacc as _bacc
    from concourse import mybir as _mybir
    from concourse.bass_utils import run_bass_kernel_spmd as _run

    get = {name: np.ascontiguousarray(v) for name, v in inputs.items()}
    arrays = {}
    arrays["xT"] = np.ascontiguousarray(get["x"][0].T).reshape(KD, P, T)
    arrays["pT"] = np.ascontiguousarray(get["p_2"][0, 0].T).reshape(2, P, T)
    rows = []
    for name, n in VECS:
        v = get[name].reshape(-1)
        if name in ("q_norm_w", "k_norm_w"):
            v = np.concatenate([v, v])
        rows.append(v.reshape(n, P))
    arrays["vecs"] = np.ascontiguousarray(np.concatenate(rows).T)
    pieces = []
    for _, parts in stream():
        tiles = [get[name][0][r0:r1][:, cols].reshape((r1 - r0) // P, P, len(cols)) for name, r0, r1, cols in parts]
        pieces.append(np.concatenate(tiles, axis=2).transpose(1, 0, 2).reshape(-1))
    arrays["stream"] = np.concatenate(pieces)
    arrays["gate"] = np.ascontiguousarray(
        get["w_ada"][0][:, 2 * D:].reshape(4, 2, P, D).transpose(0, 2, 1, 3)).reshape(4, P, 2 * D)
    arrays["con"] = constants()
    for name in ("w_pool", "positions_2", "g_ple_2"):
        arrays[name] = get[name]
    nc = _bacc.Bacc("TRN2", target_bir_lowering=False, num_devices=1)
    args = {name: nc.dram_tensor(f"in_{name}_dram", v.shape, _mybir.dt.from_np(v.dtype), kind="ExternalInput").ap()
            for name, v in arrays.items()}
    out = nc.dram_tensor("out_0_dram", (1, T, D), _mybir.dt.float32, kind="ExternalOutput").ap()
    build(nc, args, out)
    r = _run(nc, [{f"in_{name}_dram": v for name, v in arrays.items()}], core_ids=[0])
    return r.results[0]["out_0_dram"]
```
